# Optimizing a Trainium2 kernel written in Bass

```python
import math
import jax, jax.numpy as jnp
from jax import lax
import numpy as np

D_MODEL = 1024
BATCH = 1
SEQ = 256
DEPTH = 2

N_MIXERS = 2
N_EVEN = (DEPTH + 1) // 2
N_ODD = DEPTH // 2
N_MOD = 6
POOL_WINDOWS = (2, 4, 8, 16)
N_POOL_GROUPS = len(POOL_WINDOWS)
POOL_GROUP_DIM = D_MODEL // N_POOL_GROUPS
N_HEADS = 8
HEAD_DIM = D_MODEL // (2 * N_HEADS)
V_HEAD_DIM = 2 * HEAD_DIM
LAMBDA_VEC_INIT_STD = 0.1
N_BUCKETS = 32
MAX_DISTANCE = 128
Q_BLOCK = 128
D_FF = ((8 * D_MODEL // 3 + 255) // 256) * 256
N_EXPERTS = 8
TOP_K = 2
D_FF_EXPERT = 7 * D_MODEL // 2
EPS = 1e-6

kernel_name = "hybrid_pool_diffattn_moe_trunk"

def rms_norm(x, g):
    xf = x.astype(jnp.float32)
    y = xf * lax.rsqrt(jnp.mean(xf * xf, axis=-1, keepdims=True) + EPS)
    return (y * g.astype(jnp.float32)).astype(x.dtype)

def pool_mixer(h, w_grp, scale):
    B, S, D = h.shape
    hf = h.reshape(B, S, N_POOL_GROUPS, POOL_GROUP_DIM).astype(jnp.float32)
    cs = jnp.cumsum(hf, axis=1)
    count = jnp.arange(1, S + 1, dtype=jnp.float32)
    outs = []
    for g, w in enumerate(POOL_WINDOWS):
        csg = cs[:, :, g]
        lag = jnp.pad(csg, ((0, 0), (w, 0), (0, 0)))[:, :S]
        mean = (csg - lag) / jnp.minimum(count, float(w))[None, :, None]
        outs.append(mean - hf[:, :, g])
    pooled = jnp.stack(outs, axis=2).astype(h.dtype)
    mixed = jnp.einsum('bsgc,gce->bsge', pooled, w_grp)
    return mixed.reshape(B, S, D) * scale

def rel_bucket(q_pos, k_pos):
    n = jnp.maximum(q_pos[:, None] - k_pos[None, :], 0)
    max_exact = N_BUCKETS // 2
    nf = jnp.maximum(n, 1).astype(jnp.float32)
    large = max_exact + (jnp.log(nf / max_exact) / math.log(MAX_DISTANCE / max_exact)
                         * (N_BUCKETS - max_exact)).astype(jnp.int32)
    large = jnp.minimum(large, N_BUCKETS - 1)
    return jnp.where(n < max_exact, n, large)

def diff_attention(h, w_qkv, w_o, subln_g, lam_vecs, rel_bias, lambda_init):
    B, S, D = h.shape
    q, k, v = jnp.split(h @ w_qkv, 3, axis=-1)
    q = q.reshape(B, S, N_HEADS, 2, HEAD_DIM) * (HEAD_DIM ** -0.5)
    k = k.reshape(B, S, N_HEADS, 2, HEAD_DIM)
    v = v.reshape(B, S, N_HEADS, V_HEAD_DIM)
    lv = lam_vecs.astype(jnp.float32)
    lam = jnp.exp(jnp.sum(lv[0] * lv[1])) - jnp.exp(jnp.sum(lv[2] * lv[3])) + lambda_init
    n_blk = S // Q_BLOCK
    q_blocks = q.reshape(B, n_blk, Q_BLOCK, N_HEADS, 2, HEAD_DIM).transpose(1, 0, 2, 3, 4, 5)
    k_pos = jnp.arange(S)

    def attend(args):
        q_blk, blk = args
        q_pos = blk * Q_BLOCK + jnp.arange(Q_BLOCK)
        bias = rel_bias[rel_bucket(q_pos, k_pos)].astype(jnp.float32).transpose(2, 0, 1)
        s = jnp.einsum('bqhcd,bkhcd->bhcqk', q_blk, k).astype(jnp.float32) + bias[None, :, None]
        s = jnp.where(k_pos[None, :] <= q_pos[:, None], s, -jnp.inf)
        p = jax.nn.softmax(s, axis=-1)
        a = p[:, :, 0] - lam * p[:, :, 1]
        return jnp.einsum('bhqk,bkhe->bqhe', a.astype(v.dtype), v)

    o = lax.map(attend, (q_blocks, jnp.arange(n_blk)))
    o = o.transpose(1, 0, 2, 3, 4).reshape(B, S, N_HEADS, V_HEAD_DIM)
    o = rms_norm(o, subln_g) * (1.0 - lambda_init)
    return o.reshape(B, S, D) @ w_o

def swiglu(t, w_gu, w_down):
    g, u = jnp.split(t @ w_gu, 2, axis=-1)
    return (jax.nn.silu(g) * u) @ w_down

def moe_swiglu(h, w_router, w_gu, w_down):
    B, S, D = h.shape
    t = h.reshape(-1, D)
    logits = (t @ w_router).astype(jnp.float32)
    top_val, top_idx = lax.top_k(logits, TOP_K)
    top_w = jax.nn.softmax(top_val, axis=-1)
    gates = jnp.sum(jax.nn.one_hot(top_idx, N_EXPERTS, dtype=jnp.float32) * top_w[..., None], axis=1)
    out = jnp.zeros_like(t)
    for e in range(N_EXPERTS):
        out = out + gates[:, e:e + 1].astype(t.dtype) * swiglu(t, w_gu[e], w_down[e])
    return out.reshape(B, S, D)

def setup_inputs(seed: int = 0) -> dict:
    key = jax.random.key(seed)
    ks = jax.random.split(key, 17)
    f32 = jnp.float32
    D = D_MODEL
    nrm = lambda k, shape, fan_in: jax.random.normal(k, shape, f32) * (fan_in ** -0.5)
    return {
        "x": jax.random.normal(ks[0], (BATCH, SEQ, D), f32),
        "c": jax.random.normal(ks[1], (BATCH, D), f32),
        "w_mod": nrm(ks[2], (DEPTH, D, N_MOD * D), D) * 0.5,
        "b_mod": 0.01 * jax.random.normal(ks[3], (DEPTH, N_MOD * D), f32),
        "norm_g": 1.0 + 0.05 * jax.random.normal(ks[4], (DEPTH, 4, D), f32),
        "pool_w": nrm(ks[5], (N_EVEN, N_POOL_GROUPS, POOL_GROUP_DIM, POOL_GROUP_DIM), POOL_GROUP_DIM),
        "pool_scale": 1.0 + 0.1 * jax.random.normal(ks[6], (N_EVEN, D), f32),
        "w_qkv": nrm(ks[7], (N_ODD, D, 3 * D), D),
        "w_o": nrm(ks[8], (N_ODD, D, D), D),
        "subln_g": 1.0 + 0.05 * jax.random.normal(ks[9], (N_ODD, V_HEAD_DIM), f32),
        "lambda_vecs": LAMBDA_VEC_INIT_STD * jax.random.normal(ks[10], (N_ODD, 4, HEAD_DIM), f32),
        "rel_bias": 0.5 * jax.random.normal(ks[11], (N_BUCKETS, N_HEADS), f32),
        "ffn_w_gu": nrm(ks[12], (N_EVEN, D, 2 * D_FF), D),
        "ffn_w_down": nrm(ks[13], (N_EVEN, D_FF, D), D_FF),
        "w_router": nrm(ks[14], (N_ODD, D, N_EXPERTS), D),
        "moe_w_gu": nrm(ks[15], (N_ODD, N_EXPERTS, D, 2 * D_FF_EXPERT), D),
        "moe_w_down": nrm(ks[16], (N_ODD, N_EXPERTS, D_FF_EXPERT, D), D_FF_EXPERT),
    }

def reference(x, c, w_mod, b_mod, norm_g, pool_w, pool_scale, w_qkv, w_o, subln_g,
              lambda_vecs, rel_bias, ffn_w_gu, ffn_w_down, w_router, moe_w_gu, moe_w_down):
    mod_all = jnp.einsum('bd,lde->lbe', jax.nn.silu(c), w_mod) + b_mod[:, None]
    for i in range(DEPTH):
        j = i // 2
        shift1, scale1, gate1, shift2, scale2, gate2 = jnp.split(mod_all[i], N_MOD, axis=-1)
        h = rms_norm(x, norm_g[i, 0]) * (1.0 + scale1[:, None]) + shift1[:, None]
        if i % N_MIXERS == 0:
            y = pool_mixer(h, pool_w[j], pool_scale[j])
        else:
            lambda_init = 0.8 - 0.6 * math.exp(-0.3 * i)
            y = diff_attention(h, w_qkv[j], w_o[j], subln_g[j], lambda_vecs[j], rel_bias, lambda_init)
        x = x + gate1[:, None] * rms_norm(y, norm_g[i, 1])
        h = rms_norm(x, norm_g[i, 2]) * (1.0 + scale2[:, None]) + shift2[:, None]
        if i % 2 == 0:
            y = swiglu(h, ffn_w_gu[j], ffn_w_down[j])
        else:
            y = moe_swiglu(h, w_router[j], moe_w_gu[j], moe_w_down[j])
        x = x + gate2[:, None] * rms_norm(y, norm_g[i, 3])
    return x


_drawn_inputs = setup_inputs


def setup_inputs(seed=0):
    import zlib

    import numpy as np

    out = dict(_drawn_inputs(seed))
    spreads = {}
    factors = {}
    for name, (base, spread) in spreads.items():
        noise = np.random.default_rng([zlib.crc32(name.encode()), seed]).standard_normal(out[name].shape)
        drawn = base * np.exp(spread * noise) if base else spread * noise
        out[name] = __import__('jax').numpy.asarray(drawn.astype(out[name].dtype))
    for name, factor in factors.items():
        out[name] = (out[name] * factor).astype(out[name].dtype)
    return out
```

```python
import math
from contextlib import ExitStack

import numpy as np
import concourse.bass as bass
from concourse import mybir
from concourse.alu_op_type import AluOpType as ALU

ACT = mybir.ActivationFunctionType
AX_X = mybir.AxisListType.X
F32 = mybir.dt.float32
F32R = mybir.dt.float32r
BF16 = mybir.dt.bfloat16
I32 = mybir.dt.int32
U32 = mybir.dt.uint32

P = 128
D = 1024
S = 256
T = S // P
KC = D // P
EPS = 1e-6
N_MOD = 6
WINDOWS = (2, 4, 8, 16)
NH = 8
HD = 64
N_BUCKETS = 32
MAX_DISTANCE = 128
FF = 2816
NE = 8
FE = 3584
LAMBDA_INIT = 0.8 - 0.6 * math.exp(-0.3 * 1)
NEG = -3.0e38

RAW = 6
SPL = 3
UNIT = 2048
FC = 256
NCF = FF // FC
NCE = FE // FC

MOD_UNITS = N_MOD * KC // 2
R_FFN, Q_FFN = MOD_UNITS, 0
MOD_STEPS = MOD_UNITS // 3
R_QKV, Q_QKV = R_FFN + 3 * NCF + MOD_UNITS, Q_FFN + 3 * NCF
R_WO, Q_WO = R_QKV + 12, Q_QKV + 12
R_MOE, Q_MOE = R_WO + 4, Q_WO + 4
EXPERT_UNITS = 3 * NCE
assert EXPERT_UNITS % RAW == 0 and EXPERT_UNITS % SPL == 0 and MOD_UNITS % RAW == 0

ROW = [[0, 1, 2, 3, 4, 5], [6, 0, 1, 2, 3, 4]]


def shape_constants():
    consts = np.zeros((P, 5, P), np.float32)
    consts[:, 0] = np.eye(P)
    consts[:, 1] = 1.0
    consts[:, 2] = np.triu(np.ones((P, P)), 1)
    consts[:, 3] = np.arange(P)[None, :]
    consts[:, 4] = np.eye(P)[::-1]
    pool = np.zeros((P, len(WINDOWS), S + P), np.float32)
    for g, w in enumerate(WINDOWS):
        full = np.zeros((S, S), np.float64)
        for s in range(S):
            lo = max(0, s - w + 1)
            full[lo:s + 1, s] = 1.0 / min(s + 1, w)
            full[s, s] -= 1.0
        pool[:, g, 0:S] = full[0:P]
        pool[:, g, S:] = full[P:, P:]
    n = S - 1 - np.arange(S)
    exact = N_BUCKETS // 2
    nf = np.maximum(n, 1).astype(np.float32)
    large = exact + (np.log(nf / np.float32(exact)) / np.float32(math.log(MAX_DISTANCE / exact))
                     * np.float32(N_BUCKETS - exact)).astype(np.int32)
    bucket = np.where(n < exact, n, np.minimum(large, N_BUCKETS - 1))
    onehot = np.zeros((N_BUCKETS, S), np.float32)
    onehot[bucket, np.arange(S)] = 1.0
    return consts.reshape(P, 5 * P), pool.reshape(P, -1), onehot


def build_trunk(nc, x, c, w_mod, b_mod, norm_g, pool_w, pool_scale, w_qkv, w_o, subln_g, lambda_vecs,
                rel_bias, ffn_w_gu, ffn_w_down, w_router, moe_w_gu, moe_w_down,
                consts_in, pool_in, onehot_in, out):
    bias_dram = nc.dram_tensor("bias_by_distance", (NH, S + P), F32, kind="Internal").ap()

    with ExitStack() as ctx:
        def sb(name, shape, dt=F32):
            return ctx.enter_context(nc.sbuf_tensor(name, shape, dt))

        def sem(name):
            return ctx.enter_context(nc.semaphore(name))

        raw = sb("raw", [P, RAW, UNIT])
        whi = sb("whi", [P, SPL, UNIT], F32R)
        wlo = sb("wlo", [P, SPL, UNIT], F32R)
        rows = sb("rows", [P, 7, D])
        xs = sb("xs", [P, T, D])
        hs = sb("hs", [P, T, D])
        thi = sb("thi", [P, UNIT], F32R)
        tlo = sb("tlo", [P, UNIT], F32R)
        ahi = sb("ahi", [P, 512], F32R)
        alo = sb("alo", [P, 512], F32R)
        gain = sb("gain", [P, D])
        scr = sb("scr", [P, 6 * D])
        ysb = sb("ysb", [P, T, D])
        tmp = sb("tmp", [P, 2304])
        consts = sb("consts", [P, 5, P])
        subln = sb("subln", [P, P])
        zeros = sb("zeros", [P, P], BF16)
        wr = sb("wr", [P, KC, NE])
        silu_c = sb("silu_c", [P, KC])
        ss = sb("ss", [P, 16])
        rstd = sb("rstd", [P, 16])
        minus_half = sb("minus_half", [P, 16])
        lam = sb("lam", [P, 4])
        stat = sb("stat", [P, 2, 3, 4])
        oss = sb("oss", [P, T, NH])
        posm = sb("posm", [P, T, NE + 1])
        gates = sb("gates", [P, T, NE])
        flag = sb("flag", [P, 1], I32)

        ident, ones, before, slots, reverse = (consts[:, i, :] for i in range(5))
        thi3 = thi[:, :].rearrange("p (k s) -> p k s", k=KC)
        tlo3 = tlo[:, :].rearrange("p (k s) -> p k s", k=KC)
        ghi = thi[:, 0:D].rearrange("p (k s) -> p k s", k=KC)
        glo = tlo[:, 0:D].rearrange("p (k s) -> p k s", k=KC)
        pool_m = scr[:, 0:4 * 384].rearrange("p (g s) -> p g s", g=4)
        poolw = scr[:, 1536:3584].rearrange("p (g c e) -> p g c e", g=4, c=2)
        onehot = scr[0:N_BUCKETS, 3584:3840]
        relb = scr[0:N_BUCKETS, 3840:3848]
        bias_row = scr[0:NH, 3848:3848 + S + P]
        lamv = scr[:, 4352:4608].rearrange("p (v d) -> p v d", v=4)
        lamj = scr[:, 4608:4672]
        bias_rev = scr[:, 4096:6144].rearrange("p (h k) -> p h k", h=NH)
        qk_t = scr[:, 0:4096].rearrange("p (m s) -> p m s", m=2 * NH)
        vs = scr[:, 4096:6144].rearrange("p (t e) -> p t e", t=T)
        ht32 = scr[:, 0:2048].rearrange("p (k s) -> p k s", k=KC)
        moe_out = scr[:, 2048:4096].rearrange("p (t d) -> p t d", t=T)
        y_e = scr[:, 4096:5120]
        pooled_t = ysb[:, :, :].rearrange("p t (k s) -> p (t k) s", s=S)
        bias_t = ysb[:, :, :].rearrange("p t (k s) -> p (t k) s", s=S)
        att_s = [tmp[:, 1152 * b:1152 * b + 768].rearrange("p (c k) -> p c k", c=2) for b in range(2)]
        att_at = [tmp[:, 1152 * b + 768:1152 * (b + 1)] for b in range(2)]
        sg = tmp[:, 0:512]
        actf = tmp[:, 512:1024]
        sel = tmp[:, 1024:1280].rearrange("p (t s) -> p t s", t=T)
        selg = tmp[:, 1280:1536].rearrange("p (t s) -> p t s", t=T)
        selg_t = tmp[:, 1536:1792]
        rt = tmp[:, 1792:2304]
        logits = rt[:, 0:16].rearrange("p (t e) -> p t e", t=T)
        top = rt[:, 16:32].rearrange("p (t e) -> p t e", t=T)
        idx_f = rt[:, 48:64].rearrange("p (t e) -> p t e", t=T)
        oh = [rt[:, 64 + 16 * i:80 + 16 * i].rearrange("p (t e) -> p t e", t=T) for i in range(2)]
        mask = rt[:, 96:112].rearrange("p (t e) -> p t e", t=T)
        w2 = rt[:, 112:120]
        cnt = rt[:, 120:124]
        diff = rt[:, 124:126]

        top_idx = sb("top_idx", [P, T, 8], U32)

        ps = ctx.enter_context(nc.psum_tensor("ps", [P, 8, 512], F32))

        def bank(b, n=512):
            return ps[:, b, 0:n]

        raw_loaded = [sem(f"raw_loaded{i}") for i in range(RAW)]
        hi_ready = sem("hi_ready")
        unit_done = sem("unit_done")
        unit_used = sem("unit_used")
        x_loaded = sem("x_loaded")
        c_loaded = sem("c_loaded")
        consts_loaded = sem("consts_loaded")
        pool_loaded = sem("pool_loaded")
        small_loaded = sem("small_loaded")
        scale_loaded = sem("scale_loaded")
        gain_loaded = sem("gain_loaded")
        bmod_loaded = sem("bmod_loaded")
        rows_zeroed = sem("rows_zeroed")
        zeros_ready = sem("zeros_ready")
        silu_ready = sem("silu_ready")
        gemv = sem("gemv")
        row_ps = sem("row_ps")
        row_done = sem("row_done")
        ss_ready = sem("ss_ready")
        half_ready = sem("half_ready")
        ms_ready = sem("ms_ready")
        rstd_ready = sem("rstd_ready")
        oms_ready = sem("oms_ready")
        orstd_ready = sem("orstd_ready")
        h_ready = sem("h_ready")
        ht_ps = sem("ht_ps")
        ht_hi = sem("ht_hi")
        ht_lo = sem("ht_lo")
        ht32_ready = sem("ht32_ready")
        x_done = sem("x_done")
        link_s = sem("vector_link")
        dist_ps = sem("dist_ps")
        dist_ready = sem("dist_ready")
        dist_stored = sem("dist_stored")
        bias_loaded = sem("bias_loaded")
        bias_ps = sem("bias_ps")
        bias_ready = sem("bias_ready")
        lam_prod = sem("lam_prod")
        lam_exp = sem("lam_exp")
        pooled_ps = sem("pooled_ps")
        pooled_ready = sem("pooled_ready")
        mix_ps = sem("mix_ps")
        y_scaled = sem("y_scaled")
        f_sg = sem("f_sg")
        f_act = sem("f_act")
        f_ahi = sem("f_ahi")
        f_alo = sem("f_alo")
        qkv_ready = sem("qkv_ready")
        sc_ps = sem("sc_ps")
        sc_max = sem("sc_max")
        sc_exp = sem("sc_exp")
        att_ready = sem("att_ready")
        at_ps = sem("at_ps")
        at_ready = sem("at_ready")
        o_ps = sem("o_ps")
        o_ready = sem("o_ready")
        on_ready = sem("on_ready")
        ot_ps = sem("ot_ps")
        ot_hi = sem("ot_hi")
        ot_lo = sem("ot_lo")
        lg_ps = sem("lg_ps")
        top_ready = sem("top_ready")
        e2_ready = sem("e2_ready")
        mask_ready = sem("mask_ready")
        pos_ps = sem("pos_ps")
        route_ready = sem("route_ready")
        over_ready = sem("over_ready")
        sel_ready = sem("sel_ready")
        selg_ready = sem("selg_ready")
        selt_cleared = sem("selt_cleared")
        selt_ps = sem("selt_ps")
        selt_ready = sem("selt_ready")
        g_ps = sem("g_ps")
        g_hi = sem("g_hi")
        g_lo = sem("g_lo")
        e_sg = sem("e_sg")
        e_act = sem("e_act")
        e_at = sem("e_at")
        e_ahi = sem("e_ahi")
        e_alo = sem("e_alo")
        y_ready = sem("y_ready")
        scat_ps = sem("scat_ps")
        scat_done = sem("scat_done")
        stored = sem("stored")

        block = ctx.enter_context(nc.Block())

        @block.sync
        def _(sp):
            def load(r, rounds, halves):
                if r >= RAW:
                    sp.wait_ge(unit_done, r - RAW + 1 + rounds * RAW)
                dst = raw[:, r % RAW, :]
                for view, src in halves(dst):
                    sp.dma_start(view, src).then_inc(raw_loaded[r % RAW], 16)

            def mod_unit(l, pair, g):
                def halves(dst):
                    for kk in range(2):
                        yield (dst[:, kk * D:(kk + 1) * D],
                               w_mod[l].rearrange("(p k) f -> p k f", k=KC)[:, pair * 2 + kk, g * D:(g + 1) * D])
                return halves

            def gu_unit(w, width, chunk, kh):
                def halves(dst):
                    v = dst.rearrange("p (k g j) -> p k g j", k=4, g=2)
                    src = w.rearrange("(k p) f -> p k f", p=P)
                    for g in range(2):
                        yield v[:, :, g, :], src[:, kh * 4:kh * 4 + 4, bass.ds(chunk * FC + g * width, FC)]
                return halves

            def down_unit(w, chunk):
                def halves(dst):
                    for j in range(2):
                        yield dst[:, j * D:(j + 1) * D], w[bass.ds((chunk * 2 + j) * P, P), :]
                return halves

            def col_unit(w, col, kh):
                def halves(dst):
                    v = dst.rearrange("p (k j) -> p k j", k=4)
                    src = w.rearrange("(k p) f -> p k f", p=P)
                    for i in range(2):
                        yield v[:, 2 * i:2 * i + 2, :], src[:, kh * 4 + 2 * i:kh * 4 + 2 * i + 2, col:col + 512]
                return halves

            sp.dma_start(silu_c[:, :], c.rearrange("a (p k) -> (a p) k", k=KC)).then_inc(c_loaded, 16)
            sp.dma_start(xs[:, :, :], x[0].rearrange("(t p) d -> p t d", p=P)).then_inc(x_loaded, 16)
            for half in range(2):
                for it in range(2):
                    for u in range(6):
                        load(half * 12 + it * 6 + u, 0, mod_unit(0, it * 2 + u // 3, half * 3 + u % 3))
            w_gu, w_dn = ffn_w_gu[0], ffn_w_down[0]
            load(R_FFN, 0, gu_unit(w_gu, FF, 0, 0))
            load(R_FFN + 1, 0, gu_unit(w_gu, FF, 0, 1))
            with sp.Fori(0, MOD_STEPS // 2) as it:
                for st in range(2):
                    r = R_FFN + 2 + 6 * st
                    load(r, it * 2, gu_unit(w_gu, FF, it * 2 + st + 1, 0))
                    load(r + 1, it * 2, gu_unit(w_gu, FF, it * 2 + st + 1, 1))
                    for g in range(3):
                        load(r + 2 + g, it * 2, mod_unit(1, it, st * 3 + g))
                    load(r + 5, it * 2, down_unit(w_dn, it * 2 + st))
            r = R_FFN + 2 + 6 * MOD_STEPS
            for s in range(MOD_STEPS, NCF - 1):
                load(r, 0, gu_unit(w_gu, FF, s + 1, 0))
                load(r + 1, 0, gu_unit(w_gu, FF, s + 1, 1))
                load(r + 2, 0, down_unit(w_dn, s))
                r += 3
            load(r, 0, down_unit(w_dn, NCF - 1))
            for g in range(6):
                for kh in range(2):
                    load(R_QKV + 2 * g + kh, 0, col_unit(w_qkv[0], g * 512, kh))
            for g in range(2):
                for kh in range(2):
                    load(R_WO + 2 * g + kh, 0, col_unit(w_o[0], g * 512, kh))

            def experts(ps_no):
                base = R_MOE + ps_no * NE * EXPERT_UNITS
                with sp.Fori(0, NE) as e:
                    gu, dn, eo = moe_w_gu[0, e], moe_w_down[0, e], e * (EXPERT_UNITS // RAW)
                    for s in range(2):
                        load(base + 2 * s, eo, gu_unit(gu, FE, s, 0))
                        load(base + 2 * s + 1, eo, gu_unit(gu, FE, s, 1))
                    with sp.Fori(0, (NCE - 2) // 2) as it:
                        for st in range(2):
                            r, ro = base + 4 + 3 * st, eo + it
                            load(r, ro, gu_unit(gu, FE, it * 2 + st + 2, 0))
                            load(r + 1, ro, gu_unit(gu, FE, it * 2 + st + 2, 1))
                            load(r + 2, ro, down_unit(dn, it * 2 + st))
                    load(base + 40, eo, down_unit(dn, NCE - 2))
                    load(base + 41, eo, down_unit(dn, NCE - 1))

            experts(0)
            sp.wait_ge(route_ready, 1)
            over = sp.value_load(flag[0:1, 0:1], min_val=0, max_val=1)
            with sp.If(over > 0):
                experts(1)
            for t in range(T):
                sp.wait_ge(x_done, 3 * T + t + 1)
                sp.dma_start(out[0].rearrange("(t p) d -> p t d", p=P)[:, t, :], xs[:, t, :]).then_inc(stored, 16)
            sp.wait_ge(stored, 16 * T)

        @block.gpsimd
        def _(pool):
            pool.memset(rows[:, :, :], 0.0).then_inc(rows_zeroed, 1)
            pool.memset(zeros[:, :], 0.0).then_inc(zeros_ready, 1)
            pool.dma_start(consts[:, :, :], consts_in.rearrange("p (i s) -> p i s", i=5)).then_inc(consts_loaded, 16)
            pool.wait_ge(rows_zeroed, 1)
            pool.dma_start(rows[0:1, 0:6, :], b_mod[0:1, :].rearrange("a (g d) -> a g d", d=D)).then_inc(bmod_loaded, 16)
            pool.dma_start(gain[:, :], norm_g[0, 0, :].partition_broadcast(P)).then_inc(gain_loaded, 16)
            pool.dma_start(pool_m, pool_in.rearrange("p (g s) -> p g s", g=4)).then_inc(pool_loaded, 16)
            pool.dma_start(poolw, pool_w[0].rearrange("g (c p) e -> p g c e", p=P)).then_inc(pool_loaded, 16)
            pool.dma_start(rows[:, 6, :], pool_scale[0, :].partition_broadcast(P)).then_inc(scale_loaded, 16)
            pool.dma_start(onehot, onehot_in).then_inc(small_loaded, 16)
            pool.dma_start(relb, rel_bias).then_inc(small_loaded, 16)
            pool.dma_start(lamv, lambda_vecs[0].partition_broadcast(P)).then_inc(small_loaded, 16)
            pool.dma_start(subln[:, :], subln_g[0, :].partition_broadcast(P)).then_inc(small_loaded, 16)
            pool.dma_start(wr[:, :, :], w_router[0].rearrange("(k p) e -> p k e", p=P)).then_inc(small_loaded, 16)

            def next_gain(i):
                l, j = divmod(i - 1, 4)
                pool.wait_ge(row_done, 6 * l + (1, 2, 4, 5)[j] + 1)
                pool.dma_start(gain[:, :], norm_g[i // 4, i % 4, :].partition_broadcast(P)).then_inc(gain_loaded, 16)

            pool.memset(minus_half[:, :], -0.5).then_inc(half_ready, 1)
            pool.wait_ge(half_ready, 1)

            def inverse_roots(i, col):
                for t in range(T):
                    cc = 4 * i + col + t
                    pool.wait_ge(ms_ready, cc + 1)
                    pool.tensor_tensor(rstd[:, cc:cc + 1], ss[:, cc:cc + 1], minus_half[:, 0:1], ALU.pow).then_inc(rstd_ready, 1)

            next_gain(1)
            pool.wait_ge(dist_ready, 2)
            pool.dma_start(bias_dram, bias_row).then_inc(dist_stored, 16)
            pool.wait_ge(dist_stored, 16)
            pool.wait_ge(lam_exp, 1)
            pool.dma_start(bias_rev, bass.AP(tensor=bias_dram.tensor, offset=0,
                                             ap=[(1, P), (S + P, NH), (1, S)])).then_inc(bias_loaded, 16)
            next_gain(2)
            inverse_roots(0, 0)
            inverse_roots(0, 2)
            next_gain(3)
            next_gain(4)
            inverse_roots(1, 0)
            pool.wait_ge(h_ready, 2 * T)
            pool.memset(rows[:, 0:5, :], 0.0).then_inc(rows_zeroed, 1)
            pool.memset(rows[:, 6, :], 0.0).then_inc(rows_zeroed, 1)
            pool.wait_ge(rows_zeroed, 3)
            pool.dma_start(rows[0:1, 0:5, :], b_mod[1:2, D:6 * D].rearrange("a (g d) -> a g d", d=D)).then_inc(bmod_loaded, 16)
            pool.dma_start(rows[0:1, 6, :], b_mod[1:2, 0:D]).then_inc(bmod_loaded, 16)
            next_gain(5)
            inverse_roots(1, 2)
            inverse_roots(2, 0)
            next_gain(6)
            next_gain(7)
            pool.wait_ge(oms_ready, 1)
            pool.tensor_tensor(oss[:, :, :].rearrange("p t h -> p (t h)"), oss[:, :, :].rearrange("p t h -> p (t h)"),
                               minus_half[:, :], ALU.pow).then_inc(orstd_ready, 1)
            inverse_roots(2, 2)
            inverse_roots(3, 0)
            inverse_roots(3, 2)

        @block.scalar
        def _(act):
            def high(r, q, rounds=0, qo=0):
                act.wait_ge(raw_loaded[r % RAW], 32 * (r // RAW + 1) + 32 * rounds)
                if q >= SPL - 1:
                    act.wait_ge(unit_used, max(q - SPL + 1, 1) + qo)
                act.activation(whi[:, q % SPL, :], raw[:, r % RAW, :], ACT.Copy).then_inc(hi_ready, 1)

            def square_x(i):
                for t in range(T):
                    if i == 0:
                        act.wait_ge(x_loaded, 16)
                    else:
                        act.wait_ge(x_done, T * (i - 1) + t + 1)
                    act.activation(hs[:, t, :], xs[:, t, :], ACT.Square,
                                   accum_out=ss[:, 4 * i + t:4 * i + t + 1]).then_inc(ss_ready, 1)

            def high_transposed(i):
                for b in range(4):
                    act.wait_ge(ht_ps, 4 * (i - 1) + b + 1)
                    act.activation(thi[:, 512 * b:512 * b + 512], bank(b), ACT.Copy).then_inc(ht_hi, 1)

            def square_y_psum(i, q_end):
                act.wait_ge(unit_used, q_end)
                for t in range(T):
                    act.activation(ysb[:, t, :].rearrange("p (h d) -> p h d", h=2), ps[:, 4 + 2 * t:6 + 2 * t, :],
                                   ACT.Square, accum_out=ss[:, 4 * i + 2 + t:4 * i + 3 + t]).then_inc(ss_ready, 1)

            act.wait_ge(c_loaded, 16)
            act.activation(silu_c[:, :], silu_c[:, :], ACT.Silu).then_inc(silu_ready, 1)
            act.wait_ge(lam_prod, 2)
            act.activation(lam[:, 2:4], lam[:, 0:2], ACT.Exp).then_inc(lam_exp, 1)

            square_x(0)
            for b in range(4):
                act.wait_ge(pooled_ps, b + 1)
                act.copy(pooled_t[:, 2 * b:2 * b + 2, :], bank(b).rearrange("p (k s) -> p k s", k=2)).then_inc(pooled_ready, 1)
            for t in range(T):
                act.wait_ge(y_scaled, t + 1)
                act.activation(hs[:, t, :], ysb[:, t, :], ACT.Square, accum_out=ss[:, 2 + t:3 + t]).then_inc(ss_ready, 1)

            square_x(1)
            high(R_FFN, 0)
            high(R_FFN + 1, 1)
            high_transposed(1)

            def ffn_act(s, it=0):
                act.wait_ge(unit_used, 3 * s + 2 + it * 6)
                b = 2 * (s % 2)
                act.activation(sg.rearrange("p (j s) -> p j s", j=2), ps[:, b:b + 2, 0:FC], ACT.Silu).then_inc(f_sg, 1)
                act.wait_ge(f_act, s + 1 + it * 2)
                act.activation(ahi[:, :], actf, ACT.Copy).then_inc(f_ahi, 1)

            def ffn_step(s, r, mod, it=0):
                q = 2 + 3 * s
                high(r, q, it * 2, it * 6)
                high(r + 1, q + 1, it * 2, it * 6)
                ffn_act(s, it)
                high(r + (5 if mod else 2), q + 2, it * 2, it * 6)

            with act.Fori(0, MOD_STEPS // 2) as it:
                for st in range(2):
                    ffn_step(st, R_FFN + 2 + 6 * st, True, it)
            for s in range(MOD_STEPS, NCF - 1):
                ffn_step(s, R_FFN + 2 + 3 * MOD_STEPS + 3 * s, False)
            ffn_act(NCF - 1)
            high(R_QKV - 1, Q_QKV - 1)
            square_y_psum(1, Q_QKV)

            square_x(2)
            high(R_QKV, Q_QKV)
            high(R_QKV + 1, Q_QKV + 1)
            high_transposed(2)
            for b in range(4):
                act.wait_ge(bias_ps, b + 1)
                act.copy(bias_t[:, 2 * b:2 * b + 2, :], bank(b).rearrange("p (h k) -> p h k", h=2)).then_inc(bias_ready, 1)

            def qkv_out(g):
                act.wait_ge(unit_used, Q_QKV + 2 * g + 2)
                src = ps[:, 4 + 2 * (g % 2):6 + 2 * (g % 2), :]
                if g < 4:
                    dst = qk_t[:, 4 * g:4 * g + 4, :].rearrange("p (b m) s -> p b (m s)", b=2)
                else:
                    dst = vs[:, :, (g - 4) * 512:(g - 3) * 512]
                act.copy(dst, src).then_inc(qkv_ready, 1)

            for g in range(1, 6):
                high(R_QKV + 2 * g, Q_QKV + 2 * g)
                high(R_QKV + 2 * g + 1, Q_QKV + 2 * g + 1)
                qkv_out(g - 1)
            qkv_out(5)
            def exps(h):
                act.wait_ge(sc_max, h + 1)
                p = h % 2
                for cc in range(2):
                    for t in range(T):
                        k0, k1 = (0, P) if t == 0 else (P, P + S)
                        act.activation(att_s[p][:, cc, k0:k1], att_s[p][:, cc, k0:k1], ACT.Exp, scale=HD ** -0.5,
                                       bias=stat[:, p, 0, 2 * cc + t:2 * cc + t + 1],
                                       accum_out=stat[:, p, 1, 2 * cc + t:2 * cc + t + 1]).then_inc(sc_exp, 1)

            def at_copy(h):
                act.wait_ge(at_ps, h + 1)
                act.copy(att_at[h % 2], bank(4 + h % 2, 384)).then_inc(at_ready, 1)

            def o_copy(h):
                act.wait_ge(o_ps, h + 1)
                act.copy(hs[:, :, h * P:h * P + P], bank(6 + h % 2, S).rearrange("p (t e) -> p t e", t=T)).then_inc(o_ready, 1)

            exps(0)
            for h in range(NH):
                if h + 1 < NH:
                    exps(h + 1)
                at_copy(h)
                if h > 0:
                    o_copy(h - 1)
            o_copy(NH - 1)
            for u in range(3):
                high(R_WO + u, Q_WO + u)
            for b in range(4):
                act.wait_ge(ot_ps, b + 1)
                act.activation(thi[:, 512 * b:512 * b + 512], bank(b), ACT.Copy).then_inc(ot_hi, 1)
            high(R_WO + 3, Q_WO + 3)
            square_y_psum(2, Q_MOE)

            square_x(3)
            for b in range(4):
                act.wait_ge(ht_ps, 4 * 2 + b + 1)
                act.copy(ht32[:, 2 * b:2 * b + 2, :], bank(b).rearrange("p (k s) -> p k s", k=2)).then_inc(ht32_ready, 1)
            act.wait_ge(top_ready, 1)
            act.activation(w2[:, 0:2], diff, ACT.Exp).then_inc(e2_ready, 1)

            def experts(ps_no):
                r0, q0, j0 = (R_MOE + ps_no * NE * EXPERT_UNITS, Q_MOE + ps_no * NE * EXPERT_UNITS, ps_no * NE)
                n0 = ps_no * (NE + 1)

                def gathered_high(n):
                    for b in range(2):
                        act.wait_ge(g_ps, 2 * n + b + 1)
                        act.activation(thi[:, 512 * b:512 * b + 512], bank(6 + b), ACT.Copy).then_inc(g_hi, 1)

                def expert_out(used):
                    act.wait_ge(unit_used, used)
                    for b in range(2):
                        act.copy(y_e[:, 512 * b:512 * b + 512], bank(4 + b)).then_inc(y_ready, 1)

                gathered_high(n0)
                with act.Fori(0, NE) as e:
                    j, ro, qo = e + j0, e * (EXPERT_UNITS // RAW), e * EXPERT_UNITS

                    def silu_gate(s, used, it=0):
                        act.wait_ge(unit_used, q0 + used + qo + it * 6)
                        act.activation(sg[:, 0:FC], bank(s % 2)[:, 0:FC], ACT.Silu).then_inc(e_sg, 1)

                    def act_high(s, so=0):
                        act.wait_ge(e_at, j * NCE + s + 1 + so)
                        act.activation(ahi[:, (s % 2) * FC:(s % 2) * FC + FC], bank(2 + s % 2, FC), ACT.Copy).then_inc(e_ahi, 1)

                    for u in range(3):
                        high(r0 + u, q0 + u, ro, qo)
                    expert_out(q0 + qo)
                    silu_gate(0, 2)
                    high(r0 + 3, q0 + 3, ro, qo)
                    with act.Fori(0, (NCE - 2) // 2) as it:
                        for st in range(2):
                            u = 4 + 3 * st
                            high(r0 + u, q0 + u, ro + it, qo + it * 6)
                            high(r0 + u + 1, q0 + u + 1, ro + it, qo + it * 6)
                            act_high(st, it * 2)
                            silu_gate(st + 1, 4 + 2 * st, it)
                            high(r0 + u + 2, q0 + u + 2, ro + it, qo + it * 6)
                    act_high(NCE - 2)
                    silu_gate(NCE - 1, EXPERT_UNITS - 3)
                    high(r0 + 40, q0 + 40, ro, qo)
                    act.wait_ge(selt_ps, j + 1)
                    act.copy(selg_t, bank(0, S)).then_inc(selt_ready, 1)
                    gathered_high(e + n0 + 1)
                    act_high(NCE - 1)
                    high(r0 + 41, q0 + 41, ro, qo)
                expert_out(q0 + NE * EXPERT_UNITS)

            experts(0)
            act.wait_ge(route_ready, 1)
            over = act.value_load(flag[0:1, 0:1], min_val=0, max_val=1)
            with act.If(over > 0):
                experts(1)

        @block.vector
        def _(dve):
            links = [0]

            def link(ins):
                links[0] += 1
                ins.then_inc(link_s, 1)
                dve.wait_ge(link_s, links[0])

            def low(r, q, rounds=0, qo=0):
                dve.wait_ge(hi_ready, q + 1 + qo)
                dve.tensor_tensor(wlo[:, q % SPL, :], raw[:, r % RAW, :], whi[:, q % SPL, :].bitcast(F32),
                                  ALU.subtract).then_inc(unit_done, 1)

            def low_from(dst, src, hi_part, sem_out):
                dve.tensor_tensor(dst, src, hi_part.bitcast(F32), ALU.subtract).then_inc(sem_out, 1)

            def gemv_step(r, row_slots, cols, n, prev, rounds=0, no=0, ro=0):
                for kk in range(2):
                    for u in range(3):
                        if kk == 0:
                            dve.wait_ge(raw_loaded[(r + u) % RAW], 32 * ((r + u) // RAW + 1) + 32 * rounds)
                            if prev is not None:
                                dve.wait_ge(unit_done, prev + u + 1 + ro)
                        else:
                            dve.wait_ge(gemv, 3 * n + u + 1 + no)
                        row = rows[:, row_slots[u], :]
                        dve.scalar_tensor_tensor(row, raw[:, (r + u) % RAW, kk * D:kk * D + D], cols[kk], row,
                                                 ALU.mult, ALU.add).then_inc(unit_done if kk else gemv, 1)

            def finish_rows(l, groups):
                for g in groups:
                    n = 6 * l + g
                    dve.wait_ge(row_ps, n + 1)
                    b = 6 if l == 0 else 2 * (g % 2)
                    src = ps[:, b:b + 2, :]
                    row = rows[:, ROW[l][g], :].rearrange("p (h d) -> p h d", h=2)
                    gv = gain[:, :].rearrange("p (h d) -> p h d", h=2)
                    if g % 3:
                        dve.wait_ge(gain_loaded, 16 * (4 * l + {1: 0, 2: 1, 4: 2, 5: 3}[g] + 1))
                    if g % 3 == 0:
                        dve.tensor_copy(row, src).then_inc(row_done, 1)
                    elif g % 3 == 1:
                        dve.scalar_tensor_tensor(row, src, 1.0, gv, ALU.add, ALU.mult).then_inc(row_done, 1)
                    else:
                        dve.tensor_tensor(row, src, gv, ALU.mult).then_inc(row_done, 1)

            def inverse_root(i, t, col):
                dve.wait_ge(ss_ready, 4 * i + col + 1)
                cc = 4 * i + col
                dve.tensor_scalar(ss[:, cc:cc + 1], ss[:, cc:cc + 1], 1.0 / D, EPS, ALU.mult, ALU.add).then_inc(ms_ready, 1)
                dve.wait_ge(rstd_ready, cc + 1)
                return rstd[:, cc:cc + 1]

            def modulated(i):
                l, g = divmod(i, 2)
                dve.wait_ge(row_done, 6 * l + 3 * g + 2)
                for t in range(T):
                    rs = inverse_root(i, t, t)
                    link(dve.scalar_tensor_tensor(hs[:, t, :], xs[:, t, :], rs, rows[:, ROW[l][3 * g + 1], :], ALU.mult, ALU.mult))
                    dve.tensor_tensor(hs[:, t, :], hs[:, t, :], rows[:, ROW[l][3 * g], :], ALU.add).then_inc(h_ready, 1)

            def residual(i, y_of):
                l, g = divmod(i, 2)
                dve.wait_ge(row_done, 6 * l + 3 * g + 3)
                for t in range(T):
                    rs = inverse_root(i, t, 2 + t)
                    y = y_of(t)
                    dst, gv = ysb[:, t, :], rows[:, ROW[l][3 * g + 2], :]
                    if len(y.shape) == 3:
                        dst, gv = (v.rearrange("p (h d) -> p h d", h=2) for v in (dst, gv))
                    link(dve.scalar_tensor_tensor(dst, y, rs, gv, ALU.mult, ALU.mult))
                    dve.tensor_tensor(xs[:, t, :], xs[:, t, :], ysb[:, t, :], ALU.add).then_inc(x_done, 1)

            def low_transposed(i):
                for b in range(4):
                    dve.wait_ge(ht_hi, 4 * (i - 1) + b + 1)
                    low_from(tlo[:, 512 * b:512 * b + 512], bank(b), thi[:, 512 * b:512 * b + 512], ht_lo)

            dve.wait_ge(small_loaded, 80)
            dve.memset(bias_row[:, S:S + P], NEG).then_inc(dist_ready, 1)
            dve.wait_ge(dist_ps, 1)
            dve.tensor_scalar(bias_row[:, 0:S], ps[0:NH, 5, 0:S], HD ** 0.5, None, ALU.mult).then_inc(dist_ready, 1)
            for i in range(2):
                if i:
                    dve.wait_ge(lam_prod, 1)
                dve.tensor_tensor_reduce(lamj, lamv[:, 2 * i, :], lamv[:, 2 * i + 1, :], 1.0, 0.0,
                                         ALU.mult, ALU.add, lam[:, i:i + 1]).then_inc(lam_prod, 1)
            dve.wait_ge(lam_exp, 1)
            link(dve.tensor_tensor(lam[:, 0:1], lam[:, 3:4], lam[:, 2:3], ALU.subtract))
            link(dve.tensor_scalar(lam[:, 0:1], lam[:, 0:1], -LAMBDA_INIT, None, ALU.add))
            link(dve.tensor_scalar(subln[:, :], subln[:, :], 1.0 - LAMBDA_INIT, None, ALU.mult))

            dve.wait_ge(silu_ready, 1)
            dve.wait_ge(bmod_loaded, 16)
            for n in range(4):
                gemv_step(3 * n, [0, 1, 2], [silu_c[:, 2 * n + kk:2 * n + kk + 1] for kk in range(2)], n,
                          3 * (n - 1) if n else None)
            finish_rows(0, (0, 1, 2))
            modulated(0)
            for n in range(4, 8):
                m = n - 4
                gemv_step(3 * n, [3, 4, 5], [silu_c[:, 2 * m + kk:2 * m + kk + 1] for kk in range(2)], n,
                          3 * (n - 1) if m else None)
            dve.wait_ge(scale_loaded, 16)
            dve.wait_ge(mix_ps, 1)
            for t in range(T):
                dve.tensor_tensor(ysb[:, t, :].rearrange("p (h d) -> p h d", h=2), ps[:, 4 + 2 * t:6 + 2 * t, :],
                                  rows[:, 6, :].rearrange("p (h d) -> p h d", h=2), ALU.mult).then_inc(y_scaled, 1)
            dve.wait_ge(y_scaled, T)
            residual(0, lambda t: ysb[:, t, :])
            finish_rows(0, (3, 4, 5))

            modulated(1)
            low(R_FFN, 0)
            low(R_FFN + 1, 1)
            low_transposed(1)
            dve.wait_ge(bmod_loaded, 48)

            def ffn_act(s, so=0):
                dve.wait_ge(f_sg, s + 1 + so)
                b = 2 * (s % 2)
                dve.tensor_tensor(actf.rearrange("p (j s) -> p j s", j=2), sg.rearrange("p (j s) -> p j s", j=2),
                                  ps[:, b:b + 2, FC:2 * FC], ALU.mult).then_inc(f_act, 1)
                dve.wait_ge(f_ahi, s + 1 + so)
                low_from(alo[:, :], actf, ahi[:, :], f_alo)

            with dve.Fori(0, MOD_STEPS // 2) as it:
                for st in range(2):
                    r, q = R_FFN + 2 + 6 * st, 2 + 3 * st
                    low(r, q, it * 2, it * 6)
                    low(r + 1, q + 1, it * 2, it * 6)
                    gemv_step(r + 2, [ROW[1][3 * st + u] for u in range(3)],
                              [silu_c[:, bass.ds(it * 2 + kk, 1)] for kk in range(2)],
                              MOD_STEPS + st, r + 2 - 2 * RAW, it * 2, it * 6, it * 12)
                    ffn_act(st, it * 2)
                    low(r + 5, q + 2, it * 2, it * 6)
            for s in range(MOD_STEPS, NCF - 1):
                r = R_FFN + 2 + 3 * MOD_STEPS + 3 * s
                low(r, 2 + 3 * s)
                low(r + 1, 3 + 3 * s)
                ffn_act(s)
                low(r + 2, 4 + 3 * s)
            ffn_act(NCF - 1)
            low(R_QKV - 1, Q_QKV - 1)
            finish_rows(1, (0, 1))
            residual(1, lambda t: ps[:, 4 + 2 * t:6 + 2 * t, :])

            modulated(2)
            low(R_QKV, Q_QKV)
            low(R_QKV + 1, Q_QKV + 1)
            low_transposed(2)
            for g in range(1, 6):
                low(R_QKV + 2 * g, Q_QKV + 2 * g)
                low(R_QKV + 2 * g + 1, Q_QKV + 2 * g + 1)
                if g in (1, 3):
                    finish_rows(1, (g + 1, g + 2))
            dve.wait_ge(bias_ready, 4)

            def row_max(h):
                dve.wait_ge(sc_ps, h + 1)
                p = h % 2
                for cc in range(2):
                    for t in range(T):
                        k0, k1 = (0, P) if t == 0 else (P, P + S)
                        ins = dve.tensor_tensor_reduce(att_s[p][:, cc, k0:k1], ps[:, 2 * p + cc, k0:k1],
                                                       bias_t[:, h, P:S] if t == 0 else bias_t[:, h, :], 1.0, NEG,
                                                       ALU.add, ALU.max, stat[:, p, 0, 2 * cc + t:2 * cc + t + 1])
                link(ins)
                dve.tensor_scalar(stat[:, p, 0, :], stat[:, p, 0, :], -HD ** -0.5, None, ALU.mult).then_inc(sc_max, 1)

            def combine(h):
                p = h % 2
                dve.wait_ge(sc_exp, 4 * h + 4)
                link(dve.reciprocal(stat[:, p, 2, :], stat[:, p, 1, :]))
                link(dve.tensor_scalar(stat[:, p, 2, 2:4], stat[:, p, 2, 2:4], lam[:, 0:1], None, ALU.mult))
                cuts = ((0, P), (P, P + S))
                for t, (k0, k1) in enumerate(cuts):
                    ins = dve.tensor_scalar(att_s[p][:, 0, k0:k1], att_s[p][:, 0, k0:k1], stat[:, p, 2, t:t + 1], None, ALU.mult)
                link(ins)
                for t, (k0, k1) in enumerate(cuts):
                    ins = dve.scalar_tensor_tensor(att_s[p][:, 0, k0:k1], att_s[p][:, 1, k0:k1], stat[:, p, 2, 2 + t:3 + t],
                                                   att_s[p][:, 0, k0:k1], ALU.mult, ALU.add)
                ins.then_inc(att_ready, 1)

            row_max(0)
            for h in range(NH):
                if h + 1 < NH:
                    if h > 0:
                        dve.wait_ge(at_ps, h)
                    row_max(h + 1)
                combine(h)
            dve.wait_ge(o_ready, NH)
            for t in range(T):
                link(dve.tensor_tensor(ysb[:, t, :], hs[:, t, :], hs[:, t, :], ALU.mult))
                link(dve.tensor_reduce(oss[:, t, :], ysb[:, t, :].rearrange("p (h e) -> p h e", h=NH), AX_X, ALU.add))
            dve.tensor_scalar(oss[:, :, :], oss[:, :, :], 1.0 / P, EPS, ALU.mult, ALU.add).then_inc(oms_ready, 1)
            dve.wait_ge(orstd_ready, 1)
            for t in range(T):
                o = hs[:, t, :].rearrange("p (h e) -> p h e", h=NH)
                link(dve.tensor_tensor(o, o, oss[:, t, :].unsqueeze(2).broadcast_to([P, NH, P]), ALU.mult))
                dve.tensor_tensor(o, o, subln[:, :].unsqueeze(1).broadcast_to([P, NH, P]), ALU.mult).then_inc(on_ready, 1)
            for u in range(3):
                low(R_WO + u, Q_WO + u)
            for b in range(4):
                dve.wait_ge(ot_hi, b + 1)
                low_from(tlo[:, 512 * b:512 * b + 512], bank(b), thi[:, 512 * b:512 * b + 512], ot_lo)
            low(R_WO + 3, Q_WO + 3)
            residual(2, lambda t: ps[:, 4 + 2 * t:6 + 2 * t, :])

            modulated(3)
            dve.wait_ge(lg_ps, 1)
            link(dve.tensor_copy(logits, bank(4, 16).rearrange("p (t e) -> p t e", t=T)))
            for t in range(T):
                ins = dve.max(top[:, t, :], logits[:, t, :])
            link(ins)
            dve.tensor_tensor(diff, top[:, :, 1], top[:, :, 0], ALU.subtract).then_inc(top_ready, 1)
            for t in range(T):
                ins = dve.max_index(top_idx[:, t, :], top[:, t, :], logits[:, t, :])
            link(ins)
            link(dve.tensor_copy(idx_f, top_idx[:, :, :]))
            for i in range(2):
                for t in range(T):
                    ins = dve.tensor_scalar(oh[i][:, t, :], slots[:, 0:NE], idx_f[:, t, i:i + 1], None, ALU.is_equal)
            link(ins)
            dve.tensor_tensor(mask, oh[0], oh[1], ALU.add).then_inc(mask_ready, 1)
            dve.wait_ge(e2_ready, 1)
            link(dve.tensor_scalar(w2[:, 2:4], w2[:, 0:2], 1.0, None, ALU.add))
            link(dve.reciprocal(w2[:, 4:6], w2[:, 2:4]))
            link(dve.tensor_tensor(w2[:, 6:8], w2[:, 4:6], w2[:, 0:2], ALU.mult))
            for t in range(T):
                link(dve.tensor_scalar(gates[:, t, :], oh[0][:, t, :], w2[:, 4 + t:5 + t], None, ALU.mult))
                link(dve.scalar_tensor_tensor(gates[:, t, :], oh[1][:, t, :], w2[:, 6 + t:7 + t], gates[:, t, :], ALU.mult, ALU.add))
            dve.wait_ge(pos_ps, 1)
            link(dve.scalar_tensor_tensor(posm[:, :, 0:NE], bank(5, 16).rearrange("p (t e) -> p t e", t=T), 1.0, mask, ALU.add, ALU.mult))
            dve.memset(posm[:, :, NE:NE + 1], -1.0)
            link(dve.tensor_scalar(posm[:, :, 0:NE], posm[:, :, 0:NE], -1.0, None, ALU.add))
            link(dve.tensor_reduce(cnt[:, 0:1], ps[:, 5, 16:24], AX_X, ALU.max))
            link(dve.tensor_scalar(cnt[:, 1:2], cnt[:, 0:1], float(P), None, ALU.is_gt))
            link(dve.memset(moe_out, 0.0))
            dve.tensor_copy(flag[:, :], cnt[:, 1:2]).then_inc(route_ready, 1)

            def experts(ps_no):
                r0, q0, j0 = (R_MOE + ps_no * NE * EXPERT_UNITS, Q_MOE + ps_no * NE * EXPERT_UNITS, ps_no * NE)
                n0 = ps_no * (NE + 1)

                def select(e):
                    for t in range(T):
                        dve.tensor_scalar(sel[:, t, :], slots, posm[:, t, bass.ds(e, 1)], None, ALU.is_equal).then_inc(sel_ready, 1)

                def gathered_low(n):
                    for b in range(2):
                        dve.wait_ge(g_hi, 2 * n + b + 1)
                        low_from(tlo[:, 512 * b:512 * b + 512], bank(6 + b), thi[:, 512 * b:512 * b + 512], g_lo)

                def add_scattered(n):
                    for t in range(T):
                        for half in range(2):
                            dve.wait_ge(scat_ps, 4 * n + 2 * t + half + 1)
                            dst = moe_out[:, t, half * 512:half * 512 + 512]
                            dve.tensor_tensor(dst, dst, bank(6 - 4 * t + half), ALU.add).then_inc(scat_done, 1)

                dve.memset(selg_t, 0.0).then_inc(selt_cleared, 1)
                select(0)
                gathered_low(n0)
                with dve.Fori(0, NE) as e:
                    j, ro, qo = e + j0, e * (EXPERT_UNITS // RAW), e * EXPERT_UNITS

                    def times_up(s, so=0):
                        dve.wait_ge(e_sg, j * NCE + s + 1 + so)
                        dve.tensor_tensor(actf[:, 0:FC], sg[:, 0:FC], bank(s % 2)[:, FC:2 * FC], ALU.mult).then_inc(e_act, 1)

                    def act_low(s, so=0):
                        dve.wait_ge(e_ahi, j * NCE + s + 1 + so)
                        a = (s % 2) * FC
                        low_from(alo[:, a:a + FC], bank(2 + s % 2, FC), ahi[:, a:a + FC], e_alo)

                    for u in range(3):
                        low(r0 + u, q0 + u, ro, qo)
                    times_up(0)
                    low(r0 + 3, q0 + 3, ro, qo)
                    add_scattered(e + n0)
                    for t in range(T):
                        dve.tensor_scalar(selg[:, t, :], slots, posm[:, t, bass.ds(e, 1)], gates[:, t, bass.ds(e, 1)],
                                          ALU.is_equal, ALU.mult).then_inc(selg_ready, 1)
                    select(e + 1)
                    with dve.Fori(0, (NCE - 2) // 2) as it:
                        for st in range(2):
                            u = 4 + 3 * st
                            low(r0 + u, q0 + u, ro + it, qo + it * 6)
                            low(r0 + u + 1, q0 + u + 1, ro + it, qo + it * 6)
                            act_low(st, it * 2)
                            times_up(st + 1, it * 2)
                            low(r0 + u + 2, q0 + u + 2, ro + it, qo + it * 6)
                    act_low(NCE - 2)
                    times_up(NCE - 1)
                    low(r0 + 40, q0 + 40, ro, qo)
                    gathered_low(e + n0 + 1)
                    act_low(NCE - 1)
                    low(r0 + 41, q0 + 41, ro, qo)
                add_scattered(n0 + NE)
                dve.wait_ge(scat_done, 4 * (n0 + NE + 1))

            dve.wait_ge(route_ready, 1)
            experts(0)
            over = dve.value_load(flag[0:1, 0:1], min_val=0, max_val=1)
            with dve.If(over > 0):
                link_less = dve.tensor_scalar(posm[:, :, :], posm[:, :, :], float(-P), None, ALU.add)
                link_less.then_inc(over_ready, 1)
                dve.wait_ge(over_ready, 1)
                experts(1)
            for t in range(T):
                dve.tensor_tensor_reduce(ysb[:, t, :], moe_out[:, t, :], moe_out[:, t, :], 1.0, 0.0,
                                         ALU.mult, ALU.add, ss[:, 14 + t:15 + t]).then_inc(ss_ready, 1)
            residual(3, lambda t: moe_out[:, t, :])

        @block.tensor
        def _(pe):
            def row_sum(l, g):
                n = 6 * l + g
                b = 6 if l == 0 else 2 * (g % 2)
                if n % 6 >= (1 if l == 0 else 2):
                    pe.wait_ge(row_done, n - (0 if l == 0 else 1))
                for h in range(2):
                    mm = pe.matmul(bank(b + h), ones, rows[:, ROW[l][g], h * 512:h * 512 + 512], start=True, stop=True)
                mm.then_inc(row_ps, 1)

            def transposes(done):
                for b in range(4):
                    for k in (2 * b, 2 * b + 1):
                        for t in range(T):
                            c0 = (k % 2) * S + t * P
                            mm = pe.transpose(ps[:, b, c0:c0 + P], hs[:, t, k * P:k * P + P], ident)
                    mm.then_inc(done, 1)

            def three(out, a_hi, a_lo, b_hi, b_lo, start, stop, check):
                pe.matmul(out, a_hi, b_hi, start=start, stop=False, skip_group_check=check)
                pe.matmul(out, a_hi, b_lo, start=False, stop=False, skip_group_check=check)
                return pe.matmul(out, a_lo, b_hi, start=False, stop=stop, skip_group_check=check)

            def zero_bank(b):
                for h in range(4):
                    pe.matmul(ps[:, b, h * P:h * P + P], zeros[:, :], zeros[:, :], start=(h == 0), stop=False,
                              skip_group_check=True)

            pe.wait_ge(consts_loaded, 16)
            pe.wait_ge(small_loaded, 80)
            pe.matmul(ps[0:NH, 5, 0:S], relb, onehot, start=True, stop=True).then_inc(dist_ps, 1)
            pe.wait_ge(unit_done, 12)
            for g in range(3):
                row_sum(0, g)
            pe.wait_ge(pool_loaded, 32)
            pe.wait_ge(h_ready, T)
            for b in range(4):
                for t in range(T):
                    for k in (2 * b, 2 * b + 1):
                        c0 = (k % 2) * S
                        g = k // 2
                        if t == 0:
                            mm = pe.matmul(ps[:, b, c0:c0 + S], hs[:, 0, k * P:k * P + P], pool_m[:, g, 0:S],
                                           start=(k % 2 == 0), stop=False, skip_group_check=True)
                        else:
                            mm = pe.matmul(ps[:, b, c0 + P:c0 + S], hs[:, 1, k * P:k * P + P], pool_m[:, g, S:S + P],
                                           start=False, stop=True, skip_group_check=True)
                mm.then_inc(pooled_ps, 1)
            pe.wait_ge(pooled_ready, 4)
            pe.wait_ge(row_done, 3)
            pe.wait_ge(dist_ready, 2)
            for t in range(T):
                for g in range(4):
                    for k in range(2):
                        mm = pe.matmul(ps[:, 4 + 2 * t + g // 2, (g % 2) * FC:(g % 2) * FC + FC],
                                       pooled_t[:, 2 * g + k, t * P:t * P + P], poolw[:, g, k, :],
                                       start=(g % 2 == 0 and k == 0), stop=(k == 1), skip_group_check=True)
            mm.then_inc(mix_ps, 1)
            pe.wait_ge(unit_done, 24)
            pe.wait_ge(y_scaled, T)
            for g in range(3, 6):
                row_sum(0, g)
            pe.wait_ge(h_ready, 2 * T)
            transposes(ht_ps)
            pe.wait_ge(ht_lo, 4)
            pe.wait_ge(zeros_ready, 1)
            pe.wait_ge(row_done, 6)
            for b in range(4, 8):
                zero_bank(b)

            def ffn_gate_up(s, r, q, it=0):
                for kh in range(2):
                    pe.wait_ge(unit_done, r + kh + 1 + it * 12)
                    sl = (q + kh) % SPL
                    for kk in range(4):
                        k = 4 * kh + kk
                        for jj in range(2):
                            for g in range(2):
                                c0 = kk * 512 + g * FC + jj * P
                                o = ps[:, 2 * (s % 2) + jj, g * S:g * S + S]
                                mm = three(o, whi[:, sl, c0:c0 + P], wlo[:, sl, c0:c0 + P], thi3[:, k, :], tlo3[:, k, :],
                                           k == 0 and g == 0, k == KC - 1 and g == 1, True)
                    mm.then_inc(unit_used, 1)

            def ffn_down(s, r, q, it=0, last=False):
                pe.wait_ge(f_alo, s + 1 + it * 2)
                pe.wait_ge(unit_done, r + 1 + it * 12)
                sl = q % SPL
                for jj in range(2):
                    for t in range(T):
                        a = slice(jj * S + t * P, jj * S + t * P + P)
                        for half in range(2):
                            w = slice(jj * D + half * 512, jj * D + half * 512 + 512)
                            mm = three(bank(4 + 2 * t + half), ahi[:, a], alo[:, a], whi[:, sl, w], wlo[:, sl, w],
                                       False, last and jj == 1, True)
                mm.then_inc(unit_used, 1)

            ffn_gate_up(0, R_FFN, 0)
            with pe.Fori(0, MOD_STEPS // 2) as it:
                for st in range(2):
                    r, q = R_FFN + 2 + 6 * st, 2 + 3 * st
                    ffn_gate_up(st + 1, r, q, it)
                    ffn_down(st, r + 5, q + 2, it)
            for s in range(MOD_STEPS, NCF - 1):
                r, q = R_FFN + 2 + 3 * MOD_STEPS + 3 * s, 2 + 3 * s
                ffn_gate_up(s + 1, r, q)
                ffn_down(s, r + 2, q + 2)
            ffn_down(NCF - 1, R_QKV - 1, Q_QKV - 1, last=True)

            pe.wait_ge(unit_done, R_QKV - 1)
            row_sum(1, 0)
            row_sum(1, 1)
            pe.wait_ge(h_ready, 3 * T)
            transposes(ht_ps)
            pe.wait_ge(ht_lo, 8)
            pe.wait_ge(bias_loaded, 16)
            for b in range(4):
                pe.matmul(bank(b), reverse, bias_rev[:, 2 * b:2 * b + 2, :].rearrange("p h k -> p (h k)"),
                          start=True, stop=True).then_inc(bias_ps, 1)

            def qkv_group(g):
                if g >= 2:
                    pe.wait_ge(qkv_ready, g - 1)
                for kh in range(2):
                    r, q = R_QKV + 2 * g + kh, Q_QKV + 2 * g + kh
                    pe.wait_ge(unit_done, r + 1)
                    for kk in range(4):
                        k = 4 * kh + kk
                        if g < 4:
                            for m in range(4):
                                c0 = kk * 512 + m * P
                                o = ps[:, 4 + 2 * (g % 2) + m // 2, (m % 2) * S:(m % 2) * S + S]
                                mm = three(o, whi[:, q % SPL, c0:c0 + P], wlo[:, q % SPL, c0:c0 + P],
                                           thi3[:, k, :], tlo3[:, k, :], k == 0 and m % 2 == 0, k == KC - 1 and m % 2 == 1, True)
                        else:
                            for t in range(T):
                                w = slice(kk * 512, kk * 512 + 512)
                                mm = three(bank(4 + 2 * (g % 2) + t), thi3[:, k, t * P:t * P + P], tlo3[:, k, t * P:t * P + P],
                                           whi[:, q % SPL, w], wlo[:, q % SPL, w], k == 0, k == KC - 1, False)
                    mm.then_inc(unit_used, 1)

            for g in range(6):
                qkv_group(g)
                if g in (0, 2):
                    pe.wait_ge(bias_ready, 4)
                    row_sum(1, g + 2)
                    row_sum(1, g + 3)
            pe.wait_ge(qkv_ready, 6)
            pe.wait_ge(row_done, 12)

            def scores(h):
                if h >= 2:
                    pe.wait_ge(sc_max, h - 1)
                for cc in range(2):
                    rows_c = slice(cc * HD, cc * HD + HD)
                    b = 2 * (h % 2) + cc
                    pe.matmul(ps[:, b, 0:P], qk_t[rows_c, h, 0:P], qk_t[rows_c, NH + h, 0:P], start=True, stop=True)
                    mm = pe.matmul(ps[:, b, P:P + S], qk_t[rows_c, h, P:S], qk_t[rows_c, NH + h, :], start=True, stop=True)
                mm.then_inc(sc_ps, 1)

            def values(h):
                pe.wait_ge(at_ready, h + 1)
                if h >= 2:
                    pe.wait_ge(o_ready, h - 1)
                b, at, cols = 6 + h % 2, att_at[h % 2], slice(h * P, h * P + P)
                pe.matmul(ps[:, b, 0:P], at[:, 0:P], vs[:, 0, cols], start=True, stop=True)
                pe.matmul(ps[:, b, P:S], at[:, P:2 * P], vs[:, 0, cols], start=True, stop=False)
                pe.matmul(ps[:, b, P:S], at[:, 2 * P:3 * P], vs[:, 1, cols], start=False, stop=True).then_inc(o_ps, 1)

            scores(0)
            for h in range(NH):
                if h + 1 < NH:
                    scores(h + 1)
                if h > 0:
                    values(h - 1)
                pe.wait_ge(att_ready, h + 1)
                for i in range(3):
                    mm = pe.transpose(ps[:, 4 + h % 2, i * P:i * P + P], att_s[h % 2][:, 0, i * P:i * P + P], ident)
                mm.then_inc(at_ps, 1)
            values(NH - 1)
            pe.wait_ge(on_ready, T)
            transposes(ot_ps)
            pe.wait_ge(ot_lo, 4)
            for half in range(2):
                for kh in range(2):
                    r, q = R_WO + 2 * half + kh, Q_WO + 2 * half + kh
                    pe.wait_ge(unit_done, r + 1)
                    for kk in range(4):
                        k, w = 4 * kh + kk, slice(kk * 512, kk * 512 + 512)
                        for t in range(T):
                            mm = three(bank(4 + 2 * t + half), thi3[:, k, t * P:t * P + P], tlo3[:, k, t * P:t * P + P],
                                       whi[:, q % SPL, w], wlo[:, q % SPL, w], k == 0, k == KC - 1, False)
                    mm.then_inc(unit_used, 1)

            pe.wait_ge(h_ready, 4 * T)
            transposes(ht_ps)
            pe.wait_ge(ht32_ready, 4)
            for t in range(T):
                for k in range(KC):
                    mm = pe.matmul(ps[:, 4, t * NE:t * NE + NE], ht32[:, k, t * P:t * P + P], wr[:, k, :],
                                   start=(k == 0), stop=(k == KC - 1))
            mm.then_inc(lg_ps, 1)
            pe.wait_ge(mask_ready, 1)
            pe.matmul(ps[:, 5, 0:NE], before, mask[:, 0, :], start=True, stop=True)
            pe.matmul(ps[:, 5, NE:2 * NE], ones, mask[:, 0, :], start=True, stop=False)
            pe.matmul(ps[:, 5, NE:2 * NE], before, mask[:, 1, :], start=False, stop=True)
            pe.matmul(ps[:, 5, 2 * NE:3 * NE], ones, mask[:, 0, :], start=True, stop=False)
            pe.matmul(ps[:, 5, 2 * NE:3 * NE], ones, mask[:, 1, :], start=False, stop=True).then_inc(pos_ps, 1)

            def experts(ps_no):
                r0, q0, j0 = (R_MOE + ps_no * NE * EXPERT_UNITS, Q_MOE + ps_no * NE * EXPERT_UNITS, ps_no * NE)
                n0 = ps_no * (NE + 1)

                def gather(n):
                    pe.wait_ge(sel_ready, T * n + T)
                    for b in range(2):
                        for k in range(4 * b, 4 * b + 4):
                            for t in range(T):
                                mm = pe.matmul(ps[:, 6 + b, (k % 4) * P:(k % 4) * P + P], hs[:, t, k * P:k * P + P],
                                               sel[:, t, :], start=(t == 0), stop=(t == T - 1))
                        mm.then_inc(g_ps, 1)

                def scatter(n):
                    pe.wait_ge(y_ready, 2 * n + 2)
                    for t in range(T):
                        for half in range(2):
                            pe.matmul(bank(6 - 4 * t + half), selg_t[:, t * P:t * P + P], y_e[:, half * 512:half * 512 + 512],
                                      start=True, stop=True).then_inc(scat_ps, 1)

                pe.wait_ge(selt_cleared, ps_no + 1)
                gather(n0)
                with pe.Fori(0, NE) as e:
                    j, ro = e + j0, e * EXPERT_UNITS

                    def gate_up(s, u, it=0):
                        for kh in range(2):
                            pe.wait_ge(unit_done, r0 + u + kh + 1 + ro + it * 6)
                            sl = (q0 + u + kh) % SPL
                            for kk in range(4):
                                k, w = 4 * kh + kk, slice(kk * 512, kk * 512 + 512)
                                mm = three(bank(s % 2), ghi[:, k, :], glo[:, k, :], whi[:, sl, w], wlo[:, sl, w],
                                           k == 0, k == KC - 1, False)
                            mm.then_inc(unit_used, 1)

                    def turn(s, it=0):
                        pe.wait_ge(e_act, j * NCE + s + 1 + it * 2)
                        for jj in range(2):
                            mm = pe.transpose(ps[:, 2 + s % 2, jj * P:jj * P + P], actf[:, jj * P:jj * P + P], ident)
                        mm.then_inc(e_at, 1)

                    def down(s, u, it=0, last=False):
                        pe.wait_ge(e_alo, j * NCE + s + 1 + it * 2)
                        pe.wait_ge(unit_done, r0 + u + 1 + ro + it * 6)
                        sl = (q0 + u) % SPL
                        for jj in range(2):
                            a = slice((s % 2) * FC + jj * P, (s % 2) * FC + jj * P + P)
                            for half in range(2):
                                w = slice(jj * D + half * 512, jj * D + half * 512 + 512)
                                mm = three(bank(4 + half), ahi[:, a], alo[:, a], whi[:, sl, w], wlo[:, sl, w],
                                           False, last and jj == 1, True)
                        mm.then_inc(unit_used, 1)

                    pe.wait_ge(g_lo, 2 * (e + n0) + 2)
                    gate_up(0, 0)
                    scatter(e + n0)
                    gate_up(1, 2)
                    pe.wait_ge(scat_done, 4 * (e + n0) + 4)
                    turn(0)
                    zero_bank(4)
                    zero_bank(5)
                    with pe.Fori(0, (NCE - 2) // 2) as it:
                        for st in range(2):
                            gate_up(st, 4 + 3 * st, it)
                            turn(st + 1, it)
                            down(st, 6 + 3 * st, it)
                    pe.wait_ge(selg_ready, T * j + T)
                    for t in range(T):
                        mm = pe.transpose(ps[:, 0, t * P:t * P + P], selg[:, t, :], ident)
                    mm.then_inc(selt_ps, 1)
                    gather(e + n0 + 1)
                    turn(NCE - 1)
                    down(NCE - 2, 40)
                    down(NCE - 1, 41, last=True)
                    pe.wait_ge(selt_ready, j + 1)
                scatter(n0 + NE)

            pe.wait_ge(route_ready, 1)
            experts(0)
            over = pe.value_load(flag[0:1, 0:1], min_val=0, max_val=1)
            with pe.If(over > 0):
                experts(1)


def kernel(x, c, w_mod, b_mod, norm_g, pool_w, pool_scale, w_qkv, w_o, subln_g, lambda_vecs, rel_bias,
           ffn_w_gu, ffn_w_down, w_router, moe_w_gu, moe_w_down):
    import concourse.bacc as bacc
    from concourse.bass_utils import run_bass_kernel_spmd

    consts, pool_m, onehot = shape_constants()
    arrays = dict(x=x, c=c, w_mod=w_mod, b_mod=b_mod, norm_g=norm_g, pool_w=pool_w, pool_scale=pool_scale,
                  w_qkv=w_qkv, w_o=w_o, subln_g=subln_g, lambda_vecs=lambda_vecs, rel_bias=rel_bias,
                  ffn_w_gu=ffn_w_gu, ffn_w_down=ffn_w_down, w_router=w_router, moe_w_gu=moe_w_gu,
                  moe_w_down=moe_w_down, consts_in=consts, pool_in=pool_m, onehot_in=onehot)
    arrays = {name: np.ascontiguousarray(a) for name, a in arrays.items()}
    nc = bacc.Bacc("TRN2", target_bir_lowering=False, num_devices=1,
                   dynamic_dma_scratch_size=8192)
    aps = {name: nc.dram_tensor(name, a.shape, F32, kind="ExternalInput").ap() for name, a in arrays.items()}
    out = nc.dram_tensor("out", (1, S, D), F32, kind="ExternalOutput").ap()
    build_trunk(nc, out=out, **aps)
    result = run_bass_kernel_spmd(nc, [arrays], core_ids=[0])
    return result.results[0]["out"]
```

```python
import math
from contextlib import ExitStack

import numpy as np
import concourse.bass as bass
from concourse import mybir
from concourse.alu_op_type import AluOpType as ALU

ACT = mybir.ActivationFunctionType
AX_X = mybir.AxisListType.X
F32 = mybir.dt.float32
F32R = mybir.dt.float32r
BF16 = mybir.dt.bfloat16
I32 = mybir.dt.int32
U32 = mybir.dt.uint32

P = 128
D = 1024
S = 256
T = S // P
KC = D // P
EPS = 1e-6
N_MOD = 6
WINDOWS = (2, 4, 8, 16)
NH = 8
HD = 64
N_BUCKETS = 32
MAX_DISTANCE = 128
FF = 2816
NE = 8
FE = 3584
LAMBDA_INIT = 0.8 - 0.6 * math.exp(-0.3 * 1)
NEG = -3.0e38

RAW = 6
SPL = 3
UNIT = 2048
FC = 256
NCF = FF // FC
NCE = FE // FC

MOD_UNITS = N_MOD * KC // 2
R_FFN, Q_FFN = MOD_UNITS, 0
MOD_STEPS = MOD_UNITS // 3
R_QKV, Q_QKV = R_FFN + 3 * NCF + MOD_UNITS, Q_FFN + 3 * NCF
R_WO, Q_WO = R_QKV + 12, Q_QKV + 12
R_MOE, Q_MOE = R_WO + 4, Q_WO + 4
EXPERT_UNITS = 3 * NCE
assert EXPERT_UNITS % RAW == 0 and EXPERT_UNITS % SPL == 0 and MOD_UNITS % RAW == 0

ROW = [[0, 1, 2, 3, 4, 5], [6, 0, 1, 2, 3, 4]]
ROW_ORDER = [[1, 0, 2, 4, 3, 5], [1, 0, 2, 3, 4, 5]]
ROW_BANK = [[4, 6, 6, 0, 2, 6], [0, 2, 0, 2, 0, 2]]
ROW_GAIN = {1: 0, 2: 1, 4: 2, 5: 3}


def row_rank(l, g):
    return 6 * l + ROW_ORDER[l].index(g) + 1


def shape_constants():
    consts = np.zeros((P, 5, P), np.float32)
    consts[:, 0] = np.eye(P)
    consts[:, 1] = 1.0
    consts[:, 2] = np.triu(np.ones((P, P)), 1)
    consts[:, 3] = np.arange(P)[None, :]
    consts[:, 4] = np.eye(P)[::-1]
    pool = np.zeros((P, len(WINDOWS), S + P), np.float32)
    for g, w in enumerate(WINDOWS):
        full = np.zeros((S, S), np.float64)
        for s in range(S):
            lo = max(0, s - w + 1)
            full[lo:s + 1, s] = 1.0 / min(s + 1, w)
            full[s, s] -= 1.0
        pool[:, g, 0:S] = full[0:P]
        pool[:, g, S:] = full[P:, P:]
    n = S - 1 - np.arange(S)
    exact = N_BUCKETS // 2
    nf = np.maximum(n, 1).astype(np.float32)
    large = exact + (np.log(nf / np.float32(exact)) / np.float32(math.log(MAX_DISTANCE / exact))
                     * np.float32(N_BUCKETS - exact)).astype(np.int32)
    bucket = np.where(n < exact, n, np.minimum(large, N_BUCKETS - 1))
    onehot = np.zeros((N_BUCKETS, S), np.float32)
    onehot[bucket, np.arange(S)] = 1.0
    return consts.reshape(P, 5 * P), pool.reshape(P, -1), onehot


def build_trunk(nc, x, c, w_mod, b_mod, norm_g, pool_w, pool_scale, w_qkv, w_o, subln_g, lambda_vecs,
                rel_bias, ffn_w_gu, ffn_w_down, w_router, moe_w_gu, moe_w_down,
                consts_in, pool_in, onehot_in, out):
    bias_dram = nc.dram_tensor("bias_by_distance", (NH, S + P), F32, kind="Internal").ap()

    with ExitStack() as ctx:
        def sb(name, shape, dt=F32):
            return ctx.enter_context(nc.sbuf_tensor(name, shape, dt))

        def sem(name):
            return ctx.enter_context(nc.semaphore(name))

        raw = sb("raw", [P, RAW, UNIT])
        whi = sb("whi", [P, SPL, UNIT], F32R)
        wlo = sb("wlo", [P, SPL, UNIT], F32R)
        rows = sb("rows", [P, 7, D])
        xs = sb("xs", [P, T, D])
        hs = sb("hs", [P, T, D])
        thi = sb("thi", [P, UNIT], F32R)
        tlo = sb("tlo", [P, UNIT], F32R)
        ahi = sb("ahi", [P, 512], F32R)
        alo = sb("alo", [P, 512], F32R)
        gain = sb("gain", [P, 2, D])
        scr = sb("scr", [P, 6 * D])
        ysb = sb("ysb", [P, T, D])
        tmp = sb("tmp", [P, 2304])
        consts = sb("consts", [P, 5, P])
        subln = sb("subln", [P, P])
        zeros = sb("zeros", [P, P], BF16)
        wr = sb("wr", [P, KC, NE])
        silu_c = sb("silu_c", [P, KC])
        ss = sb("ss", [P, 16])
        rstd = sb("rstd", [P, 16])
        minus_half = sb("minus_half", [P, 8])
        lam = sb("lam", [P, 4])
        stat = sb("stat", [P, 4, 3, 4])
        oss = sb("oss", [P, NH, T])
        posm = sb("posm", [P, T, NE + 1])
        gates = sb("gates", [P, T, NE])
        flag = sb("flag", [P, 1], I32)

        ident, ones, before, slots, reverse = (consts[:, i, :] for i in range(5))
        thi3 = thi[:, :].rearrange("p (k s) -> p k s", k=KC)
        tlo3 = tlo[:, :].rearrange("p (k s) -> p k s", k=KC)
        ghi = thi[:, 0:D].rearrange("p (k s) -> p k s", k=KC)
        glo = tlo[:, 0:D].rearrange("p (k s) -> p k s", k=KC)
        pool_m = scr[:, 0:4 * 384].rearrange("p (g s) -> p g s", g=4)
        poolw = scr[:, 1536:3584].rearrange("p (g c e) -> p g c e", g=4, c=2)
        onehot = scr[0:N_BUCKETS, 3584:3840]
        relb = scr[0:N_BUCKETS, 3840:3848]
        bias_row = scr[0:NH, 3848:3848 + S + P]
        lamv = scr[:, 4352:4608].rearrange("p (v d) -> p v d", v=4)
        lamj = scr[:, 4608:4672]
        bias_rev = scr[:, 4096:6144].rearrange("p (h k) -> p h k", h=NH)
        qk_t = scr[:, 0:4096].rearrange("p (m s) -> p m s", m=2 * NH)
        vs = scr[:, 4096:6144].rearrange("p (t e) -> p t e", t=T)
        ht32 = scr[:, 0:2048].rearrange("p (k s) -> p k s", k=KC)
        moe_out = scr[:, 2048:4096].rearrange("p (t d) -> p t d", t=T)
        y_e = scr[:, 4096:5120]
        pooled_t = ysb[:, :, :].rearrange("p t (k s) -> p (t k) s", s=S)
        bias_t = ysb[:, :, :].rearrange("p t (k s) -> p (t k) s", s=S)
        att_s = [tmp[:, 768 * b:768 * b + 768].rearrange("p (c k) -> p c k", c=2) for b in range(3)]
        att_at = [gain[:, 0, 384 * b:384 * b + 384] for b in range(2)]
        junk = gain[:, 0, 768:1024].rearrange("p (t e) -> p t e", t=T)
        sg = tmp[:, 0:512]
        actf = tmp[:, 512:1024]
        sel = tmp[:, 1024:1280].rearrange("p (t s) -> p t s", t=T)
        selg = tmp[:, 1280:1536].rearrange("p (t s) -> p t s", t=T)
        selg_t = tmp[:, 1536:1792]
        rt = tmp[:, 1792:2304]
        logits = rt[:, 0:16].rearrange("p (t e) -> p t e", t=T)
        top = rt[:, 16:32].rearrange("p (t e) -> p t e", t=T)
        idx_f = rt[:, 48:64].rearrange("p (t e) -> p t e", t=T)
        oh = [rt[:, 64 + 16 * i:80 + 16 * i].rearrange("p (t e) -> p t e", t=T) for i in range(2)]
        mask = rt[:, 96:112].rearrange("p (t e) -> p t e", t=T)
        w2 = rt[:, 112:120]
        cnt = rt[:, 120:124]
        diff = rt[:, 124:126]

        top_idx = sb("top_idx", [P, T, 8], U32)

        ps = ctx.enter_context(nc.psum_tensor("ps", [P, 8, 512], F32))

        def bank(b, n=512):
            return ps[:, b, 0:n]

        raw_loaded = [sem(f"raw_loaded{i}") for i in range(RAW)]
        hi_ready = sem("hi_ready")
        unit_done = sem("unit_done")
        unit_used = sem("unit_used")
        x_loaded = sem("x_loaded")
        c_loaded = sem("c_loaded")
        consts_loaded = sem("consts_loaded")
        pool_loaded = sem("pool_loaded")
        small_loaded = sem("small_loaded")
        lam_loaded = sem("lam_loaded")
        wr_loaded = sem("wr_loaded")
        scale_loaded = sem("scale_loaded")
        gain_loaded = [sem(f"gain_loaded{i}") for i in range(2)]
        bmod_loaded = [sem(f"bmod_loaded{i}") for i in range(4)]
        mixer_rows_zeroed = sem("mixer_rows_zeroed")
        rows_zeroed = sem("rows_zeroed")
        zeros_ready = sem("zeros_ready")
        silu_ready = sem("silu_ready")
        gemv = sem("gemv")
        row_ps = sem("row_ps")
        row_done = sem("row_done")
        ss_ready = sem("ss_ready")
        half_ready = sem("half_ready")
        ms_ready = sem("ms_ready")
        rstd_ready = sem("rstd_ready")
        oms_ready = sem("oms_ready")
        omse_ready = sem("omse_ready")
        orstd_ready = sem("orstd_ready")
        h_ready = sem("h_ready")
        ht_ps = sem("ht_ps")
        ht_hi = sem("ht_hi")
        ht_lo = sem("ht_lo")
        ht32_ready = sem("ht32_ready")
        x_done = sem("x_done")
        link_s = sem("vector_link")
        dist_ps = sem("dist_ps")
        dist_ready = sem("dist_ready")
        dist_stored = sem("dist_stored")
        bias_loaded = sem("bias_loaded")
        bias_ps = sem("bias_ps")
        bias_ready = sem("bias_ready")
        lam_prod = sem("lam_prod")
        lam_exp = sem("lam_exp")
        pooled_ps = sem("pooled_ps")
        pooled_ready = sem("pooled_ready")
        mix_ps = sem("mix_ps")
        y_scaled = sem("y_scaled")
        f_sg = sem("f_sg")
        f_act = sem("f_act")
        f_ahi = sem("f_ahi")
        f_alo = sem("f_alo")
        qkv_ready = sem("qkv_ready")
        sc_ps = sem("sc_ps")
        sc_max = sem("sc_max")
        sc_exp = sem("sc_exp")
        att_ready = sem("att_ready")
        at_ps = sem("at_ps")
        at_ready = sem("at_ready")
        o_ps = sem("o_ps")
        o_ready = sem("o_ready")
        on_ready = sem("on_ready")
        ot_ps = sem("ot_ps")
        ot_hi = sem("ot_hi")
        ot_lo = sem("ot_lo")
        lg_ps = sem("lg_ps")
        top_ready = sem("top_ready")
        e2_ready = sem("e2_ready")
        mask_ready = sem("mask_ready")
        pos_ps = sem("pos_ps")
        route_ready = sem("route_ready")
        over_ready = sem("over_ready")
        sel_ready = sem("sel_ready")
        selg_ready = sem("selg_ready")
        selt_cleared = sem("selt_cleared")
        moe_cleared = sem("moe_cleared")
        selt_ps = sem("selt_ps")
        selt_ready = sem("selt_ready")
        g_ps = sem("g_ps")
        g_hi = sem("g_hi")
        g_lo = sem("g_lo")
        e_sg = sem("e_sg")
        e_act = sem("e_act")
        e_at = sem("e_at")
        e_ahi = sem("e_ahi")
        e_alo = sem("e_alo")
        y_ready = sem("y_ready")
        scat_ps = sem("scat_ps")
        scat_done = sem("scat_done")
        stored = sem("stored")

        block = ctx.enter_context(nc.Block())

        @block.sync
        def _(sp):
            def load(r, rounds, halves):
                if r >= RAW:
                    sp.wait_ge(unit_done, r - RAW + 1 + rounds * RAW)
                dst = raw[:, r % RAW, :]
                for view, src in halves(dst):
                    sp.dma_start(view, src).then_inc(raw_loaded[r % RAW], 16)

            def mod_unit(l, pair, g):
                def halves(dst):
                    for kk in range(2):
                        yield (dst[:, kk * D:(kk + 1) * D],
                               w_mod[l].rearrange("(p k) f -> p k f", k=KC)[:, pair * 2 + kk, g * D:(g + 1) * D])
                return halves

            def gu_unit(w, width, chunk, kh):
                def halves(dst):
                    v = dst.rearrange("p (k g j) -> p k g j", k=4, g=2)
                    src = w.rearrange("(k p) f -> p k f", p=P)
                    for g in range(2):
                        yield v[:, :, g, :], src[:, kh * 4:kh * 4 + 4, bass.ds(chunk * FC + g * width, FC)]
                return halves

            def down_unit(w, chunk):
                def halves(dst):
                    for j in range(2):
                        yield dst[:, j * D:(j + 1) * D], w[bass.ds((chunk * 2 + j) * P, P), :]
                return halves

            def col_unit(w, col, kh):
                def halves(dst):
                    v = dst.rearrange("p (k j) -> p k j", k=4)
                    src = w.rearrange("(k p) f -> p k f", p=P)
                    for i in range(2):
                        yield v[:, 2 * i:2 * i + 2, :], src[:, kh * 4 + 2 * i:kh * 4 + 2 * i + 2, col:col + 512]
                return halves

            sp.dma_start(silu_c[:, :], c.rearrange("a (p k) -> (a p) k", k=KC)).then_inc(c_loaded, 16)
            for half in range(2):
                for it in range(2):
                    for u in range(6):
                        load(half * 12 + it * 6 + u, 0, mod_unit(0, it * 2 + u // 3, half * 3 + u % 3))
                    if half == 0 and it == 1:
                        sp.dma_start(xs[:, :, :], x[0].rearrange("(t p) d -> p t d", p=P)).then_inc(x_loaded, 16)
            w_gu, w_dn = ffn_w_gu[0], ffn_w_down[0]
            load(R_FFN, 0, gu_unit(w_gu, FF, 0, 0))
            load(R_FFN + 1, 0, gu_unit(w_gu, FF, 0, 1))
            with sp.Fori(0, MOD_STEPS // 2) as it:
                for st in range(2):
                    r = R_FFN + 2 + 6 * st
                    load(r, it * 2, gu_unit(w_gu, FF, it * 2 + st + 1, 0))
                    load(r + 1, it * 2, gu_unit(w_gu, FF, it * 2 + st + 1, 1))
                    for g in range(3):
                        load(r + 2 + g, it * 2, mod_unit(1, it, st * 3 + g))
                    load(r + 5, it * 2, down_unit(w_dn, it * 2 + st))
            r = R_FFN + 2 + 6 * MOD_STEPS
            for s in range(MOD_STEPS, NCF - 1):
                load(r, 0, gu_unit(w_gu, FF, s + 1, 0))
                load(r + 1, 0, gu_unit(w_gu, FF, s + 1, 1))
                load(r + 2, 0, down_unit(w_dn, s))
                r += 3
            load(r, 0, down_unit(w_dn, NCF - 1))
            for g in range(6):
                for kh in range(2):
                    load(R_QKV + 2 * g + kh, 0, col_unit(w_qkv[0], g * 512, kh))
            for g in range(2):
                for kh in range(2):
                    load(R_WO + 2 * g + kh, 0, col_unit(w_o[0], g * 512, kh))

            def experts(ps_no):
                base = R_MOE + ps_no * NE * EXPERT_UNITS
                with sp.Fori(0, NE) as e:
                    gu, dn, eo = moe_w_gu[0, e], moe_w_down[0, e], e * (EXPERT_UNITS // RAW)
                    for s in range(2):
                        load(base + 2 * s, eo, gu_unit(gu, FE, s, 0))
                        load(base + 2 * s + 1, eo, gu_unit(gu, FE, s, 1))
                    with sp.Fori(0, (NCE - 2) // 2) as it:
                        for st in range(2):
                            r, ro = base + 4 + 3 * st, eo + it
                            load(r, ro, gu_unit(gu, FE, it * 2 + st + 2, 0))
                            load(r + 1, ro, gu_unit(gu, FE, it * 2 + st + 2, 1))
                            load(r + 2, ro, down_unit(dn, it * 2 + st))
                    load(base + 40, eo, down_unit(dn, NCE - 2))
                    load(base + 41, eo, down_unit(dn, NCE - 1))

            experts(0)
            sp.wait_ge(route_ready, 1)
            over = sp.value_load(flag[0:1, 0:1], min_val=0, max_val=1)
            with sp.If(over > 0):
                experts(1)
            for t in range(T):
                sp.wait_ge(x_done, 3 * T + t + 1)
                sp.dma_start(out[0].rearrange("(t p) d -> p t d", p=P)[:, t, :], xs[:, t, :]).then_inc(stored, 16)
            sp.wait_ge(stored, 16 * T)

        @block.gpsimd
        def _(pool):
            pool.dma_start(relb, rel_bias).then_inc(small_loaded, 16)
            pool.dma_start(onehot, onehot_in).then_inc(small_loaded, 16)
            pool.wait_ge(mixer_rows_zeroed, 1)
            pool.dma_start(rows[0:1, 0:3, :], b_mod[0:1, 0:3 * D].rearrange("a (g d) -> a g d", d=D)).then_inc(bmod_loaded[0], 16)
            pool.memset(bias_row[:, S:S + P], NEG).then_inc(dist_ready, 1)
            pool.dma_start(consts[:, :, :], consts_in.rearrange("p (i s) -> p i s", i=5)).then_inc(consts_loaded, 16)
            pool.memset(rows[:, 3:6, :], 0.0).then_inc(rows_zeroed, 1)
            pool.memset(zeros[:, :], 0.0).then_inc(zeros_ready, 1)
            pool.memset(minus_half[:, :], -0.5).then_inc(half_ready, 1)

            def load_gain(i):
                pool.dma_start(gain[:, i % 2, :], norm_g[i // 4, i % 4, :].partition_broadcast(P)).then_inc(gain_loaded[i % 2], 16)

            def next_gain(i):
                l, j = divmod(i - 2, 4)
                pool.wait_ge(row_done, row_rank(l, (1, 2, 4, 5)[j]))
                load_gain(i)

            pool.wait_ge(unit_done, 3)
            load_gain(0)
            pool.wait_ge(unit_done, 6)
            pool.wait_ge(rows_zeroed, 1)
            pool.dma_start(rows[0:1, 3:6, :], b_mod[0:1, 3 * D:6 * D].rearrange("a (g d) -> a g d", d=D)).then_inc(bmod_loaded[1], 16)
            load_gain(1)
            pool.wait_ge(unit_done, 9)
            pool.dma_start(pool_m, pool_in.rearrange("p (g s) -> p g s", g=4)).then_inc(pool_loaded, 16)
            pool.dma_start(poolw, pool_w[0].rearrange("g (c p) e -> p g c e", p=P)).then_inc(pool_loaded, 16)
            pool.dma_start(rows[:, 6, :], pool_scale[0, :].partition_broadcast(P)).then_inc(scale_loaded, 16)
            pool.dma_start(lamv, lambda_vecs[0].partition_broadcast(P)).then_inc(lam_loaded, 16)
            pool.dma_start(subln[:, :], subln_g[0, :].partition_broadcast(P)).then_inc(lam_loaded, 16)
            pool.dma_start(wr[:, :, :], w_router[0].rearrange("(k p) e -> p k e", p=P)).then_inc(wr_loaded, 16)

            def inverse_roots(i, col):
                for t in range(T):
                    cc = 4 * i + col + t
                    pool.wait_ge(ms_ready, cc + 1)
                    pool.tensor_tensor(rstd[:, cc:cc + 1], ss[:, cc:cc + 1], minus_half[:, 0:1], ALU.pow).then_inc(rstd_ready, 1)

            pool.wait_ge(half_ready, 1)
            inverse_roots(0, 0)
            pool.wait_ge(dist_ready, 2)
            pool.dma_start(bias_dram, bias_row).then_inc(dist_stored, 16)
            pool.wait_ge(dist_stored, 16)
            next_gain(2)
            next_gain(3)
            pool.wait_ge(lam_prod, 2)
            pool.dma_start(bias_rev, bass.AP(tensor=bias_dram.tensor, offset=0,
                                             ap=[(1, P), (S + P, NH), (1, S)])).then_inc(bias_loaded, 16)
            inverse_roots(0, 2)
            pool.wait_ge(x_done, T)
            pool.memset(rows[:, 0:3, :], 0.0).then_inc(rows_zeroed, 1)
            pool.memset(rows[:, 6, :], 0.0).then_inc(rows_zeroed, 1)
            pool.wait_ge(rows_zeroed, 3)
            pool.dma_start(rows[0:1, 0:3, :], b_mod[1:2, D:4 * D].rearrange("a (g d) -> a g d", d=D)).then_inc(bmod_loaded[2], 16)
            pool.dma_start(rows[0:1, 6, :], b_mod[1:2, 0:D]).then_inc(bmod_loaded[2], 16)
            inverse_roots(1, 0)
            pool.wait_ge(h_ready, 2 * T)
            pool.memset(rows[:, 3:5, :], 0.0).then_inc(rows_zeroed, 1)
            pool.wait_ge(rows_zeroed, 4)
            pool.dma_start(rows[0:1, 3:5, :], b_mod[1:2, 4 * D:6 * D].rearrange("a (g d) -> a g d", d=D)).then_inc(bmod_loaded[3], 16)
            next_gain(4)
            next_gain(5)
            inverse_roots(1, 2)
            inverse_roots(2, 0)

            for half in range(2):
                pool.wait_ge(omse_ready, half + 1)
                o4 = oss[:, half * 4:half * 4 + 4, :].rearrange("p h t -> p (h t)")
                pool.tensor_tensor(o4, o4, minus_half[:, :], ALU.pow).then_inc(orstd_ready, 1)
            pool.wait_ge(o_ps, NH)
            next_gain(6)
            next_gain(7)
            pool.memset(moe_out, 0.0).then_inc(moe_cleared, 1)
            pool.memset(selg_t, 0.0).then_inc(selt_cleared, 1)
            inverse_roots(2, 2)
            inverse_roots(3, 0)
            pool.wait_ge(route_ready, 1)
            over = pool.value_load(flag[0:1, 0:1], min_val=0, max_val=1)
            with pool.If(over > 0):
                pool.wait_ge(over_ready, 1)
                pool.memset(selg_t, 0.0).then_inc(selt_cleared, 1)
            inverse_roots(3, 2)

        @block.scalar
        def _(act):
            def high(r, q, rounds=0, qo=0):
                act.wait_ge(raw_loaded[r % RAW], 32 * (r // RAW + 1) + 32 * rounds)
                if q >= SPL - 1:
                    act.wait_ge(unit_used, max(q - SPL + 1, 1) + qo)
                act.activation(whi[:, q % SPL, :], raw[:, r % RAW, :], ACT.Copy).then_inc(hi_ready, 1)

            def square_x(i):
                for t in range(T):
                    if i == 0:
                        act.wait_ge(x_loaded, 16)
                    else:
                        act.wait_ge(x_done, T * (i - 1) + t + 1)
                    act.activation(hs[:, t, :], xs[:, t, :], ACT.Square, scale=D ** -0.5,
                                   accum_out=ss[:, 4 * i + t:4 * i + t + 1]).then_inc(ss_ready, 1)

            def high_transposed(i):
                for b in range(4):
                    act.wait_ge(ht_ps, 4 * (i - 1) + b + 1)
                    act.activation(thi[:, 512 * b:512 * b + 512], bank(b), ACT.Copy).then_inc(ht_hi, 1)

            def square_y_psum(i, q_end):
                act.wait_ge(unit_used, q_end)
                for t in range(T):
                    act.activation(ysb[:, t, :].rearrange("p (h d) -> p h d", h=2), ps[:, 4 + 2 * t:6 + 2 * t, :],
                                   ACT.Square, scale=D ** -0.5, accum_out=ss[:, 4 * i + 2 + t:4 * i + 3 + t]).then_inc(ss_ready, 1)

            act.wait_ge(c_loaded, 16)
            act.activation(silu_c[:, :], silu_c[:, :], ACT.Silu).then_inc(silu_ready, 1)
            act.wait_ge(dist_ps, 1)
            act.activation(bias_row[:, 0:S], ps[0:NH, 5, 0:S], ACT.Copy, scale=HD ** 0.5).then_inc(dist_ready, 1)

            square_x(0)
            for b in range(4):
                act.wait_ge(pooled_ps, b + 1)
                act.copy(pooled_t[:, 2 * b:2 * b + 2, :], bank(b).rearrange("p (k s) -> p k s", k=2)).then_inc(pooled_ready, 1)
            act.wait_ge(lam_prod, 2)
            act.activation(lam[:, 2:4], lam[:, 0:2], ACT.Exp).then_inc(lam_exp, 1)
            for t in range(T):
                act.wait_ge(y_scaled, t + 1)
                act.activation(hs[:, t, :], ysb[:, t, :], ACT.Square, scale=D ** -0.5, accum_out=ss[:, 2 + t:3 + t]).then_inc(ss_ready, 1)

            high(R_FFN, 0)
            high(R_FFN + 1, 1)
            square_x(1)
            high_transposed(1)

            def ffn_act(s, it=0):
                act.wait_ge(unit_used, 3 * s + 2 + it * 6)
                b = 2 * (s % 2)
                act.activation(sg.rearrange("p (j s) -> p j s", j=2), ps[:, b:b + 2, 0:FC], ACT.Silu).then_inc(f_sg, 1)
                act.wait_ge(f_act, s + 1 + it * 2)
                act.activation(ahi[:, :], actf, ACT.Copy).then_inc(f_ahi, 1)

            def ffn_step(s, r, mod, it=0):
                q = 2 + 3 * s
                high(r, q, it * 2, it * 6)
                high(r + 1, q + 1, it * 2, it * 6)
                ffn_act(s, it)
                high(r + (5 if mod else 2), q + 2, it * 2, it * 6)

            with act.Fori(0, MOD_STEPS // 2) as it:
                for st in range(2):
                    ffn_step(st, R_FFN + 2 + 6 * st, True, it)
            for s in range(MOD_STEPS, NCF - 1):
                ffn_step(s, R_FFN + 2 + 3 * MOD_STEPS + 3 * s, False)
            high(R_QKV - 1, Q_QKV - 1)
            ffn_act(NCF - 1)
            high(R_QKV, Q_QKV)
            high(R_QKV + 1, Q_QKV + 1)
            square_y_psum(1, Q_QKV)

            square_x(2)
            for b in range(4):
                act.wait_ge(bias_ps, b + 1)
                act.copy(bias_t[:, 2 * b:2 * b + 2, :], bank(4 + b).rearrange("p (h k) -> p h k", h=2)).then_inc(bias_ready, 1)
            high_transposed(2)

            def qkv_out(g):
                act.wait_ge(unit_used, Q_QKV + 2 * g + 2)
                src = ps[:, 4 + 2 * (g % 2):6 + 2 * (g % 2), :]
                if g < 4:
                    dst = qk_t[:, 4 * g:4 * g + 4, :].rearrange("p (b m) s -> p b (m s)", b=2)
                else:
                    dst = vs[:, :, (g - 4) * 512:(g - 3) * 512]
                act.copy(dst, src).then_inc(qkv_ready, 1)

            for g in range(1, 6):
                high(R_QKV + 2 * g, Q_QKV + 2 * g)
                high(R_QKV + 2 * g + 1, Q_QKV + 2 * g + 1)
                qkv_out(g - 1)

            def exps(h):
                act.wait_ge(sc_max, h + 1)
                a, st = att_s[h % 3], stat[:, h % 4]
                for cc in range(2):
                    for t in range(T):
                        k0, k1 = (0, P) if t == 0 else (P, P + S)
                        act.activation(a[:, cc, k0:k1], a[:, cc, k0:k1], ACT.Exp, scale=HD ** -0.5,
                                       bias=st[:, 0, 2 * cc + t:2 * cc + t + 1],
                                       accum_out=st[:, 1, 2 * cc + t:2 * cc + t + 1]).then_inc(sc_exp, 1)

            def at_copy(h):
                act.wait_ge(at_ps, h + 1)
                act.copy(att_at[h % 2], bank(4 + h % 2, 384)).then_inc(at_ready, 1)

            def o_copy(h):
                act.wait_ge(o_ps, h + 1)
                for t in range(T):
                    act.activation(hs[:, t, h * P:h * P + P], ps[:, 6 + h % 2, t * P:t * P + P], ACT.Copy,
                                   scale=stat[:, h % 4, 2, t:t + 1]).then_inc(o_ready, 1)

            exps(0)
            qkv_out(5)
            for h in range(NH):
                if h > 0:
                    at_copy(h - 1)
                if h + 1 < NH:
                    exps(h + 1)
                if h > 1:
                    o_copy(h - 2)
            high(R_WO, Q_WO)
            at_copy(NH - 1)
            o_copy(NH - 2)
            o_copy(NH - 1)
            high(R_WO + 1, Q_WO + 1)
            for b in range(4):
                act.wait_ge(ot_ps, b + 1)
                act.activation(thi[:, 512 * b:512 * b + 512], bank(b), ACT.Copy).then_inc(ot_hi, 1)
            high(R_WO + 2, Q_WO + 2)
            high(R_WO + 3, Q_WO + 3)
            square_y_psum(2, Q_MOE)

            square_x(3)
            for b in range(4):
                act.wait_ge(ht_ps, 4 * 2 + b + 1)
                act.copy(ht32[:, 2 * b:2 * b + 2, :], bank(b).rearrange("p (k s) -> p k s", k=2)).then_inc(ht32_ready, 1)
            act.wait_ge(top_ready, 1)
            act.activation(w2[:, 0:2], diff, ACT.Exp).then_inc(e2_ready, 1)

            def experts(ps_no):
                r0, q0, j0 = (R_MOE + ps_no * NE * EXPERT_UNITS, Q_MOE + ps_no * NE * EXPERT_UNITS, ps_no * NE)
                n0 = ps_no * (NE + 1)

                def gathered_high(n):
                    for b in range(2):
                        act.wait_ge(g_ps, 2 * n + b + 1)
                        act.activation(thi[:, 512 * b:512 * b + 512], bank(6 + b), ACT.Copy).then_inc(g_hi, 1)

                def expert_out(used):
                    act.wait_ge(unit_used, used)
                    for b in range(2):
                        act.copy(y_e[:, 512 * b:512 * b + 512], bank(4 + b)).then_inc(y_ready, 1)

                gathered_high(n0)
                with act.Fori(0, NE) as e:
                    j, ro, qo = e + j0, e * (EXPERT_UNITS // RAW), e * EXPERT_UNITS

                    def silu_gate(s, used, it=0):
                        act.wait_ge(unit_used, q0 + used + qo + it * 6)
                        act.activation(sg[:, 0:FC], bank(s % 2)[:, 0:FC], ACT.Silu).then_inc(e_sg, 1)

                    def act_high(s, so=0):
                        act.wait_ge(e_at, j * NCE + s + 1 + so)
                        act.activation(ahi[:, (s % 2) * FC:(s % 2) * FC + FC], bank(2 + s % 2, FC), ACT.Copy).then_inc(e_ahi, 1)

                    for u in range(3):
                        high(r0 + u, q0 + u, ro, qo)
                    expert_out(q0 + qo)
                    silu_gate(0, 2)
                    high(r0 + 3, q0 + 3, ro, qo)
                    with act.Fori(0, (NCE - 2) // 2) as it:
                        for st in range(2):
                            u = 4 + 3 * st
                            high(r0 + u, q0 + u, ro + it, qo + it * 6)
                            high(r0 + u + 1, q0 + u + 1, ro + it, qo + it * 6)
                            act_high(st, it * 2)
                            silu_gate(st + 1, 4 + 2 * st, it)
                            high(r0 + u + 2, q0 + u + 2, ro + it, qo + it * 6)
                    act_high(NCE - 2)
                    silu_gate(NCE - 1, EXPERT_UNITS - 3)
                    high(r0 + 40, q0 + 40, ro, qo)
                    act.wait_ge(selt_ps, j + 1)
                    act.copy(selg_t, bank(0, S)).then_inc(selt_ready, 1)
                    gathered_high(e + n0 + 1)
                    act_high(NCE - 1)
                    high(r0 + 41, q0 + 41, ro, qo)
                expert_out(q0 + NE * EXPERT_UNITS)

            experts(0)
            act.wait_ge(route_ready, 1)
            over = act.value_load(flag[0:1, 0:1], min_val=0, max_val=1)
            with act.If(over > 0):
                experts(1)

        @block.vector
        def _(dve):
            links = [0]

            def link(ins):
                links[0] += 1
                ins.then_inc(link_s, 1)
                dve.wait_ge(link_s, links[0])

            def low(r, q, rounds=0, qo=0):
                dve.wait_ge(hi_ready, q + 1 + qo)
                dve.tensor_tensor(wlo[:, q % SPL, :], raw[:, r % RAW, :], whi[:, q % SPL, :].bitcast(F32),
                                  ALU.subtract).then_inc(unit_done, 1)

            def low_from(dst, src, hi_part, sem_out):
                dve.tensor_tensor(dst, src, hi_part.bitcast(F32), ALU.subtract).then_inc(sem_out, 1)

            def gemv_step(r, row_slots, cols, n, prev, rounds=0, no=0, ro=0):
                for kk in range(2):
                    for u in range(3):
                        if kk == 0:
                            dve.wait_ge(raw_loaded[(r + u) % RAW], 32 * ((r + u) // RAW + 1) + 32 * rounds)
                            if prev is not None:
                                dve.wait_ge(unit_done, prev + u + 1 + ro)
                        else:
                            dve.wait_ge(gemv, 3 * n + u + 1 + no)
                        row = rows[:, row_slots[u], :]
                        dve.scalar_tensor_tensor(row, raw[:, (r + u) % RAW, kk * D:kk * D + D], cols[kk], row,
                                                 ALU.mult, ALU.add).then_inc(unit_done if kk else gemv, 1)

            def finish_rows(l, groups):
                for g in groups:
                    dve.wait_ge(row_ps, row_rank(l, g))
                    b = ROW_BANK[l][g]
                    src = ps[:, b:b + 2, :]
                    row = rows[:, ROW[l][g], :].rearrange("p (h d) -> p h d", h=2)
                    if g % 3:
                        i = 4 * l + ROW_GAIN[g]
                        gv = gain[:, i % 2, :].rearrange("p (h d) -> p h d", h=2)
                        dve.wait_ge(gain_loaded[i % 2], 16 * (i // 2 + 1))
                    if g % 3 == 0:
                        dve.tensor_copy(row, src).then_inc(row_done, 1)
                    elif g % 3 == 1:
                        dve.scalar_tensor_tensor(row, src, 1.0, gv, ALU.add, ALU.mult).then_inc(row_done, 1)
                    else:
                        dve.tensor_tensor(row, src, gv, ALU.mult).then_inc(row_done, 1)

            def inverse_root(i, col):
                cc = 4 * i + col
                dve.wait_ge(rstd_ready, cc + 1)
                return rstd[:, cc:cc + 1]

            def add_eps(i, col):
                for t in range(T):
                    cc = 4 * i + col + t
                    dve.wait_ge(ss_ready, cc + 1)
                    dve.tensor_scalar(ss[:, cc:cc + 1], ss[:, cc:cc + 1], EPS, None, ALU.add).then_inc(ms_ready, 1)

            def modulated(i):
                l, g = divmod(i, 2)
                if i:
                    add_eps(i, 0)
                dve.wait_ge(row_done, max(row_rank(l, 3 * g), row_rank(l, 3 * g + 1)))
                for t in range(T):
                    rs = inverse_root(i, t)
                    link(dve.scalar_tensor_tensor(hs[:, t, :], xs[:, t, :], rs, rows[:, ROW[l][3 * g + 1], :], ALU.mult, ALU.mult))
                    dve.tensor_tensor(hs[:, t, :], hs[:, t, :], rows[:, ROW[l][3 * g], :], ALU.add).then_inc(h_ready, 1)

            def residual(i, y_of):
                l, g = divmod(i, 2)
                add_eps(i, 2)
                dve.wait_ge(row_done, row_rank(l, 3 * g + 2))
                for t in range(T):
                    rs = inverse_root(i, 2 + t)
                    y = y_of(t)
                    dst, gv = ysb[:, t, :], rows[:, ROW[l][3 * g + 2], :]
                    if len(y.shape) == 3:
                        dst, gv = (v.rearrange("p (h d) -> p h d", h=2) for v in (dst, gv))
                    link(dve.scalar_tensor_tensor(dst, y, rs, gv, ALU.mult, ALU.mult))
                    dve.tensor_tensor(xs[:, t, :], xs[:, t, :], ysb[:, t, :], ALU.add).then_inc(x_done, 1)

            def low_transposed(i):
                for b in range(4):
                    dve.wait_ge(ht_hi, 4 * (i - 1) + b + 1)
                    low_from(tlo[:, 512 * b:512 * b + 512], bank(b), thi[:, 512 * b:512 * b + 512], ht_lo)

            dve.memset(rows[:, 0:3, :], 0.0).then_inc(mixer_rows_zeroed, 1)
            dve.wait_ge(silu_ready, 1)

            def mod0_step(n):
                m = n % 4
                gemv_step(3 * n, [n // 4 * 3 + u for u in range(3)], [silu_c[:, 2 * m + kk:2 * m + kk + 1] for kk in range(2)],
                          n, 3 * (n - 1) if m else None)

            dve.wait_ge(bmod_loaded[0], 16)
            for n in range(4):
                mod0_step(n)
            add_eps(0, 0)
            dve.wait_ge(bmod_loaded[1], 16)
            mod0_step(4)
            finish_rows(0, (1, 0))
            modulated(0)
            finish_rows(0, (2,))
            mod0_step(5)
            dve.wait_ge(lam_loaded, 32)
            for i in range(2):
                if i:
                    dve.wait_ge(lam_prod, 1)
                dve.tensor_tensor_reduce(lamj, lamv[:, 2 * i, :], lamv[:, 2 * i + 1, :], 1.0, 0.0,
                                         ALU.mult, ALU.add, lam[:, i:i + 1]).then_inc(lam_prod, 1)
            mod0_step(6)
            dve.wait_ge(scale_loaded, 16)
            dve.wait_ge(mix_ps, 1)
            for t in range(T):
                dve.tensor_tensor(ysb[:, t, :].rearrange("p (h d) -> p h d", h=2), ps[:, 4 + 2 * t:6 + 2 * t, :],
                                  rows[:, 6, :].rearrange("p (h d) -> p h d", h=2), ALU.mult).then_inc(y_scaled, 1)
            mod0_step(7)
            dve.wait_ge(y_scaled, T)
            residual(0, lambda t: ysb[:, t, :])
            finish_rows(0, (4, 3))

            low(R_FFN, 0)
            low(R_FFN + 1, 1)
            modulated(1)
            low_transposed(1)
            finish_rows(0, (5,))
            dve.wait_ge(lam_exp, 1)
            link(dve.tensor_tensor(lam[:, 0:1], lam[:, 3:4], lam[:, 2:3], ALU.subtract))
            link(dve.tensor_scalar(lam[:, 0:1], lam[:, 0:1], -LAMBDA_INIT, None, ALU.add))
            link(dve.tensor_scalar(subln[:, :], subln[:, :], 1.0 - LAMBDA_INIT, None, ALU.mult))
            dve.wait_ge(bmod_loaded[2], 32)
            dve.wait_ge(bmod_loaded[3], 16)

            def ffn_act(s, so=0):
                dve.wait_ge(f_sg, s + 1 + so)
                b = 2 * (s % 2)
                dve.tensor_tensor(actf.rearrange("p (j s) -> p j s", j=2), sg.rearrange("p (j s) -> p j s", j=2),
                                  ps[:, b:b + 2, FC:2 * FC], ALU.mult).then_inc(f_act, 1)
                dve.wait_ge(f_ahi, s + 1 + so)
                low_from(alo[:, :], actf, ahi[:, :], f_alo)

            with dve.Fori(0, MOD_STEPS // 2) as it:
                for st in range(2):
                    r, q = R_FFN + 2 + 6 * st, 2 + 3 * st
                    low(r, q, it * 2, it * 6)
                    low(r + 1, q + 1, it * 2, it * 6)
                    gemv_step(r + 2, [ROW[1][3 * st + u] for u in range(3)],
                              [silu_c[:, bass.ds(it * 2 + kk, 1)] for kk in range(2)],
                              MOD_STEPS + st, r + 2 - 2 * RAW, it * 2, it * 6, it * 12)
                    ffn_act(st, it * 2)
                    low(r + 5, q + 2, it * 2, it * 6)
            for s in range(MOD_STEPS, NCF - 1):
                r = R_FFN + 2 + 3 * MOD_STEPS + 3 * s
                low(r, 2 + 3 * s)
                low(r + 1, 3 + 3 * s)
                ffn_act(s)
                low(r + 2, 4 + 3 * s)
            low(R_QKV - 1, Q_QKV - 1)
            ffn_act(NCF - 1)
            finish_rows(1, (1,))
            low(R_QKV, Q_QKV)
            low(R_QKV + 1, Q_QKV + 1)
            finish_rows(1, (0,))
            residual(1, lambda t: ps[:, 4 + 2 * t:6 + 2 * t, :])

            modulated(2)
            low_transposed(2)
            for g in range(1, 6):
                low(R_QKV + 2 * g, Q_QKV + 2 * g)
                low(R_QKV + 2 * g + 1, Q_QKV + 2 * g + 1)
            dve.wait_ge(bias_ready, 4)

            def row_max(h):
                dve.wait_ge(sc_ps, h + 1)
                if h >= 3:
                    dve.wait_ge(at_ps, h - 2)
                a, st = att_s[h % 3], stat[:, h % 4]
                for cc in range(2):
                    for t in range(T):
                        k0, k1 = (0, P) if t == 0 else (P, P + S)
                        ins = dve.tensor_tensor_reduce(a[:, cc, k0:k1], ps[:, 2 * (h % 2) + cc, k0:k1],
                                                       bias_t[:, h, P:S] if t == 0 else bias_t[:, h, :], 1.0, NEG,
                                                       ALU.add, ALU.max, st[:, 0, 2 * cc + t:2 * cc + t + 1])
                link(ins)
                dve.tensor_scalar(st[:, 0, :], st[:, 0, :], -HD ** -0.5, None, ALU.mult).then_inc(sc_max, 1)

            def combine(h):
                a, st = att_s[h % 3], stat[:, h % 4]
                dve.wait_ge(sc_exp, 4 * h + 4)
                link(dve.reciprocal(st[:, 2, :], st[:, 1, :]))
                link(dve.scalar_tensor_tensor(st[:, 2, 2:4], st[:, 2, 2:4], lam[:, 0:1], st[:, 1, 0:2], ALU.mult, ALU.mult))
                for t, (k0, k1) in enumerate(((0, P), (P, P + S))):
                    ins = dve.scalar_tensor_tensor(a[:, 0, k0:k1], a[:, 1, k0:k1], st[:, 2, 2 + t:3 + t],
                                                   a[:, 0, k0:k1], ALU.mult, ALU.add)
                ins.then_inc(att_ready, 1)

            def head_square(h):
                dve.wait_ge(o_ready, T * (h + 1))
                if h > 0:
                    dve.wait_ge(oms_ready, T * h)
                for t in range(T):
                    o = hs[:, t, h * P:h * P + P]
                    dve.tensor_tensor_reduce(junk[:, t, :], o, o, 1.0 / P, 0.0, ALU.mult, ALU.add,
                                             oss[:, h, t:t + 1]).then_inc(oms_ready, 1)

            def head_eps(half):
                dve.wait_ge(oms_ready, (half + 1) * T * NH // 2)
                o4 = oss[:, half * 4:half * 4 + 4, :].rearrange("p h t -> p (h t)")
                dve.tensor_scalar(o4, o4, EPS, None, ALU.add).then_inc(omse_ready, 1)

            def head_norm(half):
                dve.wait_ge(orstd_ready, half + 1)
                for h in range(4 * half, 4 * half + 4):
                    for t in range(T):
                        o = hs[:, t, h * P:h * P + P]
                        ins = dve.scalar_tensor_tensor(o, o, oss[:, h, t:t + 1], subln[:, :], ALU.mult, ALU.mult)
                    ins.then_inc(on_ready, 1)

            row_max(0)
            row_max(1)
            for h in range(NH):
                combine(h)
                if h + 2 < NH:
                    row_max(h + 2)
                if h >= 3:
                    head_square(h - 3)
                if h == NH - 2:
                    head_eps(0)
            head_square(NH - 3)
            head_norm(0)
            head_square(NH - 2)
            head_square(NH - 1)
            head_eps(1)
            low(R_WO, Q_WO)
            finish_rows(1, (2, 3))
            head_norm(1)
            for b in range(4):
                dve.wait_ge(ot_hi, b + 1)
                low_from(tlo[:, 512 * b:512 * b + 512], bank(b), thi[:, 512 * b:512 * b + 512], ot_lo)
            for u in range(1, 4):
                low(R_WO + u, Q_WO + u)
            finish_rows(1, (4,))
            residual(2, lambda t: ps[:, 4 + 2 * t:6 + 2 * t, :])

            modulated(3)
            dve.wait_ge(lg_ps, 1)
            link(dve.tensor_copy(logits, bank(4, 16).rearrange("p (t e) -> p t e", t=T)))
            for t in range(T):
                ins = dve.max(top[:, t, :], logits[:, t, :])
            link(ins)
            dve.tensor_tensor(diff, top[:, :, 1], top[:, :, 0], ALU.subtract).then_inc(top_ready, 1)
            for t in range(T):
                ins = dve.max_index(top_idx[:, t, :], top[:, t, :], logits[:, t, :])
            link(ins)
            link(dve.tensor_copy(idx_f, top_idx[:, :, :]))
            for i in range(2):
                for t in range(T):
                    ins = dve.tensor_scalar(oh[i][:, t, :], slots[:, 0:NE], idx_f[:, t, i:i + 1], None, ALU.is_equal)
            link(ins)
            dve.tensor_tensor(mask, oh[0], oh[1], ALU.add).then_inc(mask_ready, 1)
            dve.wait_ge(e2_ready, 1)
            link(dve.tensor_scalar(w2[:, 2:4], w2[:, 0:2], 1.0, None, ALU.add))
            link(dve.reciprocal(w2[:, 4:6], w2[:, 2:4]))
            link(dve.tensor_tensor(w2[:, 6:8], w2[:, 4:6], w2[:, 0:2], ALU.mult))
            for t in range(T):
                link(dve.tensor_scalar(gates[:, t, :], oh[0][:, t, :], w2[:, 4 + t:5 + t], None, ALU.mult))
                link(dve.scalar_tensor_tensor(gates[:, t, :], oh[1][:, t, :], w2[:, 6 + t:7 + t], gates[:, t, :], ALU.mult, ALU.add))
            dve.wait_ge(pos_ps, 1)
            link(dve.scalar_tensor_tensor(posm[:, :, 0:NE], bank(5, 16).rearrange("p (t e) -> p t e", t=T), 1.0, mask, ALU.add, ALU.mult))
            dve.memset(posm[:, :, NE:NE + 1], -1.0)
            link(dve.tensor_scalar(posm[:, :, 0:NE], posm[:, :, 0:NE], -1.0, None, ALU.add))
            link(dve.tensor_reduce(cnt[:, 0:1], ps[:, 5, 16:24], AX_X, ALU.max))
            link(dve.tensor_scalar(cnt[:, 1:2], cnt[:, 0:1], float(P), None, ALU.is_gt))
            dve.tensor_copy(flag[:, :], cnt[:, 1:2]).then_inc(route_ready, 1)

            def experts(ps_no):
                r0, q0, j0 = (R_MOE + ps_no * NE * EXPERT_UNITS, Q_MOE + ps_no * NE * EXPERT_UNITS, ps_no * NE)
                n0 = ps_no * (NE + 1)

                def select(e):
                    for t in range(T):
                        dve.tensor_scalar(sel[:, t, :], slots, posm[:, t, bass.ds(e, 1)], None, ALU.is_equal).then_inc(sel_ready, 1)

                def gathered_low(n):
                    for b in range(2):
                        dve.wait_ge(g_hi, 2 * n + b + 1)
                        low_from(tlo[:, 512 * b:512 * b + 512], bank(6 + b), thi[:, 512 * b:512 * b + 512], g_lo)

                def add_scattered(n):
                    for t in range(T):
                        for half in range(2):
                            dve.wait_ge(scat_ps, 4 * n + 2 * t + half + 1)
                            dst = moe_out[:, t, half * 512:half * 512 + 512]
                            dve.tensor_tensor(dst, dst, bank(6 - 4 * t + half), ALU.add).then_inc(scat_done, 1)

                select(0)
                if ps_no == 0:
                    finish_rows(1, (5,))
                gathered_low(n0)
                with dve.Fori(0, NE) as e:
                    j, ro, qo = e + j0, e * (EXPERT_UNITS // RAW), e * EXPERT_UNITS

                    def times_up(s, so=0):
                        dve.wait_ge(e_sg, j * NCE + s + 1 + so)
                        dve.tensor_tensor(actf[:, 0:FC], sg[:, 0:FC], bank(s % 2)[:, FC:2 * FC], ALU.mult).then_inc(e_act, 1)

                    def act_low(s, so=0):
                        dve.wait_ge(e_ahi, j * NCE + s + 1 + so)
                        a = (s % 2) * FC
                        low_from(alo[:, a:a + FC], bank(2 + s % 2, FC), ahi[:, a:a + FC], e_alo)

                    for u in range(3):
                        low(r0 + u, q0 + u, ro, qo)
                    times_up(0)
                    low(r0 + 3, q0 + 3, ro, qo)
                    add_scattered(e + n0)
                    for t in range(T):
                        dve.tensor_scalar(selg[:, t, :], slots, posm[:, t, bass.ds(e, 1)], gates[:, t, bass.ds(e, 1)],
                                          ALU.is_equal, ALU.mult).then_inc(selg_ready, 1)
                    select(e + 1)
                    with dve.Fori(0, (NCE - 2) // 2) as it:
                        for st in range(2):
                            u = 4 + 3 * st
                            low(r0 + u, q0 + u, ro + it, qo + it * 6)
                            low(r0 + u + 1, q0 + u + 1, ro + it, qo + it * 6)
                            act_low(st, it * 2)
                            times_up(st + 1, it * 2)
                            low(r0 + u + 2, q0 + u + 2, ro + it, qo + it * 6)
                    act_low(NCE - 2)
                    times_up(NCE - 1)
                    low(r0 + 40, q0 + 40, ro, qo)
                    gathered_low(e + n0 + 1)
                    act_low(NCE - 1)
                    low(r0 + 41, q0 + 41, ro, qo)
                add_scattered(n0 + NE)
                dve.wait_ge(scat_done, 4 * (n0 + NE + 1))

            dve.wait_ge(route_ready, 1)
            dve.wait_ge(moe_cleared, 1)
            experts(0)
            over = dve.value_load(flag[0:1, 0:1], min_val=0, max_val=1)
            with dve.If(over > 0):
                link_less = dve.tensor_scalar(posm[:, :, :], posm[:, :, :], float(-P), None, ALU.add)
                link_less.then_inc(over_ready, 1)
                dve.wait_ge(over_ready, 1)
                experts(1)
            for t in range(T):
                dve.tensor_tensor_reduce(ysb[:, t, :], moe_out[:, t, :], moe_out[:, t, :], 1.0 / D, 0.0,
                                         ALU.mult, ALU.add, ss[:, 14 + t:15 + t]).then_inc(ss_ready, 1)
            residual(3, lambda t: moe_out[:, t, :])

        @block.tensor
        def _(pe):
            def row_sum(l, g):
                for h in range(2):
                    mm = pe.matmul(bank(ROW_BANK[l][g] + h), ones, rows[:, ROW[l][g], h * 512:h * 512 + 512], start=True, stop=True)
                mm.then_inc(row_ps, 1)

            def transposes(done, heads=False):
                for b in range(4):
                    if heads:
                        pe.wait_ge(on_ready, 2 * b + 2)
                    for k in (2 * b, 2 * b + 1):
                        for t in range(T):
                            c0 = (k % 2) * S + t * P
                            mm = pe.transpose(ps[:, b, c0:c0 + P], hs[:, t, k * P:k * P + P], ident)
                    mm.then_inc(done, 1)

            def three(out, a_hi, a_lo, b_hi, b_lo, start, stop, check):
                pe.matmul(out, a_hi, b_hi, start=start, stop=False, skip_group_check=check)
                pe.matmul(out, a_hi, b_lo, start=False, stop=False, skip_group_check=check)
                return pe.matmul(out, a_lo, b_hi, start=False, stop=stop, skip_group_check=check)

            def zero_bank(b):
                for h in range(4):
                    pe.matmul(ps[:, b, h * P:h * P + P], zeros[:, :], zeros[:, :], start=(h == 0), stop=False,
                              skip_group_check=True)

            pe.wait_ge(consts_loaded, 16)
            pe.wait_ge(small_loaded, 32)
            pe.matmul(ps[0:NH, 5, 0:S], relb, onehot, start=True, stop=True).then_inc(dist_ps, 1)
            pe.wait_ge(unit_done, 12)
            pe.wait_ge(dist_ready, 2)
            row_sum(0, 1)
            row_sum(0, 0)
            pe.wait_ge(row_done, row_rank(0, 1))
            row_sum(0, 2)
            pe.wait_ge(pool_loaded, 32)
            pe.wait_ge(h_ready, T)
            for b in range(4):
                for t in range(T):
                    for k in (2 * b, 2 * b + 1):
                        c0 = (k % 2) * S
                        g = k // 2
                        if t == 0:
                            mm = pe.matmul(ps[:, b, c0:c0 + S], hs[:, 0, k * P:k * P + P], pool_m[:, g, 0:S],
                                           start=(k % 2 == 0), stop=False, skip_group_check=True)
                        else:
                            mm = pe.matmul(ps[:, b, c0 + P:c0 + S], hs[:, 1, k * P:k * P + P], pool_m[:, g, S:S + P],
                                           start=False, stop=True, skip_group_check=True)
                mm.then_inc(pooled_ps, 1)
            pe.wait_ge(pooled_ready, 4)
            pe.wait_ge(row_done, 3)
            for t in range(T):
                for g in range(4):
                    for k in range(2):
                        mm = pe.matmul(ps[:, 4 + 2 * t + g // 2, (g % 2) * FC:(g % 2) * FC + FC],
                                       pooled_t[:, 2 * g + k, t * P:t * P + P], poolw[:, g, k, :],
                                       start=(g % 2 == 0 and k == 0), stop=(k == 1), skip_group_check=True)
            mm.then_inc(mix_ps, 1)
            pe.wait_ge(unit_done, 24)
            pe.wait_ge(y_scaled, T)
            for g in (4, 3, 5):
                row_sum(0, g)
            pe.wait_ge(h_ready, 2 * T)
            transposes(ht_ps)

            def ffn_gate_up(s, r, q, it=0, first=False):
                for kh in range(2):
                    pe.wait_ge(unit_done, r + kh + 1 + it * 12)
                    sl = (q + kh) % SPL
                    for kk in range(4):
                        k = 4 * kh + kk
                        if first and k % 2 == 0:
                            pe.wait_ge(ht_lo, max(k // 2 + 1, 2))
                        for jj in range(2):
                            for g in range(2):
                                c0 = kk * 512 + g * FC + jj * P
                                o = ps[:, 2 * (s % 2) + jj, g * S:g * S + S]
                                mm = three(o, whi[:, sl, c0:c0 + P], wlo[:, sl, c0:c0 + P], thi3[:, k, :], tlo3[:, k, :],
                                           k == 0 and g == 0, k == KC - 1 and g == 1, True)
                    mm.then_inc(unit_used, 1)

            def ffn_down(s, r, q, it=0, last=False):
                pe.wait_ge(f_alo, s + 1 + it * 2)
                pe.wait_ge(unit_done, r + 1 + it * 12)
                sl = q % SPL
                for jj in range(2):
                    for t in range(T):
                        a = slice(jj * S + t * P, jj * S + t * P + P)
                        for half in range(2):
                            w = slice(jj * D + half * 512, jj * D + half * 512 + 512)
                            mm = three(bank(4 + 2 * t + half), ahi[:, a], alo[:, a], whi[:, sl, w], wlo[:, sl, w],
                                       False, last and jj == 1, True)
                mm.then_inc(unit_used, 1)

            ffn_gate_up(0, R_FFN, 0, first=True)
            pe.wait_ge(zeros_ready, 1)
            pe.wait_ge(row_done, 6)
            for b in range(4, 8):
                zero_bank(b)
            with pe.Fori(0, MOD_STEPS // 2) as it:
                for st in range(2):
                    r, q = R_FFN + 2 + 6 * st, 2 + 3 * st
                    ffn_gate_up(st + 1, r, q, it)
                    ffn_down(st, r + 5, q + 2, it)
            for s in range(MOD_STEPS, NCF - 1):
                r, q = R_FFN + 2 + 3 * MOD_STEPS + 3 * s, 2 + 3 * s
                ffn_gate_up(s + 1, r, q)
                ffn_down(s, r + 2, q + 2)
            row_sum(1, 1)
            ffn_down(NCF - 1, R_QKV - 1, Q_QKV - 1, last=True)
            row_sum(1, 0)
            pe.wait_ge(bias_loaded, 16)
            pe.wait_ge(x_done, 2 * T)
            for b in range(4):
                pe.matmul(bank(4 + b), reverse, bias_rev[:, 2 * b:2 * b + 2, :].rearrange("p h k -> p (h k)"),
                          start=True, stop=True).then_inc(bias_ps, 1)
            pe.wait_ge(h_ready, 3 * T)
            transposes(ht_ps)
            pe.wait_ge(bias_ready, 4)

            def qkv_group(g):
                if g >= 2:
                    pe.wait_ge(qkv_ready, g - 1)
                for kh in range(2):
                    r, q = R_QKV + 2 * g + kh, Q_QKV + 2 * g + kh
                    pe.wait_ge(unit_done, r + 1)
                    for kk in range(4):
                        k = 4 * kh + kk
                        if g == 0 and k % 2 == 0:
                            pe.wait_ge(ht_lo, 4 + k // 2 + 1)
                        if g < 4:
                            for m in range(4):
                                c0 = kk * 512 + m * P
                                o = ps[:, 4 + 2 * (g % 2) + m // 2, (m % 2) * S:(m % 2) * S + S]
                                mm = three(o, whi[:, q % SPL, c0:c0 + P], wlo[:, q % SPL, c0:c0 + P],
                                           thi3[:, k, :], tlo3[:, k, :], k == 0 and m % 2 == 0, k == KC - 1 and m % 2 == 1, True)
                        else:
                            for t in range(T):
                                w = slice(kk * 512, kk * 512 + 512)
                                mm = three(bank(4 + 2 * (g % 2) + t), thi3[:, k, t * P:t * P + P], tlo3[:, k, t * P:t * P + P],
                                           whi[:, q % SPL, w], wlo[:, q % SPL, w], k == 0, k == KC - 1, False)
                    mm.then_inc(unit_used, 1)

            for g in range(5):
                qkv_group(g)

            def scores(h):
                if h >= 2:
                    pe.wait_ge(sc_max, h - 1)
                for cc in range(2):
                    rows_c = slice(cc * HD, cc * HD + HD)
                    b = 2 * (h % 2) + cc
                    pe.matmul(ps[:, b, 0:P], qk_t[rows_c, h, 0:P], qk_t[rows_c, NH + h, 0:P], start=True, stop=True)
                    mm = pe.matmul(ps[:, b, P:P + S], qk_t[rows_c, h, P:S], qk_t[rows_c, NH + h, :], start=True, stop=True)
                mm.then_inc(sc_ps, 1)

            def values(h):
                pe.wait_ge(at_ready, h + 1)
                if h >= 2:
                    pe.wait_ge(o_ready, h - 1)
                b, at, cols = 6 + h % 2, att_at[h % 2], slice(h * P, h * P + P)
                pe.matmul(ps[:, b, 0:P], at[:, 0:P], vs[:, 0, cols], start=True, stop=True)
                pe.matmul(ps[:, b, P:S], at[:, P:2 * P], vs[:, 0, cols], start=True, stop=False)
                pe.matmul(ps[:, b, P:S], at[:, 2 * P:3 * P], vs[:, 1, cols], start=False, stop=True).then_inc(o_ps, 1)

            scores(0)
            scores(1)
            qkv_group(5)
            scores(2)
            pe.wait_ge(qkv_ready, 6)
            for h in range(NH):
                pe.wait_ge(att_ready, h + 1)
                if h >= 2:
                    pe.wait_ge(at_ready, h - 1)
                for i in range(3):
                    mm = pe.transpose(ps[:, 4 + h % 2, i * P:i * P + P], att_s[h % 3][:, 0, i * P:i * P + P], ident)
                mm.then_inc(at_ps, 1)
                if h + 3 < NH:
                    scores(h + 3)
                if h > 0:
                    values(h - 1)
            values(NH - 1)
            row_sum(1, 2)
            row_sum(1, 3)
            pe.wait_ge(row_done, row_rank(1, 3))
            transposes(ot_ps, heads=True)
            for half in range(2):
                for kh in range(2):
                    r, q = R_WO + 2 * half + kh, Q_WO + 2 * half + kh
                    pe.wait_ge(unit_done, r + 1)
                    for kk in range(4):
                        k, w = 4 * kh + kk, slice(kk * 512, kk * 512 + 512)
                        if half == 0 and k % 2 == 0:
                            pe.wait_ge(ot_lo, k // 2 + 1)
                        for t in range(T):
                            mm = three(bank(4 + 2 * t + half), thi3[:, k, t * P:t * P + P], tlo3[:, k, t * P:t * P + P],
                                       whi[:, q % SPL, w], wlo[:, q % SPL, w], k == 0, k == KC - 1, False)
                    mm.then_inc(unit_used, 1)
            row_sum(1, 4)

            pe.wait_ge(h_ready, 4 * T)
            transposes(ht_ps)
            pe.wait_ge(wr_loaded, 16)
            for k in range(KC):
                if k % 2 == 0:
                    pe.wait_ge(ht32_ready, k // 2 + 1)
                for t in range(T):
                    mm = pe.matmul(ps[:, 4, t * NE:t * NE + NE], ht32[:, k, t * P:t * P + P], wr[:, k, :],
                                   start=(k == 0 and t == 0), stop=(k == KC - 1), skip_group_check=True)
            mm.then_inc(lg_ps, 1)
            row_sum(1, 5)
            pe.wait_ge(mask_ready, 1)
            pe.matmul(ps[:, 5, 0:NE], before, mask[:, 0, :], start=True, stop=True)
            pe.matmul(ps[:, 5, NE:2 * NE], ones, mask[:, 0, :], start=True, stop=False)
            pe.matmul(ps[:, 5, NE:2 * NE], before, mask[:, 1, :], start=False, stop=True)
            pe.matmul(ps[:, 5, 2 * NE:3 * NE], ones, mask[:, 0, :], start=True, stop=False)
            pe.matmul(ps[:, 5, 2 * NE:3 * NE], ones, mask[:, 1, :], start=False, stop=True).then_inc(pos_ps, 1)

            def experts(ps_no):
                r0, q0, j0 = (R_MOE + ps_no * NE * EXPERT_UNITS, Q_MOE + ps_no * NE * EXPERT_UNITS, ps_no * NE)
                n0 = ps_no * (NE + 1)

                def gather(n):
                    pe.wait_ge(sel_ready, T * n + T)
                    for b in range(2):
                        for k in range(4 * b, 4 * b + 4):
                            for t in range(T):
                                mm = pe.matmul(ps[:, 6 + b, (k % 4) * P:(k % 4) * P + P], hs[:, t, k * P:k * P + P],
                                               sel[:, t, :], start=(t == 0), stop=(t == T - 1))
                        mm.then_inc(g_ps, 1)

                def scatter(n):
                    pe.wait_ge(y_ready, 2 * n + 2)
                    for t in range(T):
                        for half in range(2):
                            pe.matmul(bank(6 - 4 * t + half), selg_t[:, t * P:t * P + P], y_e[:, half * 512:half * 512 + 512],
                                      start=True, stop=True).then_inc(scat_ps, 1)

                pe.wait_ge(selt_cleared, ps_no + 1)
                gather(n0)
                with pe.Fori(0, NE) as e:
                    j, ro = e + j0, e * EXPERT_UNITS

                    def gate_up(s, u, it=0):
                        for kh in range(2):
                            pe.wait_ge(unit_done, r0 + u + kh + 1 + ro + it * 6)
                            sl = (q0 + u + kh) % SPL
                            for kk in range(4):
                                k, w = 4 * kh + kk, slice(kk * 512, kk * 512 + 512)
                                mm = three(bank(s % 2), ghi[:, k, :], glo[:, k, :], whi[:, sl, w], wlo[:, sl, w],
                                           k == 0, k == KC - 1, False)
                            mm.then_inc(unit_used, 1)

                    def turn(s, it=0):
                        pe.wait_ge(e_act, j * NCE + s + 1 + it * 2)
                        for jj in range(2):
                            mm = pe.transpose(ps[:, 2 + s % 2, jj * P:jj * P + P], actf[:, jj * P:jj * P + P], ident)
                        mm.then_inc(e_at, 1)

                    def down(s, u, it=0, last=False):
                        pe.wait_ge(e_alo, j * NCE + s + 1 + it * 2)
                        pe.wait_ge(unit_done, r0 + u + 1 + ro + it * 6)
                        sl = (q0 + u) % SPL
                        for jj in range(2):
                            a = slice((s % 2) * FC + jj * P, (s % 2) * FC + jj * P + P)
                            for half in range(2):
                                w = slice(jj * D + half * 512, jj * D + half * 512 + 512)
                                mm = three(bank(4 + half), ahi[:, a], alo[:, a], whi[:, sl, w], wlo[:, sl, w],
                                           False, last and jj == 1, True)
                        mm.then_inc(unit_used, 1)

                    pe.wait_ge(g_lo, 2 * (e + n0) + 2)
                    gate_up(0, 0)
                    scatter(e + n0)
                    gate_up(1, 2)
                    pe.wait_ge(scat_done, 4 * (e + n0) + 4)
                    turn(0)
                    zero_bank(4)
                    zero_bank(5)
                    with pe.Fori(0, (NCE - 2) // 2) as it:
                        for st in range(2):
                            gate_up(st, 4 + 3 * st, it)
                            turn(st + 1, it)
                            down(st, 6 + 3 * st, it)
                    pe.wait_ge(selg_ready, T * j + T)
                    for t in range(T):
                        mm = pe.transpose(ps[:, 0, t * P:t * P + P], selg[:, t, :], ident)
                    mm.then_inc(selt_ps, 1)
                    gather(e + n0 + 1)
                    turn(NCE - 1)
                    down(NCE - 2, 40)
                    down(NCE - 1, 41, last=True)
                    pe.wait_ge(selt_ready, j + 1)
                scatter(n0 + NE)

            pe.wait_ge(route_ready, 1)
            experts(0)
            over = pe.value_load(flag[0:1, 0:1], min_val=0, max_val=1)
            with pe.If(over > 0):
                experts(1)


def kernel(x, c, w_mod, b_mod, norm_g, pool_w, pool_scale, w_qkv, w_o, subln_g, lambda_vecs, rel_bias,
           ffn_w_gu, ffn_w_down, w_router, moe_w_gu, moe_w_down):
    import concourse.bacc as bacc
    from concourse.bass_utils import run_bass_kernel_spmd

    consts, pool_m, onehot = shape_constants()
    arrays = dict(x=x, c=c, w_mod=w_mod, b_mod=b_mod, norm_g=norm_g, pool_w=pool_w, pool_scale=pool_scale,
                  w_qkv=w_qkv, w_o=w_o, subln_g=subln_g, lambda_vecs=lambda_vecs, rel_bias=rel_bias,
                  ffn_w_gu=ffn_w_gu, ffn_w_down=ffn_w_down, w_router=w_router, moe_w_gu=moe_w_gu,
                  moe_w_down=moe_w_down, consts_in=consts, pool_in=pool_m, onehot_in=onehot)
    arrays = {name: np.ascontiguousarray(a) for name, a in arrays.items()}
    nc = bacc.Bacc("TRN2", target_bir_lowering=False, num_devices=1,
                   dynamic_dma_scratch_size=8192)
    aps = {name: nc.dram_tensor(name, a.shape, F32, kind="ExternalInput").ap() for name, a in arrays.items()}
    out = nc.dram_tensor("out", (1, S, D), F32, kind="ExternalOutput").ap()
    build_trunk(nc, out=out, **aps)
    result = run_bass_kernel_spmd(nc, [arrays], core_ids=[0])
    return result.results[0]["out"]
```

```python
import math
from contextlib import ExitStack

import numpy as np
import concourse.bass as bass
from concourse import mybir
from concourse.alu_op_type import AluOpType as ALU

ACT = mybir.ActivationFunctionType
AX_X = mybir.AxisListType.X
F32 = mybir.dt.float32
F32R = mybir.dt.float32r
BF16 = mybir.dt.bfloat16
I32 = mybir.dt.int32
U32 = mybir.dt.uint32

P = 128
D = 1024
S = 256
T = S // P
KC = D // P
EPS = 1e-6
N_MOD = 6
WINDOWS = (2, 4, 8, 16)
NH = 8
HD = 64
N_BUCKETS = 32
MAX_DISTANCE = 128
FF = 2816
NE = 8
FE = 3584
LAMBDA_INIT = 0.8 - 0.6 * math.exp(-0.3 * 1)
NEG = -3.0e38

RAW = 6
SPL = 3
UNIT = 2048
FC = 256
NCF = FF // FC
NCE = FE // FC

MIXER_MODS = [(0, g, pair) for pair in range(4) for g in range(3)]
FFN_MODS = [(0, g, pair) for pair in range(4) for g in (3, 4)]
LOOP_STEPS = 4
LOOP_MODS = [[(1, 0, 0), (1, 1, 0)], [(1, 2, 0)], [(1, 0, 1), (1, 1, 1)], [(1, 2, 1)]]
LOOP_TURNS = (NCF - 1) // LOOP_STEPS
TAIL_MODS = [[(0, 5, 0), (0, 5, 1), (0, 5, 2)], [(0, 5, 3), (1, 3, 0), (1, 3, 1)]]
QKV_MODS = [[(1, 3, 2), (1, 3, 3)], [(1, 4, 0), (1, 4, 1)], [(1, 4, 2), (1, 4, 3)], [(1, 5, 0), (1, 5, 1)],
            [(1, 5, 2), (1, 5, 3)], []]

R_FFN, Q_FFN = len(MIXER_MODS) + len(FFN_MODS), 0
TURN_MODS = sum(len(m) for m in LOOP_MODS)
TURN_UNITS = 3 * LOOP_STEPS + TURN_MODS
assert TURN_UNITS % RAW == 0 and 3 * LOOP_STEPS % SPL == 0


def ffn_steps():
    r, q, n, steps = R_FFN + 2, 2, R_FFN, []
    for s in range(LOOP_STEPS):
        steps.append((s, r, q, LOOP_MODS[s], n))
        r, q, n = r + 3 + len(LOOP_MODS[s]), q + 3, n + len(LOOP_MODS[s])
    r, q, n = (v + (LOOP_TURNS - 1) * w for v, w in zip((r, q, n), (TURN_UNITS, 3 * LOOP_STEPS, TURN_MODS)))
    for s in range(LOOP_STEPS * LOOP_TURNS, NCF - 1):
        mods = TAIL_MODS[s - LOOP_STEPS * LOOP_TURNS]
        steps.append((s, r, q, mods, n))
        r, q, n = r + 3 + len(mods), q + 3, n + len(mods)
    return steps[:LOOP_STEPS], steps[LOOP_STEPS:], r, q, n


FFN_LOOP, FFN_TAIL, R_LAST_DOWN, Q_LAST_DOWN, N_QKV_MODS = ffn_steps()
R_QKV, Q_QKV = R_LAST_DOWN + 1, Q_LAST_DOWN + 1
R_GROUP = [R_QKV + 2 * g + sum(len(m) for m in QKV_MODS[:g]) for g in range(6)]
R_WO, Q_WO = R_GROUP[5] + 2, Q_QKV + 12
R_MOE, Q_MOE = R_WO + 4, Q_WO + 4
EXPERT_UNITS = 3 * NCE
assert EXPERT_UNITS % RAW == 0 and EXPERT_UNITS % SPL == 0

ROW = [[0, 1, 2, 3, 4, 5], [6, 0, 1, 2, 3, 4]]
ROW_ORDER = [[1, 0, 2, 4, 3, 5], [1, 0, 2, 3, 4, 5]]
ROW_BANK = [[4, 6, 6, 0, 2, 2], [2, 0, 0, 2, 0, 2]]
ROW_GAIN = {1: 0, 2: 1, 4: 2, 5: 3}


def row_rank(l, g):
    return 6 * l + ROW_ORDER[l].index(g) + 1


def done_rank(l, g):
    return sum((b % 3 == 0) == (g % 3 == 0)
               for a in range(l + 1) for b in ROW_ORDER[a] if row_rank(a, b) <= row_rank(l, g))


def shape_constants():
    consts = np.zeros((P, 5, P), np.float32)
    consts[:, 0] = np.eye(P)
    consts[:, 1] = 1.0
    consts[:, 2] = np.triu(np.ones((P, P)), 1)
    consts[:, 3] = np.arange(P)[None, :]
    consts[:, 4] = np.eye(P)[::-1]
    pool = np.zeros((P, len(WINDOWS), S + P), np.float32)
    for g, w in enumerate(WINDOWS):
        full = np.zeros((S, S), np.float64)
        for s in range(S):
            lo = max(0, s - w + 1)
            full[lo:s + 1, s] = 1.0 / min(s + 1, w)
            full[s, s] -= 1.0
        pool[:, g, 0:S] = full[0:P]
        pool[:, g, S:] = full[P:, P:]
    n = S - 1 - np.arange(S)
    exact = N_BUCKETS // 2
    nf = np.maximum(n, 1).astype(np.float32)
    large = exact + (np.log(nf / np.float32(exact)) / np.float32(math.log(MAX_DISTANCE / exact))
                     * np.float32(N_BUCKETS - exact)).astype(np.int32)
    bucket = np.where(n < exact, n, np.minimum(large, N_BUCKETS - 1))
    onehot = np.zeros((N_BUCKETS, S), np.float32)
    onehot[bucket, np.arange(S)] = 1.0
    return consts.reshape(P, 5 * P), pool.reshape(P, -1), onehot


def build_trunk(nc, x, c, w_mod, b_mod, norm_g, pool_w, pool_scale, w_qkv, w_o, subln_g, lambda_vecs,
                rel_bias, ffn_w_gu, ffn_w_down, w_router, moe_w_gu, moe_w_down,
                consts_in, pool_in, onehot_in, out):
    bias_dram = nc.dram_tensor("bias_by_distance", (NH, S + P), F32, kind="Internal").ap()

    with ExitStack() as ctx:
        def sb(name, shape, dt=F32):
            return ctx.enter_context(nc.sbuf_tensor(name, shape, dt))

        def sem(name):
            return ctx.enter_context(nc.semaphore(name))

        raw = sb("raw", [P, RAW, UNIT])
        whi = sb("whi", [P, SPL, UNIT], F32R)
        wlo = sb("wlo", [P, SPL, UNIT], F32R)
        rows = sb("rows", [P, 7, D])
        xs = sb("xs", [P, T, D])
        hs = sb("hs", [P, T, D])
        thi = sb("thi", [P, UNIT], F32R)
        tlo = sb("tlo", [P, UNIT], F32R)
        ahi = sb("ahi", [P, 512], F32R)
        alo = sb("alo", [P, 512], F32R)
        gain = sb("gain", [P, 2, D])
        scr = sb("scr", [P, 6 * D])
        ysb = sb("ysb", [P, T, D])
        tmp = sb("tmp", [P, 2304])
        consts = sb("consts", [P, 5, P])
        subln = sb("subln", [P, P])
        zeros = sb("zeros", [P, P], BF16)
        wr = sb("wr", [P, KC, NE])
        silu_c = sb("silu_c", [P, KC])
        ss = sb("ss", [P, 16])
        rstd = sb("rstd", [P, 16])
        minus_half = sb("minus_half", [P, 8])
        lam = sb("lam", [P, 4])
        stat = sb("stat", [P, 4, 3, 4])
        oss = sb("oss", [P, NH, T])
        posm = sb("posm", [P, T, NE])
        gates = sb("gates", [P, T, NE])
        flag = sb("flag", [P, 1], I32)

        ident, ones, before, slots, reverse = (consts[:, i, :] for i in range(5))
        thi3 = thi[:, :].rearrange("p (k s) -> p k s", k=KC)
        tlo3 = tlo[:, :].rearrange("p (k s) -> p k s", k=KC)
        ghi = thi[:, 0:D].rearrange("p (k s) -> p k s", k=KC)
        glo = tlo[:, 0:D].rearrange("p (k s) -> p k s", k=KC)
        pool_m = scr[:, 0:4 * 384].rearrange("p (g s) -> p g s", g=4)
        poolw = scr[:, 1536:3584].rearrange("p (g c e) -> p g c e", g=4, c=2)
        onehot = scr[0:N_BUCKETS, 3584:3840]
        relb = scr[0:N_BUCKETS, 3840:3848]
        bias_row = scr[0:NH, 3848:3848 + S + P]
        lamv = scr[:, 4352:4608].rearrange("p (v d) -> p v d", v=4)
        lamj = scr[:, 4608:4672]
        bias_rev = scr[:, 4096:6144].rearrange("p (h k) -> p h k", h=NH)
        qk_t = scr[:, 0:4096].rearrange("p (m s) -> p m s", m=2 * NH)
        vs = scr[:, 4096:6144].rearrange("p (t e) -> p t e", t=T)
        ht32 = scr[:, 0:2048].rearrange("p (k s) -> p k s", k=KC)
        moe_out = scr[:, 2048:4096].rearrange("p (t d) -> p t d", t=T)
        y_e = scr[:, 4096:5120]
        pooled_t = ysb[:, :, :].rearrange("p t (k s) -> p (t k) s", s=S)
        bias_t = ysb[:, :, :].rearrange("p t (k s) -> p (t k) s", s=S)
        att_s = [tmp[:, 768 * b:768 * b + 768].rearrange("p (c k) -> p c k", c=2) for b in range(3)]
        att_at = [gain[:, 0, 384 * b:384 * b + 384] for b in range(2)]
        junk = gain[:, 0, 768:1024].rearrange("p (t e) -> p t e", t=T)
        sg = tmp[:, 0:512]
        actf = tmp[:, 512:1024]
        sel = tmp[:, 1024:1280].rearrange("p (t s) -> p t s", t=T)
        selg = tmp[:, 1280:1536].rearrange("p (t s) -> p t s", t=T)
        selg_t = tmp[:, 1536:1792]
        rt = tmp[:, 1792:2304]
        logits = rt[:, 0:16].rearrange("p (t e) -> p t e", t=T)
        top = rt[:, 16:32].rearrange("p (t e) -> p t e", t=T)
        idx_f = rt[:, 48:64].rearrange("p (t e) -> p t e", t=T)
        oh = [rt[:, 64 + 16 * i:80 + 16 * i].rearrange("p (t e) -> p t e", t=T) for i in range(2)]
        mask = rt[:, 96:112].rearrange("p (t e) -> p t e", t=T)
        w2 = rt[:, 112:120]
        cnt = rt[:, 120:124]
        diff = rt[:, 124:126]

        top_idx = sb("top_idx", [P, T, 8], U32)

        ps = ctx.enter_context(nc.psum_tensor("ps", [P, 8, 512], F32))

        def bank(b, n=512):
            return ps[:, b, 0:n]

        raw_loaded = [sem(f"raw_loaded{i}") for i in range(RAW)]
        hi_ready = sem("hi_ready")
        unit_done = sem("unit_done")
        unit_used = sem("unit_used")
        x_loaded = sem("x_loaded")
        c_loaded = sem("c_loaded")
        consts_loaded = sem("consts_loaded")
        pool_loaded = [sem(f"pool_loaded{i}") for i in range(2)]
        small_loaded = sem("small_loaded")
        lam_loaded = sem("lam_loaded")
        wr_loaded = sem("wr_loaded")
        scale_loaded = sem("scale_loaded")
        gain_loaded = [sem(f"gain_loaded{i}") for i in range(2)]
        bmod_loaded = [sem(f"bmod_loaded{i}") for i in range(4)]
        mixer_rows_zeroed = sem("mixer_rows_zeroed")
        rows_zeroed = sem("rows_zeroed")
        zeros_ready = sem("zeros_ready")
        silu_ready = sem("silu_ready")
        gemv = sem("gemv")
        row_ps = sem("row_ps")
        row_done = sem("row_done")
        shift_done = sem("shift_done")
        gated = sem("gated")
        scaled = sem("scaled")
        scale_folded = sem("scale_folded")
        ss_ready = sem("ss_ready")
        half_ready = sem("half_ready")
        ms_ready = sem("ms_ready")
        rstd_ready = sem("rstd_ready")
        oms_ready = sem("oms_ready")
        omse_ready = sem("omse_ready")
        orstd_ready = sem("orstd_ready")
        h_ready = sem("h_ready")
        ht_ps = sem("ht_ps")
        ht_hi = sem("ht_hi")
        ht_lo = sem("ht_lo")
        ht32_ready = sem("ht32_ready")
        x_done = sem("x_done")
        link_s = sem("vector_link")
        dist_ps = sem("dist_ps")
        dist_ready = sem("dist_ready")
        dist_stored = sem("dist_stored")
        bias_loaded = sem("bias_loaded")
        bias_ps = sem("bias_ps")
        bias_ready = sem("bias_ready")
        lam_prod = sem("lam_prod")
        lam_exp = sem("lam_exp")
        pooled_ps = sem("pooled_ps")
        pooled_ready = sem("pooled_ready")
        mix_ps = sem("mix_ps")
        f_sg = sem("f_sg")
        f_act = sem("f_act")
        f_ahi = sem("f_ahi")
        f_alo = sem("f_alo")
        qkv_ready = sem("qkv_ready")
        sc_ps = sem("sc_ps")
        sc_max = sem("sc_max")
        sc_exp = sem("sc_exp")
        att_ready = sem("att_ready")
        at_ps = sem("at_ps")
        at_ready = sem("at_ready")
        o_ps = sem("o_ps")
        o_ready = sem("o_ready")
        on_ready = sem("on_ready")
        ot_ps = sem("ot_ps")
        ot_hi = sem("ot_hi")
        ot_lo = sem("ot_lo")
        lg_ps = sem("lg_ps")
        top_ready = sem("top_ready")
        e2_ready = sem("e2_ready")
        mask_ready = sem("mask_ready")
        pos_ps = sem("pos_ps")
        route_ready = sem("route_ready")
        over_ready = sem("over_ready")
        sel_ready = sem("sel_ready")
        selg_ready = sem("selg_ready")
        selt_cleared = sem("selt_cleared")
        moe_cleared = sem("moe_cleared")
        selt_ps = sem("selt_ps")
        selt_ready = sem("selt_ready")
        g_ps = sem("g_ps")
        g_hi = sem("g_hi")
        g_lo = sem("g_lo")
        e_sg = sem("e_sg")
        e_act = sem("e_act")
        e_at = sem("e_at")
        e_ahi = sem("e_ahi")
        e_alo = sem("e_alo")
        y_ready = sem("y_ready")
        scat_ps = sem("scat_ps")
        scat_done = sem("scat_done")
        stored = sem("stored")

        block = ctx.enter_context(nc.Block())

        @block.sync
        def _(sp):
            def load(r, rounds, halves):
                if 3 <= r < RAW:
                    sp.wait_ge(raw_loaded[r - 3], 32)
                if r >= RAW:
                    sp.wait_ge(unit_done, r - RAW + 1 + rounds * RAW)
                dst = raw[:, r % RAW, :]
                for view, src in halves(dst):
                    sp.dma_start(view, src).then_inc(raw_loaded[r % RAW], 16)

            def mod_unit(l, g, pair):
                def halves(dst):
                    for kk in range(2):
                        yield (dst[:, kk * D:(kk + 1) * D],
                               w_mod[l].rearrange("(p k) f -> p k f", k=KC)[:, pair * 2 + kk, g * D:(g + 1) * D])
                return halves

            def gu_unit(w, width, chunk, kh):
                def halves(dst):
                    v = dst.rearrange("p (k g j) -> p k g j", k=4, g=2)
                    src = w.rearrange("(k p) f -> p k f", p=P)
                    for g in range(2):
                        yield v[:, :, g, :], src[:, kh * 4:kh * 4 + 4, bass.ds(chunk * FC + g * width, FC)]
                return halves

            def down_unit(w, chunk):
                def halves(dst):
                    for j in range(2):
                        yield dst[:, j * D:(j + 1) * D], w[bass.ds((chunk * 2 + j) * P, P), :]
                return halves

            def col_unit(w, col, kh):
                def halves(dst):
                    v = dst.rearrange("p (k j) -> p k j", k=4)
                    src = w.rearrange("(k p) f -> p k f", p=P)
                    for i in range(2):
                        yield v[:, 2 * i:2 * i + 2, :], src[:, kh * 4 + 2 * i:kh * 4 + 2 * i + 2, col:col + 512]
                return halves

            sp.dma_start(silu_c[:, :], c.rearrange("a (p k) -> (a p) k", k=KC)).then_inc(c_loaded, 16)
            for r, mod in enumerate(MIXER_MODS + FFN_MODS):
                load(r, 0, mod_unit(*mod))
                if r == RAW + 2:
                    sp.dma_start(xs[:, :, :], x[0].rearrange("(t p) d -> p t d", p=P)).then_inc(x_loaded, 16)
            w_gu, w_dn = ffn_w_gu[0], ffn_w_down[0]
            load(R_FFN, 0, gu_unit(w_gu, FF, 0, 0))
            load(R_FFN + 1, 0, gu_unit(w_gu, FF, 0, 1))

            def ffn_step(s, r, mods, it=0):
                load(r, it * (TURN_UNITS // RAW), gu_unit(w_gu, FF, it * LOOP_STEPS + s + 1, 0))
                load(r + 1, it * (TURN_UNITS // RAW), gu_unit(w_gu, FF, it * LOOP_STEPS + s + 1, 1))
                for i, (l, g, pair) in enumerate(mods):
                    load(r + 2 + i, it * (TURN_UNITS // RAW), mod_unit(l, g, it * 2 + pair))
                load(r + 2 + len(mods), it * (TURN_UNITS // RAW), down_unit(w_dn, it * LOOP_STEPS + s))

            with sp.Fori(0, LOOP_TURNS) as it:
                for s, r, _, mods, _ in FFN_LOOP:
                    ffn_step(s, r, mods, it)
            for s, r, _, mods, _ in FFN_TAIL:
                ffn_step(s, r, mods)
            load(R_LAST_DOWN, 0, down_unit(w_dn, NCF - 1))
            for g in range(6):
                for kh in range(2):
                    load(R_GROUP[g] + kh, 0, col_unit(w_qkv[0], g * 512, kh))
                for i, mod in enumerate(QKV_MODS[g]):
                    load(R_GROUP[g] + 2 + i, 0, mod_unit(*mod))
            for g in range(2):
                for kh in range(2):
                    load(R_WO + 2 * g + kh, 0, col_unit(w_o[0], g * 512, kh))

            def experts(ps_no):
                base = R_MOE + ps_no * NE * EXPERT_UNITS
                with sp.Fori(0, NE) as e:
                    gu, dn, eo = moe_w_gu[0, e], moe_w_down[0, e], e * (EXPERT_UNITS // RAW)
                    for s in range(2):
                        load(base + 2 * s, eo, gu_unit(gu, FE, s, 0))
                        load(base + 2 * s + 1, eo, gu_unit(gu, FE, s, 1))
                    with sp.Fori(0, (NCE - 2) // 2) as it:
                        for st in range(2):
                            r, ro = base + 4 + 3 * st, eo + it
                            load(r, ro, gu_unit(gu, FE, it * 2 + st + 2, 0))
                            load(r + 1, ro, gu_unit(gu, FE, it * 2 + st + 2, 1))
                            load(r + 2, ro, down_unit(dn, it * 2 + st))
                    load(base + 40, eo, down_unit(dn, NCE - 2))
                    load(base + 41, eo, down_unit(dn, NCE - 1))

            experts(0)
            sp.wait_ge(route_ready, 1)
            over = sp.value_load(flag[0:1, 0:1], min_val=0, max_val=1)
            with sp.If(over > 0):
                experts(1)
            for t in range(T):
                sp.wait_ge(x_done, 3 * T + t + 1)
                sp.dma_start(out[0].rearrange("(t p) d -> p t d", p=P)[:, t, :], xs[:, t, :]).then_inc(stored, 16)
            sp.wait_ge(stored, 16 * T)

        @block.gpsimd
        def _(pool):
            pool.dma_start(relb, rel_bias).then_inc(small_loaded, 16)
            pool.dma_start(onehot, onehot_in).then_inc(small_loaded, 16)
            pool.wait_ge(mixer_rows_zeroed, 1)
            pool.dma_start(rows[0:1, 0:3, :], b_mod[0:1, 0:3 * D].rearrange("a (g d) -> a g d", d=D)).then_inc(bmod_loaded[0], 16)
            pool.memset(bias_row[:, S:S + P], NEG).then_inc(dist_ready, 1)
            pool.dma_start(consts[:, :, :], consts_in.rearrange("p (i s) -> p i s", i=5)).then_inc(consts_loaded, 16)
            pool.memset(rows[:, 3:6, :], 0.0).then_inc(rows_zeroed, 1)
            pool.memset(zeros[:, :], 0.0).then_inc(zeros_ready, 1)
            pool.memset(minus_half[:, :], -0.5).then_inc(half_ready, 1)

            def load_gain(i):
                pool.dma_start(gain[:, i % 2, :], norm_g[i // 4, i % 4, :].partition_broadcast(P)).then_inc(gain_loaded[i % 2], 16)

            def next_gain(i):
                l, j = divmod(i - 2, 4)
                pool.wait_ge(row_done, done_rank(l, (1, 2, 4, 5)[j]))
                load_gain(i)

            pool.wait_ge(unit_done, 3)
            load_gain(0)
            pool.wait_ge(unit_done, 7)
            pool.wait_ge(rows_zeroed, 1)
            pool.dma_start(rows[0:1, 3:6, :], b_mod[0:1, 3 * D:6 * D].rearrange("a (g d) -> a g d", d=D)).then_inc(bmod_loaded[1], 16)
            load_gain(1)
            pool.dma_start(pool_m, pool_in.rearrange("p (g s) -> p g s", g=4)).then_inc(pool_loaded[0], 16)
            pool.dma_start(poolw, pool_w[0].rearrange("g (c p) e -> p g c e", p=P)).then_inc(pool_loaded[1], 16)
            pool.dma_start(rows[:, 6, :], pool_scale[0, :].partition_broadcast(P)).then_inc(scale_loaded, 16)

            def inverse_roots(i, col):
                for t in range(T):
                    cc = 4 * i + col + t
                    pool.wait_ge(ms_ready, cc + 1)
                    pool.tensor_tensor(rstd[:, cc:cc + 1], ss[:, cc:cc + 1], minus_half[:, 0:1], ALU.pow).then_inc(rstd_ready, 1)

            pool.wait_ge(half_ready, 1)
            inverse_roots(0, 0)
            pool.wait_ge(scale_loaded, 16)
            pool.wait_ge(pool_loaded[1], 16)
            for ch in range(2):
                pool.tensor_tensor(poolw[:, :, ch, :], poolw[:, :, ch, :], rows[:, 6, :].rearrange("p (g e) -> p g e", g=4),
                                   ALU.mult).then_inc(scale_folded, 1)
            pool.dma_start(lamv, lambda_vecs[0].partition_broadcast(P)).then_inc(lam_loaded, 16)
            pool.dma_start(subln[:, :], subln_g[0, :].partition_broadcast(P)).then_inc(lam_loaded, 16)
            pool.dma_start(wr[:, :, :], w_router[0].rearrange("(k p) e -> p k e", p=P)).then_inc(wr_loaded, 16)
            pool.wait_ge(dist_ready, 2)
            pool.dma_start(bias_dram, bias_row).then_inc(dist_stored, 16)
            next_gain(2)
            next_gain(3)
            inverse_roots(0, 2)
            pool.wait_ge(x_done, T)
            pool.memset(rows[:, 0:3, :], 0.0).then_inc(rows_zeroed, 1)
            pool.memset(rows[:, 6, :], 0.0).then_inc(rows_zeroed, 1)
            pool.wait_ge(rows_zeroed, 3)
            pool.dma_start(rows[0:1, 0:3, :], b_mod[1:2, D:4 * D].rearrange("a (g d) -> a g d", d=D)).then_inc(bmod_loaded[2], 16)
            pool.dma_start(rows[0:1, 6, :], b_mod[1:2, 0:D]).then_inc(bmod_loaded[2], 16)
            inverse_roots(1, 0)
            pool.wait_ge(h_ready, 2 * T)
            pool.memset(rows[:, 3:5, :], 0.0).then_inc(rows_zeroed, 1)
            pool.wait_ge(rows_zeroed, 4)
            pool.dma_start(rows[0:1, 3:5, :], b_mod[1:2, 4 * D:6 * D].rearrange("a (g d) -> a g d", d=D)).then_inc(bmod_loaded[3], 16)
            next_gain(4)
            pool.wait_ge(dist_stored, 16)
            pool.wait_ge(lam_prod, 2)
            pool.dma_start(bias_rev, bass.AP(tensor=bias_dram.tensor, offset=0,
                                             ap=[(1, P), (S + P, NH), (1, S)])).then_inc(bias_loaded, 16)
            next_gain(5)
            inverse_roots(1, 2)
            inverse_roots(2, 0)

            for half in range(2):
                pool.wait_ge(omse_ready, half + 1)
                o4 = oss[:, half * 4:half * 4 + 4, :].rearrange("p h t -> p (h t)")
                pool.tensor_tensor(o4, o4, minus_half[:, :], ALU.pow).then_inc(orstd_ready, 1)
            pool.wait_ge(o_ps, NH)
            next_gain(6)
            next_gain(7)
            pool.memset(moe_out, 0.0).then_inc(moe_cleared, 1)
            pool.memset(selg_t, 0.0).then_inc(selt_cleared, 1)
            inverse_roots(2, 2)
            inverse_roots(3, 0)
            pool.wait_ge(route_ready, 1)
            over = pool.value_load(flag[0:1, 0:1], min_val=0, max_val=1)
            with pool.If(over > 0):
                pool.wait_ge(over_ready, 1)
                pool.memset(selg_t, 0.0).then_inc(selt_cleared, 1)
            inverse_roots(3, 2)

        @block.scalar
        def _(act):
            def high(r, q, rounds=0, qo=0):
                act.wait_ge(raw_loaded[r % RAW], 32 * (r // RAW + 1) + 32 * rounds)
                if q >= SPL - 1:
                    act.wait_ge(unit_used, max(q - SPL + 1, 1) + qo)
                act.activation(whi[:, q % SPL, :], raw[:, r % RAW, :], ACT.Copy).then_inc(hi_ready, 1)

            def square_x(i):
                for t in range(T):
                    if i == 0:
                        act.wait_ge(x_loaded, 16)
                    else:
                        act.wait_ge(x_done, T * (i - 1) + t + 1)
                    act.activation(ysb[:, t, :], xs[:, t, :], ACT.Square, scale=D ** -0.5,
                                   accum_out=ss[:, 4 * i + t:4 * i + t + 1]).then_inc(ss_ready, 1)

            def high_transposed(i):
                for b in range(4):
                    act.wait_ge(ht_ps, 4 * (i - 1) + b + 1)
                    act.activation(thi[:, 512 * b:512 * b + 512], bank(b), ACT.Copy).then_inc(ht_hi, 1)

            def square_y(i):
                for t in range(T):
                    if t:
                        act.wait_ge(gated, 2 * i + 1)
                    act.activation(hs[:, t, :].rearrange("p (h d) -> p h d", h=2), ps[:, 4 + 2 * t:6 + 2 * t, :],
                                   ACT.Square, scale=D ** -0.5, accum_out=ss[:, 4 * i + 2 + t:4 * i + 3 + t]).then_inc(ss_ready, 1)

            def finish_shift(l, g):
                act.wait_ge(row_ps, row_rank(l, g))
                b = ROW_BANK[l][g]
                act.copy(rows[:, ROW[l][g], :].rearrange("p (h d) -> p h d", h=2), ps[:, b:b + 2, :]).then_inc(shift_done, 1)

            act.wait_ge(c_loaded, 16)
            act.activation(silu_c[:, :], silu_c[:, :], ACT.Silu).then_inc(silu_ready, 1)
            act.wait_ge(dist_ps, 1)
            act.activation(bias_row[:, 0:S], ps[0:NH, 5, 0:S], ACT.Copy, scale=HD ** 0.5).then_inc(dist_ready, 1)

            square_x(0)
            finish_shift(0, 0)
            for b in range(4):
                act.wait_ge(pooled_ps, b + 1)
                act.copy(pooled_t[:, 2 * b:2 * b + 2, :], bank(b).rearrange("p (k s) -> p k s", k=2)).then_inc(pooled_ready, 1)
            act.wait_ge(mix_ps, 1)
            square_y(0)

            high(R_FFN, 0)
            square_x(1)
            finish_shift(0, 3)
            high(R_FFN + 1, 1)
            high_transposed(1)
            act.wait_ge(lam_prod, 2)
            act.activation(lam[:, 2:4], lam[:, 0:2], ACT.Exp).then_inc(lam_exp, 1)

            def ffn_act(s, it=0):
                act.wait_ge(unit_used, 3 * s + 2 + it * 3 * LOOP_STEPS)
                b = 2 * (s % 2)
                act.activation(sg.rearrange("p (j s) -> p j s", j=2), ps[:, b:b + 2, 0:FC], ACT.Silu).then_inc(f_sg, 1)
                act.wait_ge(f_act, s + 1 + it * LOOP_STEPS)
                act.activation(ahi[:, :], actf, ACT.Copy).then_inc(f_ahi, 1)

            def ffn_step(s, r, q, mods, it=0):
                rounds, qo = it * (TURN_UNITS // RAW), it * 3 * LOOP_STEPS
                high(r, q, rounds, qo)
                high(r + 1, q + 1, rounds, qo)
                ffn_act(s, it)
                high(r + 2 + len(mods), q + 2, rounds, qo)

            with act.Fori(0, LOOP_TURNS) as it:
                for s, r, q, mods, _ in FFN_LOOP:
                    ffn_step(s, r, q, mods, it)
            for s, r, q, mods, _ in FFN_TAIL:
                ffn_step(s, r, q, mods)
            high(R_QKV - 1, Q_QKV - 1)
            ffn_act(NCF - 1)
            high(R_QKV, Q_QKV)
            high(R_QKV + 1, Q_QKV + 1)
            act.wait_ge(unit_used, Q_QKV)
            square_y(1)

            finish_shift(1, 0)
            square_x(2)
            act.wait_ge(ss_ready, 4 * 2 + T)
            for b in range(4):
                act.wait_ge(bias_ps, b + 1)
                act.copy(bias_t[:, 2 * b:2 * b + 2, :], bank(4 + b).rearrange("p (h k) -> p h k", h=2)).then_inc(bias_ready, 1)
            high_transposed(2)

            def qkv_out(g):
                act.wait_ge(unit_used, Q_QKV + 2 * g + 2)
                src = ps[:, 4 + 2 * (g % 2):6 + 2 * (g % 2), :]
                if g < 4:
                    dst = qk_t[:, 4 * g:4 * g + 4, :].rearrange("p (b m) s -> p b (m s)", b=2)
                else:
                    dst = vs[:, :, (g - 4) * 512:(g - 3) * 512]
                act.copy(dst, src).then_inc(qkv_ready, 1)

            for g in range(1, 6):
                high(R_GROUP[g], Q_QKV + 2 * g)
                high(R_GROUP[g] + 1, Q_QKV + 2 * g + 1)
                qkv_out(g - 1)

            def exps(h):
                act.wait_ge(sc_max, h + 1)
                a, st = att_s[h % 3], stat[:, h % 4]
                for cc in range(2):
                    for t in range(T):
                        k0, k1 = (0, P) if t == 0 else (P, P + S)
                        act.activation(a[:, cc, k0:k1], a[:, cc, k0:k1], ACT.Exp, scale=HD ** -0.5,
                                       bias=st[:, 0, 2 * cc + t:2 * cc + t + 1],
                                       accum_out=st[:, 1, 2 * cc + t:2 * cc + t + 1]).then_inc(sc_exp, 1)

            def at_copy(h):
                act.wait_ge(at_ps, h + 1)
                act.copy(att_at[h % 2], bank(4 + h % 2, 384)).then_inc(at_ready, 1)

            def o_copy(h):
                act.wait_ge(o_ps, h + 1)
                for t in range(T):
                    act.activation(hs[:, t, h * P:h * P + P], ps[:, 6 + h % 2, t * P:t * P + P], ACT.Copy,
                                   scale=stat[:, h % 4, 2, t:t + 1]).then_inc(o_ready, 1)

            for h in range(3):
                exps(h)
            at_copy(0)
            exps(3)
            qkv_out(5)
            for h in range(NH):
                if h > 1:
                    at_copy(h - 1)
                if 4 <= h + 1 < NH:
                    exps(h + 1)
                if h > 1:
                    o_copy(h - 2)
            high(R_WO, Q_WO)
            at_copy(NH - 1)
            o_copy(NH - 2)
            o_copy(NH - 1)
            high(R_WO + 1, Q_WO + 1)
            finish_shift(1, 3)
            for b in range(4):
                act.wait_ge(ot_ps, b + 1)
                act.activation(thi[:, 512 * b:512 * b + 512], bank(b), ACT.Copy).then_inc(ot_hi, 1)
            high(R_WO + 2, Q_WO + 2)
            high(R_WO + 3, Q_WO + 3)
            act.wait_ge(unit_used, Q_MOE)
            square_y(2)

            square_x(3)
            for u in range(3):
                high(R_MOE + u, Q_MOE + u)
            for b in range(4):
                act.wait_ge(ht_ps, 4 * 2 + b + 1)
                act.copy(ht32[:, 2 * b:2 * b + 2, :], bank(b).rearrange("p (k s) -> p k s", k=2)).then_inc(ht32_ready, 1)
            act.wait_ge(top_ready, 1)
            act.activation(w2[:, 0:2], diff, ACT.Exp).then_inc(e2_ready, 1)

            def experts(ps_no):
                r0, q0, j0 = (R_MOE + ps_no * NE * EXPERT_UNITS, Q_MOE + ps_no * NE * EXPERT_UNITS, ps_no * NE)
                g0, n0 = ps_no * NE, ps_no * (NE + 1)

                def gathered_high(n):
                    for b in range(2):
                        act.wait_ge(g_ps, 2 * n + b + 1)
                        act.activation(thi[:, 512 * b:512 * b + 512], bank(6 + b), ACT.Copy).then_inc(g_hi, 1)

                def expert_out(used):
                    act.wait_ge(unit_used, used)
                    for b in range(2):
                        act.copy(y_e[:, 512 * b:512 * b + 512], bank(4 + b)).then_inc(y_ready, 1)

                def expert(e, last):
                    j, ro, qo = e + j0, e * (EXPERT_UNITS // RAW), e * EXPERT_UNITS

                    def silu_gate(s, used, it=0):
                        act.wait_ge(unit_used, q0 + used + qo + it * 6)
                        act.activation(sg[:, 0:FC], bank(s % 2)[:, 0:FC], ACT.Silu).then_inc(e_sg, 1)

                    def act_high(s, so=0):
                        act.wait_ge(e_at, j * NCE + s + 1 + so)
                        act.activation(ahi[:, (s % 2) * FC:(s % 2) * FC + FC], bank(2 + s % 2, FC), ACT.Copy).then_inc(e_ahi, 1)

                    expert_out(q0 + qo)
                    high(r0 + 3, q0 + 3, ro, qo)
                    silu_gate(0, 2)
                    with act.Fori(0, (NCE - 2) // 2) as it:
                        for st in range(2):
                            u = 4 + 3 * st
                            high(r0 + u, q0 + u, ro + it, qo + it * 6)
                            high(r0 + u + 1, q0 + u + 1, ro + it, qo + it * 6)
                            act_high(st, it * 2)
                            silu_gate(st + 1, 4 + 2 * st, it)
                            high(r0 + u + 2, q0 + u + 2, ro + it, qo + it * 6)
                    act_high(NCE - 2)
                    silu_gate(NCE - 1, EXPERT_UNITS - 3)
                    high(r0 + 40, q0 + 40, ro, qo)
                    act.wait_ge(selt_ps, j + 1)
                    act.copy(selg_t, bank(0, S)).then_inc(selt_ready, 1)
                    if not last:
                        gathered_high(e + g0 + 1)
                    act_high(NCE - 1)
                    high(r0 + 41, q0 + 41, ro, qo)
                    if not last:
                        for u in range(EXPERT_UNITS, EXPERT_UNITS + 3):
                            high(r0 + u, q0 + u, ro, qo)

                if ps_no:
                    for u in range(3):
                        high(r0 + u, q0 + u)
                gathered_high(g0)
                with act.Fori(0, NE - 1) as e:
                    expert(e, False)
                expert(NE - 1, True)
                expert_out(q0 + NE * EXPERT_UNITS)

            experts(0)
            act.wait_ge(route_ready, 1)
            over = act.value_load(flag[0:1, 0:1], min_val=0, max_val=1)
            with act.If(over > 0):
                experts(1)
            for t in range(T):
                act.wait_ge(gated, T * 3 + t + 1)
                act.activation(hs[:, t, :], moe_out[:, t, :], ACT.Square, scale=D ** -0.5,
                               accum_out=ss[:, 14 + t:15 + t]).then_inc(ss_ready, 1)

        @block.vector
        def _(dve):
            links = [0]

            def link(ins):
                links[0] += 1
                ins.then_inc(link_s, 1)
                dve.wait_ge(link_s, links[0])

            def low(r, q, rounds=0, qo=0):
                dve.wait_ge(hi_ready, q + 1 + qo)
                dve.tensor_tensor(wlo[:, q % SPL, :], raw[:, r % RAW, :], whi[:, q % SPL, :].bitcast(F32),
                                  ALU.subtract).then_inc(unit_done, 1)

            def low_from(dst, src, hi_part, sem_out):
                dve.tensor_tensor(dst, src, hi_part.bitcast(F32), ALU.subtract).then_inc(sem_out, 1)

            def gemv_unit(r, l, g, cols, n, rounds=0, ro=0, no=0):
                dve.wait_ge(raw_loaded[r % RAW], 32 * (r // RAW + 1) + 32 * rounds)
                row = rows[:, ROW[l][g], :]
                if n > 0:
                    dve.wait_ge(unit_done, r + ro)
                dve.scalar_tensor_tensor(row, raw[:, r % RAW, 0:D], cols(0), row, ALU.mult, ALU.add).then_inc(gemv, 1)
                dve.wait_ge(gemv, n + 1 + no)
                dve.scalar_tensor_tensor(row, raw[:, r % RAW, D:2 * D], cols(1), row, ALU.mult, ALU.add).then_inc(unit_done, 1)

            def gemv_units(r, mods, n):
                for i, (l, g, pair) in enumerate(mods):
                    gemv_unit(r + i, l, g, lambda kk: silu_c[:, 2 * pair + kk:2 * pair + kk + 1], n + i)

            def finish_rows(l, groups):
                for g in groups:
                    dve.wait_ge(row_ps, row_rank(l, g))
                    b = ROW_BANK[l][g]
                    src = ps[:, b:b + 2, :]
                    row = rows[:, ROW[l][g], :].rearrange("p (h d) -> p h d", h=2)
                    i = 4 * l + ROW_GAIN[g]
                    gv = gain[:, i % 2, :].rearrange("p (h d) -> p h d", h=2)
                    dve.wait_ge(gain_loaded[i % 2], 16 * (i // 2 + 1))
                    if g % 3 == 1:
                        dve.scalar_tensor_tensor(row, src, 1.0, gv, ALU.add, ALU.mult).then_inc(row_done, 1)
                    else:
                        dve.tensor_tensor(row, src, gv, ALU.mult).then_inc(row_done, 1)

            def inverse_root(i, col):
                cc = 4 * i + col
                dve.wait_ge(rstd_ready, cc + 1)
                return rstd[:, cc:cc + 1]

            def add_eps(i, col, tiles=range(T)):
                for t in tiles:
                    cc = 4 * i + col + t
                    dve.wait_ge(ss_ready, cc + 1)
                    dve.tensor_scalar(ss[:, cc:cc + 1], ss[:, cc:cc + 1], EPS, None, ALU.add).then_inc(ms_ready, 1)

            def modulated(i):
                l, g = divmod(i, 2)
                dve.wait_ge(row_done, done_rank(l, 3 * g + 1))
                for t in range(T):
                    if i:
                        dve.wait_ge(x_done, T * (i - 1) + t + 1)
                    else:
                        dve.wait_ge(x_loaded, 16)
                    dve.tensor_tensor(hs[:, t, :], xs[:, t, :], rows[:, ROW[l][3 * g + 1], :], ALU.mult).then_inc(scaled, 1)
                    if i:
                        add_eps(i, 0, [t])
                dve.wait_ge(shift_done, done_rank(l, 3 * g))
                for t in range(T):
                    rs = inverse_root(i, t)
                    dve.wait_ge(scaled, T * i + t + 1)
                    dve.scalar_tensor_tensor(hs[:, t, :], hs[:, t, :], rs, rows[:, ROW[l][3 * g], :],
                                             ALU.mult, ALU.add).then_inc(h_ready, 1)

            def residual(i):
                l, g = divmod(i, 2)
                gv = rows[:, ROW[l][3 * g + 2], :].rearrange("p (h d) -> p h d", h=2)
                dve.wait_ge(row_done, done_rank(l, 3 * g + 2))
                for t in (1, 0):
                    if t == 0:
                        dve.wait_ge(ss_ready, 4 * i + 3)
                    dve.tensor_tensor(ysb[:, t, :].rearrange("p (h d) -> p h d", h=2), ps[:, 4 + 2 * t:6 + 2 * t, :], gv,
                                      ALU.mult).then_inc(gated, 1)
                add_eps(i, 2)
                for t in range(T):
                    rs = inverse_root(i, 2 + t)
                    dve.wait_ge(gated, T * (i + 1))
                    dve.scalar_tensor_tensor(xs[:, t, :], ysb[:, t, :], rs, xs[:, t, :], ALU.mult, ALU.add).then_inc(x_done, 1)

            def low_transposed(i):
                for b in range(4):
                    dve.wait_ge(ht_hi, 4 * (i - 1) + b + 1)
                    low_from(tlo[:, 512 * b:512 * b + 512], bank(b), thi[:, 512 * b:512 * b + 512], ht_lo)

            dve.memset(rows[:, 0:3, :], 0.0).then_inc(mixer_rows_zeroed, 1)
            dve.wait_ge(silu_ready, 1)

            def ffn_mods(pair):
                r = len(MIXER_MODS) + 2 * pair
                gemv_units(r, FFN_MODS[2 * pair:2 * pair + 2], r)

            dve.wait_ge(bmod_loaded[0], 16)
            gemv_units(0, MIXER_MODS, 0)
            add_eps(0, 0)
            finish_rows(0, (1,))
            modulated(0)
            dve.wait_ge(bmod_loaded[1], 16)
            ffn_mods(0)
            finish_rows(0, (2,))
            ffn_mods(1)
            ffn_mods(2)
            dve.wait_ge(mix_ps, 1)
            residual(0)
            ffn_mods(3)
            finish_rows(0, (4,))

            modulated(1)
            low(R_FFN, 0)
            low_transposed(1)
            low(R_FFN + 1, 1)
            dve.wait_ge(lam_loaded, 32)
            for i in range(2):
                if i:
                    dve.wait_ge(lam_prod, 1)
                dve.tensor_tensor_reduce(lamj, lamv[:, 2 * i, :], lamv[:, 2 * i + 1, :], 1.0, 0.0,
                                         ALU.mult, ALU.add, lam[:, i:i + 1]).then_inc(lam_prod, 1)
            dve.wait_ge(lam_exp, 1)
            link(dve.tensor_tensor(lam[:, 0:1], lam[:, 3:4], lam[:, 2:3], ALU.subtract))
            link(dve.tensor_scalar(lam[:, 0:1], lam[:, 0:1], -LAMBDA_INIT, None, ALU.add))
            link(dve.tensor_scalar(subln[:, :], subln[:, :], 1.0 - LAMBDA_INIT, None, ALU.mult))
            dve.wait_ge(bmod_loaded[2], 32)
            dve.wait_ge(bmod_loaded[3], 16)

            def ffn_act(s, so=0):
                dve.wait_ge(f_sg, s + 1 + so)
                b = 2 * (s % 2)
                dve.tensor_tensor(actf.rearrange("p (j s) -> p j s", j=2), sg.rearrange("p (j s) -> p j s", j=2),
                                  ps[:, b:b + 2, FC:2 * FC], ALU.mult).then_inc(f_act, 1)
                dve.wait_ge(f_ahi, s + 1 + so)
                low_from(alo[:, :], actf, ahi[:, :], f_alo)

            with dve.Fori(0, LOOP_TURNS) as it:
                rounds = it * (TURN_UNITS // RAW)
                for s, r, q, mods, n in FFN_LOOP:
                    low(r, q, rounds, it * 3 * LOOP_STEPS)
                    low(r + 1, q + 1, rounds, it * 3 * LOOP_STEPS)
                    for i, (l, g, pair) in enumerate(mods):
                        gemv_unit(r + 2 + i, l, g, lambda kk: silu_c[:, bass.ds(it * 4 + 2 * pair + kk, 1)], n + i,
                                  rounds, it * TURN_UNITS, it * TURN_MODS)
                    ffn_act(s, it * LOOP_STEPS)
                    low(r + 2 + len(mods), q + 2, rounds, it * 3 * LOOP_STEPS)
            for s, r, q, mods, n in FFN_TAIL:
                low(r, q)
                low(r + 1, q + 1)
                gemv_units(r + 2, mods, n)
                ffn_act(s)
                low(r + 2 + len(mods), q + 2)
            low(R_QKV - 1, Q_QKV - 1)
            ffn_act(NCF - 1)
            finish_rows(0, (5,))
            low(R_QKV, Q_QKV)
            dve.wait_ge(unit_used, Q_QKV)
            residual(1)
            finish_rows(1, (1,))

            modulated(2)
            low_transposed(2)
            low(R_QKV + 1, Q_QKV + 1)
            n = N_QKV_MODS
            for g in range(6):
                if g:
                    low(R_GROUP[g], Q_QKV + 2 * g)
                    low(R_GROUP[g] + 1, Q_QKV + 2 * g + 1)
                gemv_units(R_GROUP[g] + 2, QKV_MODS[g], n)
                n += len(QKV_MODS[g])
            dve.wait_ge(bias_ready, 4)

            def row_max(h):
                dve.wait_ge(sc_ps, h + 1)
                if h >= 3:
                    dve.wait_ge(at_ps, h - 2)
                a, st = att_s[h % 3], stat[:, h % 4]
                for cc in range(2):
                    for t in range(T):
                        k0, k1 = (0, P) if t == 0 else (P, P + S)
                        ins = dve.tensor_tensor_reduce(a[:, cc, k0:k1], ps[:, 2 * (h % 2) + cc, k0:k1],
                                                       bias_t[:, h, P:S] if t == 0 else bias_t[:, h, :], 1.0, NEG,
                                                       ALU.add, ALU.max, st[:, 0, 2 * cc + t:2 * cc + t + 1])
                link(ins)
                dve.tensor_scalar(st[:, 0, :], st[:, 0, :], -HD ** -0.5, None, ALU.mult).then_inc(sc_max, 1)

            def combine(h):
                a, st = att_s[h % 3], stat[:, h % 4]
                dve.wait_ge(sc_exp, 4 * h + 4)
                link(dve.reciprocal(st[:, 2, :], st[:, 1, :]))
                link(dve.scalar_tensor_tensor(st[:, 2, 2:4], st[:, 2, 2:4], lam[:, 0:1], st[:, 1, 0:2], ALU.mult, ALU.mult))
                for t, (k0, k1) in enumerate(((0, P), (P, P + S))):
                    ins = dve.scalar_tensor_tensor(a[:, 0, k0:k1], a[:, 1, k0:k1], st[:, 2, 2 + t:3 + t],
                                                   a[:, 0, k0:k1], ALU.mult, ALU.add)
                ins.then_inc(att_ready, 1)

            def head_square(h):
                dve.wait_ge(o_ready, T * (h + 1))
                if h > 0:
                    dve.wait_ge(oms_ready, T * h)
                for t in range(T):
                    o = hs[:, t, h * P:h * P + P]
                    dve.tensor_tensor_reduce(junk[:, t, :], o, o, 1.0 / P, 0.0, ALU.mult, ALU.add,
                                             oss[:, h, t:t + 1]).then_inc(oms_ready, 1)

            def head_eps(half):
                dve.wait_ge(oms_ready, (half + 1) * T * NH // 2)
                o4 = oss[:, half * 4:half * 4 + 4, :].rearrange("p h t -> p (h t)")
                dve.tensor_scalar(o4, o4, EPS, None, ALU.add).then_inc(omse_ready, 1)

            def head_norm(half):
                dve.wait_ge(orstd_ready, half + 1)
                for h in range(4 * half, 4 * half + 4):
                    for t in range(T):
                        o = hs[:, t, h * P:h * P + P]
                        ins = dve.scalar_tensor_tensor(o, o, oss[:, h, t:t + 1], subln[:, :], ALU.mult, ALU.mult)
                    ins.then_inc(on_ready, 1)

            row_max(0)
            row_max(1)
            for h in range(NH):
                combine(h)
                if h + 2 < NH:
                    row_max(h + 2)
                if h >= 3:
                    head_square(h - 3)
                if h == NH - 2:
                    head_eps(0)
            head_square(NH - 3)
            head_norm(0)
            head_square(NH - 2)
            head_square(NH - 1)
            head_eps(1)
            low(R_WO, Q_WO)
            finish_rows(1, (2,))
            head_norm(1)
            for b in range(4):
                dve.wait_ge(ot_hi, b + 1)
                low_from(tlo[:, 512 * b:512 * b + 512], bank(b), thi[:, 512 * b:512 * b + 512], ot_lo)
            for u in range(1, 4):
                low(R_WO + u, Q_WO + u)
            dve.wait_ge(unit_used, Q_MOE)
            residual(2)
            finish_rows(1, (4,))

            modulated(3)
            for u in range(3):
                low(R_MOE + u, Q_MOE + u)
            dve.wait_ge(lg_ps, 1)
            link(dve.tensor_copy(logits, bank(4, 16).rearrange("p (t e) -> p t e", t=T)))
            for t in range(T):
                ins = dve.max(top[:, t, :], logits[:, t, :])
            link(ins)
            dve.tensor_tensor(diff, top[:, :, 1], top[:, :, 0], ALU.subtract).then_inc(top_ready, 1)
            for t in range(T):
                ins = dve.max_index(top_idx[:, t, :], top[:, t, :], logits[:, t, :])
            link(ins)
            link(dve.tensor_copy(idx_f, top_idx[:, :, :]))
            for i in range(2):
                for t in range(T):
                    ins = dve.tensor_scalar(oh[i][:, t, :], slots[:, 0:NE], idx_f[:, t, i:i + 1], None, ALU.is_equal)
            link(ins)
            dve.tensor_tensor(mask, oh[0], oh[1], ALU.add).then_inc(mask_ready, 1)
            dve.wait_ge(e2_ready, 1)
            link(dve.tensor_scalar(w2[:, 2:4], w2[:, 0:2], 1.0, None, ALU.add))
            link(dve.reciprocal(w2[:, 4:6], w2[:, 2:4]))
            link(dve.tensor_tensor(w2[:, 6:8], w2[:, 4:6], w2[:, 0:2], ALU.mult))
            for t in range(T):
                link(dve.tensor_scalar(gates[:, t, :], oh[0][:, t, :], w2[:, 4 + t:5 + t], None, ALU.mult))
                link(dve.scalar_tensor_tensor(gates[:, t, :], oh[1][:, t, :], w2[:, 6 + t:7 + t], gates[:, t, :], ALU.mult, ALU.add))
            dve.wait_ge(pos_ps, 1)
            link(dve.scalar_tensor_tensor(posm[:, :, :], bank(5, 16).rearrange("p (t e) -> p t e", t=T), 1.0, mask, ALU.add, ALU.mult))
            link(dve.tensor_scalar(posm[:, :, :], posm[:, :, :], -1.0, None, ALU.add))
            link(dve.tensor_reduce(cnt[:, 0:1], ps[:, 5, 16:24], AX_X, ALU.max))
            link(dve.tensor_scalar(cnt[:, 1:2], cnt[:, 0:1], float(P), None, ALU.is_gt))
            dve.tensor_copy(flag[:, :], cnt[:, 1:2]).then_inc(route_ready, 1)

            def experts(ps_no):
                r0, q0, j0 = (R_MOE + ps_no * NE * EXPERT_UNITS, Q_MOE + ps_no * NE * EXPERT_UNITS, ps_no * NE)
                g0, n0 = ps_no * NE, ps_no * (NE + 1)

                def select(e):
                    for t in range(T):
                        dve.tensor_scalar(sel[:, t, :], slots, posm[:, t, bass.ds(e, 1)], None, ALU.is_equal).then_inc(sel_ready, 1)

                def gathered_low(n):
                    for b in range(2):
                        dve.wait_ge(g_hi, 2 * n + b + 1)
                        low_from(tlo[:, 512 * b:512 * b + 512], bank(6 + b), thi[:, 512 * b:512 * b + 512], g_lo)

                def add_scattered(n):
                    for t in range(T):
                        for half in range(2):
                            dve.wait_ge(scat_ps, 4 * n + 2 * t + half + 1)
                            dst = moe_out[:, t, half * 512:half * 512 + 512]
                            dve.tensor_tensor(dst, dst, bank(6 - 4 * t + half), ALU.add).then_inc(scat_done, 1)

                def expert(e, last):
                    j, ro, qo = e + j0, e * (EXPERT_UNITS // RAW), e * EXPERT_UNITS

                    def times_up(s, so=0):
                        dve.wait_ge(e_sg, j * NCE + s + 1 + so)
                        dve.tensor_tensor(actf[:, 0:FC], sg[:, 0:FC], bank(s % 2)[:, FC:2 * FC], ALU.mult).then_inc(e_act, 1)

                    def act_low(s, so=0):
                        dve.wait_ge(e_ahi, j * NCE + s + 1 + so)
                        a = (s % 2) * FC
                        low_from(alo[:, a:a + FC], bank(2 + s % 2, FC), ahi[:, a:a + FC], e_alo)

                    low(r0 + 3, q0 + 3, ro, qo)
                    times_up(0)
                    add_scattered(e + n0)
                    for t in range(T):
                        dve.tensor_scalar(selg[:, t, :], slots, posm[:, t, bass.ds(e, 1)], gates[:, t, bass.ds(e, 1)],
                                          ALU.is_equal, ALU.mult).then_inc(selg_ready, 1)
                    if not last:
                        select(e + 1)
                    with dve.Fori(0, (NCE - 2) // 2) as it:
                        for st in range(2):
                            u = 4 + 3 * st
                            low(r0 + u, q0 + u, ro + it, qo + it * 6)
                            low(r0 + u + 1, q0 + u + 1, ro + it, qo + it * 6)
                            act_low(st, it * 2)
                            times_up(st + 1, it * 2)
                            low(r0 + u + 2, q0 + u + 2, ro + it, qo + it * 6)
                    act_low(NCE - 2)
                    times_up(NCE - 1)
                    low(r0 + 40, q0 + 40, ro, qo)
                    if not last:
                        gathered_low(e + g0 + 1)
                    act_low(NCE - 1)
                    low(r0 + 41, q0 + 41, ro, qo)
                    if not last:
                        for u in range(EXPERT_UNITS, EXPERT_UNITS + 3):
                            low(r0 + u, q0 + u, ro, qo)

                select(0)
                if ps_no:
                    for u in range(3):
                        low(r0 + u, q0 + u)
                gathered_low(g0)
                if ps_no == 0:
                    finish_rows(1, (5,))
                with dve.Fori(0, NE - 1) as e:
                    expert(e, False)
                expert(NE - 1, True)
                add_scattered(n0 + NE)
                dve.wait_ge(scat_done, 4 * (n0 + NE + 1))

            dve.wait_ge(route_ready, 1)
            dve.wait_ge(moe_cleared, 1)
            experts(0)
            over = dve.value_load(flag[0:1, 0:1], min_val=0, max_val=1)
            with dve.If(over > 0):
                link_less = dve.tensor_scalar(posm[:, :, :], posm[:, :, :], float(-P), None, ALU.add)
                link_less.then_inc(over_ready, 1)
                dve.wait_ge(over_ready, 1)
                experts(1)
            gv = rows[:, ROW[1][5], :]
            dve.wait_ge(row_done, done_rank(1, 5))
            for t in range(T):
                dve.tensor_tensor(ysb[:, t, :], moe_out[:, t, :], gv, ALU.mult).then_inc(gated, 1)
            add_eps(3, 2)
            for t in range(T):
                rs = inverse_root(3, 2 + t)
                dve.wait_ge(gated, T * 3 + t + 1)
                dve.scalar_tensor_tensor(xs[:, t, :], ysb[:, t, :], rs, xs[:, t, :], ALU.mult, ALU.add).then_inc(x_done, 1)

        @block.tensor
        def _(pe):
            def row_sum(l, g):
                for h in range(2):
                    mm = pe.matmul(bank(ROW_BANK[l][g] + h), ones, rows[:, ROW[l][g], h * 512:h * 512 + 512], start=True, stop=True)
                mm.then_inc(row_ps, 1)

            def transposes(done, heads=False):
                for b in range(4):
                    if heads:
                        pe.wait_ge(on_ready, 2 * b + 2)
                    for k in (2 * b, 2 * b + 1):
                        for t in range(T):
                            c0 = (k % 2) * S + t * P
                            mm = pe.transpose(ps[:, b, c0:c0 + P], hs[:, t, k * P:k * P + P], ident)
                    mm.then_inc(done, 1)

            def three(out, a_hi, a_lo, b_hi, b_lo, start, stop, check):
                pe.matmul(out, a_hi, b_hi, start=start, stop=False, skip_group_check=check)
                pe.matmul(out, a_hi, b_lo, start=False, stop=False, skip_group_check=check)
                return pe.matmul(out, a_lo, b_hi, start=False, stop=stop, skip_group_check=check)

            def zero_bank(b):
                for h in range(4):
                    pe.matmul(ps[:, b, h * P:h * P + P], zeros[:, :], zeros[:, :], start=(h == 0), stop=False,
                              skip_group_check=True)

            pe.wait_ge(consts_loaded, 16)
            pe.wait_ge(small_loaded, 32)
            pe.matmul(ps[0:NH, 5, 0:S], relb, onehot, start=True, stop=True).then_inc(dist_ps, 1)
            pe.wait_ge(unit_done, len(MIXER_MODS))
            pe.wait_ge(dist_ready, 2)
            row_sum(0, 1)
            row_sum(0, 0)
            pe.wait_ge(row_done, done_rank(0, 1))
            row_sum(0, 2)
            pe.wait_ge(pool_loaded[0], 16)
            pe.wait_ge(h_ready, T)
            for b in range(4):
                for t in range(T):
                    for k in (2 * b, 2 * b + 1):
                        c0 = (k % 2) * S
                        g = k // 2
                        if t == 0:
                            mm = pe.matmul(ps[:, b, c0:c0 + S], hs[:, 0, k * P:k * P + P], pool_m[:, g, 0:S],
                                           start=(k % 2 == 0), stop=False, skip_group_check=True)
                        else:
                            mm = pe.matmul(ps[:, b, c0 + P:c0 + S], hs[:, 1, k * P:k * P + P], pool_m[:, g, S:S + P],
                                           start=False, stop=True, skip_group_check=True)
                mm.then_inc(pooled_ps, 1)
            pe.wait_ge(pooled_ready, 4)
            pe.wait_ge(row_done, done_rank(0, 2))
            pe.wait_ge(shift_done, done_rank(0, 0))
            pe.wait_ge(scale_folded, 2)
            for t in range(T):
                for g in range(4):
                    for k in range(2):
                        mm = pe.matmul(ps[:, 4 + 2 * t + g // 2, (g % 2) * FC:(g % 2) * FC + FC],
                                       pooled_t[:, 2 * g + k, t * P:t * P + P], poolw[:, g, k, :],
                                       start=(g % 2 == 0 and k == 0), stop=(k == 1), skip_group_check=True)
            mm.then_inc(mix_ps, 1)
            pe.wait_ge(unit_done, R_FFN)
            for g in (4, 3):
                row_sum(0, g)
            pe.wait_ge(h_ready, 2 * T)
            transposes(ht_ps)

            def ffn_gate_up(s, r, q, it=0, first=False):
                for kh in range(2):
                    pe.wait_ge(unit_done, r + kh + 1 + it * TURN_UNITS)
                    sl = (q + kh) % SPL
                    for kk in range(4):
                        k = 4 * kh + kk
                        if first and k % 2 == 0:
                            pe.wait_ge(ht_lo, max(k // 2 + 1, 2))
                        for jj in range(2):
                            for g in range(2):
                                c0 = kk * 512 + g * FC + jj * P
                                o = ps[:, 2 * (s % 2) + jj, g * S:g * S + S]
                                mm = three(o, whi[:, sl, c0:c0 + P], wlo[:, sl, c0:c0 + P], thi3[:, k, :], tlo3[:, k, :],
                                           k == 0 and g == 0, k == KC - 1 and g == 1, True)
                    mm.then_inc(unit_used, 1)

            def ffn_down(s, r, q, it=0, last=False):
                pe.wait_ge(f_alo, s + 1 + it * LOOP_STEPS)
                pe.wait_ge(unit_done, r + 1 + it * TURN_UNITS)
                sl = q % SPL
                for jj in range(2):
                    for t in range(T):
                        a = slice(jj * S + t * P, jj * S + t * P + P)
                        for half in range(2):
                            w = slice(jj * D + half * 512, jj * D + half * 512 + 512)
                            mm = three(bank(4 + 2 * t + half), ahi[:, a], alo[:, a], whi[:, sl, w], wlo[:, sl, w],
                                       False, last and jj == 1, True)
                mm.then_inc(unit_used, 1)

            ffn_gate_up(0, R_FFN, 0, first=True)
            pe.wait_ge(zeros_ready, 1)
            pe.wait_ge(x_done, T)
            for b in range(4, 8):
                zero_bank(b)
            with pe.Fori(0, LOOP_TURNS) as it:
                for s, r, q, mods, _ in FFN_LOOP:
                    ffn_gate_up(s + 1, r, q, it)
                    ffn_down(s, r + 2 + len(mods), q + 2, it)
            for s, r, q, mods, _ in FFN_TAIL:
                ffn_gate_up(s + 1, r, q)
                ffn_down(s, r + 2 + len(mods), q + 2)
            row_sum(0, 5)
            ffn_down(NCF - 1, R_LAST_DOWN, Q_LAST_DOWN, last=True)
            row_sum(1, 1)
            pe.wait_ge(row_done, done_rank(0, 5))
            row_sum(1, 0)
            pe.wait_ge(bias_loaded, 16)
            pe.wait_ge(x_done, 2 * T)
            for b in range(4):
                pe.matmul(bank(4 + b), reverse, bias_rev[:, 2 * b:2 * b + 2, :].rearrange("p h k -> p (h k)"),
                          start=True, stop=True).then_inc(bias_ps, 1)
            pe.wait_ge(h_ready, 3 * T)
            transposes(ht_ps)
            pe.wait_ge(bias_ready, 4)

            def qkv_group(g, between=None):
                if g >= 2:
                    pe.wait_ge(qkv_ready, g - 1)
                for kh in range(2):
                    if kh and between:
                        between()
                    r, q = R_GROUP[g] + kh, Q_QKV + 2 * g + kh
                    pe.wait_ge(unit_done, r + 1)
                    for kk in range(4):
                        k = 4 * kh + kk
                        if g == 0 and k % 2 == 0:
                            pe.wait_ge(ht_lo, 4 + k // 2 + 1)
                        if g < 4:
                            for m in range(4):
                                c0 = kk * 512 + m * P
                                o = ps[:, 4 + 2 * (g % 2) + m // 2, (m % 2) * S:(m % 2) * S + S]
                                mm = three(o, whi[:, q % SPL, c0:c0 + P], wlo[:, q % SPL, c0:c0 + P],
                                           thi3[:, k, :], tlo3[:, k, :], k == 0 and m % 2 == 0, k == KC - 1 and m % 2 == 1, True)
                        else:
                            for t in range(T):
                                w = slice(kk * 512, kk * 512 + 512)
                                mm = three(bank(4 + 2 * (g % 2) + t), thi3[:, k, t * P:t * P + P], tlo3[:, k, t * P:t * P + P],
                                           whi[:, q % SPL, w], wlo[:, q % SPL, w], k == 0, k == KC - 1, False)
                    mm.then_inc(unit_used, 1)

            for g in range(5):
                qkv_group(g)

            def scores(h):
                if h >= 2:
                    pe.wait_ge(sc_max, h - 1)
                for cc in range(2):
                    rows_c = slice(cc * HD, cc * HD + HD)
                    b = 2 * (h % 2) + cc
                    pe.matmul(ps[:, b, 0:P], qk_t[rows_c, h, 0:P], qk_t[rows_c, NH + h, 0:P], start=True, stop=True)
                    mm = pe.matmul(ps[:, b, P:P + S], qk_t[rows_c, h, P:S], qk_t[rows_c, NH + h, :], start=True, stop=True)
                mm.then_inc(sc_ps, 1)

            def values(h):
                pe.wait_ge(at_ready, h + 1)
                if h >= 2:
                    pe.wait_ge(o_ready, h - 1)
                b, at, cols = 6 + h % 2, att_at[h % 2], slice(h * P, h * P + P)
                pe.matmul(ps[:, b, 0:P], at[:, 0:P], vs[:, 0, cols], start=True, stop=True)
                pe.matmul(ps[:, b, P:S], at[:, P:2 * P], vs[:, 0, cols], start=True, stop=False)
                pe.matmul(ps[:, b, P:S], at[:, 2 * P:3 * P], vs[:, 1, cols], start=False, stop=True).then_inc(o_ps, 1)

            scores(0)
            scores(1)

            def turn_weights(h):
                pe.wait_ge(att_ready, h + 1)
                if h >= 2:
                    pe.wait_ge(at_ready, h - 1)
                elif h == 0:
                    pe.wait_ge(qkv_ready, 5)
                for i in range(3):
                    mm = pe.transpose(ps[:, 4 + h % 2, i * P:i * P + P], att_s[h % 3][:, 0, i * P:i * P + P], ident)
                mm.then_inc(at_ps, 1)

            def first_heads():
                scores(2)
                scores(3)
                turn_weights(0)

            qkv_group(5, first_heads)
            pe.wait_ge(qkv_ready, 6)
            for h in range(NH):
                if h > 0:
                    turn_weights(h)
                if 4 <= h + 3 < NH:
                    scores(h + 3)
                if h > 0:
                    values(h - 1)
            values(NH - 1)
            row_sum(1, 2)
            row_sum(1, 3)
            pe.wait_ge(row_done, done_rank(1, 2))
            pe.wait_ge(shift_done, done_rank(1, 3))
            transposes(ot_ps, heads=True)
            for half in range(2):
                for kh in range(2):
                    r, q = R_WO + 2 * half + kh, Q_WO + 2 * half + kh
                    pe.wait_ge(unit_done, r + 1)
                    for kk in range(4):
                        k, w = 4 * kh + kk, slice(kk * 512, kk * 512 + 512)
                        if half == 0 and k % 2 == 0:
                            pe.wait_ge(ot_lo, k // 2 + 1)
                        for t in range(T):
                            mm = three(bank(4 + 2 * t + half), thi3[:, k, t * P:t * P + P], tlo3[:, k, t * P:t * P + P],
                                       whi[:, q % SPL, w], wlo[:, q % SPL, w], k == 0, k == KC - 1, False)
                    mm.then_inc(unit_used, 1)
            row_sum(1, 4)

            pe.wait_ge(h_ready, 4 * T)
            transposes(ht_ps)
            pe.wait_ge(wr_loaded, 16)
            for k in range(KC):
                if k % 2 == 0:
                    pe.wait_ge(ht32_ready, k // 2 + 1)
                for t in range(T):
                    mm = pe.matmul(ps[:, 4, t * NE:t * NE + NE], ht32[:, k, t * P:t * P + P], wr[:, k, :],
                                   start=(k == 0 and t == 0), stop=(k == KC - 1), skip_group_check=True)
            mm.then_inc(lg_ps, 1)
            pe.wait_ge(mask_ready, 1)
            pe.matmul(ps[:, 5, 0:NE], before, mask[:, 0, :], start=True, stop=True)
            pe.matmul(ps[:, 5, NE:2 * NE], ones, mask[:, 0, :], start=True, stop=False)
            pe.matmul(ps[:, 5, NE:2 * NE], before, mask[:, 1, :], start=False, stop=True)
            pe.matmul(ps[:, 5, 2 * NE:3 * NE], ones, mask[:, 0, :], start=True, stop=False)
            pe.matmul(ps[:, 5, 2 * NE:3 * NE], ones, mask[:, 1, :], start=False, stop=True).then_inc(pos_ps, 1)

            def experts(ps_no):
                r0, q0, j0 = (R_MOE + ps_no * NE * EXPERT_UNITS, Q_MOE + ps_no * NE * EXPERT_UNITS, ps_no * NE)
                g0, n0 = ps_no * NE, ps_no * (NE + 1)

                def gather(n):
                    pe.wait_ge(sel_ready, T * n + T)
                    for b in range(2):
                        for k in range(4 * b, 4 * b + 4):
                            for t in range(T):
                                mm = pe.matmul(ps[:, 6 + b, (k % 4) * P:(k % 4) * P + P], hs[:, t, k * P:k * P + P],
                                               sel[:, t, :], start=(t == 0), stop=(t == T - 1))
                        mm.then_inc(g_ps, 1)

                def scatter(n):
                    pe.wait_ge(y_ready, 2 * n + 2)
                    for t in range(T):
                        for half in range(2):
                            pe.matmul(bank(6 - 4 * t + half), selg_t[:, t * P:t * P + P], y_e[:, half * 512:half * 512 + 512],
                                      start=True, stop=True).then_inc(scat_ps, 1)

                def expert(e, last_expert):
                    j, ro = e + j0, e * EXPERT_UNITS

                    def gate_up(s, u, it=0):
                        for kh in range(2):
                            pe.wait_ge(unit_done, r0 + u + kh + 1 + ro + it * 6)
                            sl = (q0 + u + kh) % SPL
                            for kk in range(4):
                                k, w = 4 * kh + kk, slice(kk * 512, kk * 512 + 512)
                                mm = three(bank(s % 2), ghi[:, k, :], glo[:, k, :], whi[:, sl, w], wlo[:, sl, w],
                                           k == 0, k == KC - 1, False)
                            mm.then_inc(unit_used, 1)

                    def turn(s, it=0):
                        pe.wait_ge(e_act, j * NCE + s + 1 + it * 2)
                        for jj in range(2):
                            mm = pe.transpose(ps[:, 2 + s % 2, jj * P:jj * P + P], actf[:, jj * P:jj * P + P], ident)
                        mm.then_inc(e_at, 1)

                    def down(s, u, it=0, last=False):
                        pe.wait_ge(e_alo, j * NCE + s + 1 + it * 2)
                        pe.wait_ge(unit_done, r0 + u + 1 + ro + it * 6)
                        sl = (q0 + u) % SPL
                        for jj in range(2):
                            a = slice((s % 2) * FC + jj * P, (s % 2) * FC + jj * P + P)
                            for half in range(2):
                                w = slice(jj * D + half * 512, jj * D + half * 512 + 512)
                                mm = three(bank(4 + half), ahi[:, a], alo[:, a], whi[:, sl, w], wlo[:, sl, w],
                                           False, last and jj == 1, True)
                        mm.then_inc(unit_used, 1)

                    pe.wait_ge(g_lo, 2 * (e + g0) + 2)
                    gate_up(0, 0)
                    pe.wait_ge(row_done, done_rank(1, 5))
                    scatter(e + n0)
                    gate_up(1, 2)
                    pe.wait_ge(scat_done, 4 * (e + n0) + 4)
                    turn(0)
                    zero_bank(4)
                    zero_bank(5)
                    with pe.Fori(0, (NCE - 2) // 2) as it:
                        for st in range(2):
                            gate_up(st, 4 + 3 * st, it)
                            turn(st + 1, it)
                            down(st, 6 + 3 * st, it)
                    pe.wait_ge(selg_ready, T * j + T)
                    for t in range(T):
                        mm = pe.transpose(ps[:, 0, t * P:t * P + P], selg[:, t, :], ident)
                    mm.then_inc(selt_ps, 1)
                    if not last_expert:
                        gather(e + g0 + 1)
                    turn(NCE - 1)
                    down(NCE - 2, 40)
                    down(NCE - 1, 41, last=True)
                    pe.wait_ge(selt_ready, j + 1)

                pe.wait_ge(selt_cleared, ps_no + 1)
                gather(g0)
                if ps_no == 0:
                    row_sum(1, 5)
                with pe.Fori(0, NE - 1) as e:
                    expert(e, False)
                expert(NE - 1, True)
                scatter(n0 + NE)

            pe.wait_ge(route_ready, 1)
            experts(0)
            over = pe.value_load(flag[0:1, 0:1], min_val=0, max_val=1)
            with pe.If(over > 0):
                experts(1)


def kernel(x, c, w_mod, b_mod, norm_g, pool_w, pool_scale, w_qkv, w_o, subln_g, lambda_vecs, rel_bias,
           ffn_w_gu, ffn_w_down, w_router, moe_w_gu, moe_w_down):
    import concourse.bacc as bacc
    from concourse.bass_utils import run_bass_kernel_spmd

    consts, pool_m, onehot = shape_constants()
    arrays = dict(x=x, c=c, w_mod=w_mod, b_mod=b_mod, norm_g=norm_g, pool_w=pool_w, pool_scale=pool_scale,
                  w_qkv=w_qkv, w_o=w_o, subln_g=subln_g, lambda_vecs=lambda_vecs, rel_bias=rel_bias,
                  ffn_w_gu=ffn_w_gu, ffn_w_down=ffn_w_down, w_router=w_router, moe_w_gu=moe_w_gu,
                  moe_w_down=moe_w_down, consts_in=consts, pool_in=pool_m, onehot_in=onehot)
    arrays = {name: np.ascontiguousarray(a) for name, a in arrays.items()}
    nc = bacc.Bacc("TRN2", target_bir_lowering=False, num_devices=1,
                   dynamic_dma_scratch_size=8192)
    aps = {name: nc.dram_tensor(name, a.shape, F32, kind="ExternalInput").ap() for name, a in arrays.items()}
    out = nc.dram_tensor("out", (1, S, D), F32, kind="ExternalOutput").ap()
    build_trunk(nc, out=out, **aps)
    result = run_bass_kernel_spmd(nc, [arrays], core_ids=[0])
    return result.results[0]["out"]
```
